# Optimizing a Trainium2 kernel written in Bass

```python
import math
import jax
import jax.numpy as jnp
from jax import lax
import numpy as np

D_MODEL = 1024
BATCH = 1
SEQ = 1024
DEPTH = 1
DEC_BATCH = 8
DEC_SEQ = 4
PAST_LEN = 2048
PAGE_SIZE = 128

D_MIX = D_MODEL
D_SSM = D_MIX // 2
D_DIFF = D_MIX - D_SSM
P_SSM = 64
H_SSM = D_SSM // P_SSM
N_STATE = 128
SSM_GROUPS = 2
HEADS_PER_GROUP = H_SSM // SSM_GROUPS
CONV_W = 4
CONV_DIM = D_SSM + 2 * SSM_GROUPS * N_STATE
SSD_CHUNK = 128
DH_DIFF = 64
H_DIFF = D_DIFF // (2 * DH_DIFF)
Q_BLOCK = 128
N_BUCKETS = 32
REL_MAX_DIST = 128
N_KEYS = 128
N_EXPERTS = N_KEYS * N_KEYS
PEER_HEADS = 8
PEER_TOPK = 16
D_KEY = 256
PEER_BLOCK = 128
PLE_DIM = 256
IN_COLS = D_SSM + CONV_DIM + H_SSM + 3 * D_DIFF
SPLIT_AT = (D_SSM, D_SSM + CONV_DIM, D_SSM + CONV_DIM + H_SSM,
            D_SSM + CONV_DIM + H_SSM + D_DIFF, D_SSM + CONV_DIM + H_SSM + 2 * D_DIFF)
NEG_INF = -1e30
RMS_EPS = 1e-6

kernel_name = 'hybrid_ssd_diffattn_peer_step'

def rmsnorm(x, g):
    xf = x.astype(jnp.float32)
    y = xf * lax.rsqrt(jnp.mean(xf * xf, axis=-1, keepdims=True) + RMS_EPS)
    return (y * g.astype(jnp.float32)).astype(x.dtype)

def t5_bucket(rel):
    n = jnp.maximum(rel, 0)
    max_exact = N_BUCKETS // 2
    nf = jnp.maximum(n, 1).astype(jnp.float32)
    large = max_exact + (jnp.log(nf / max_exact) / math.log(REL_MAX_DIST / max_exact)
                         * (N_BUCKETS - max_exact)).astype(jnp.int32)
    large = jnp.minimum(large, N_BUCKETS - 1)
    return jnp.where(n < max_exact, n, large)

def segsum(a):
    t = a.shape[-1]
    cs = jnp.cumsum(a, axis=-1)
    diff = cs[..., :, None] - cs[..., None, :]
    mask = jnp.tril(jnp.ones((t, t), dtype=bool))
    return jnp.where(mask, diff, -jnp.inf)

def ssd_chunked(xdt, adt, b, c, state0, chunk):
    bsz, seqlen, nh, hp = xdt.shape
    nc = seqlen // chunk
    xc = xdt.reshape(bsz, nc, chunk, nh, hp)
    ac = jnp.transpose(adt.reshape(bsz, nc, chunk, nh), (0, 3, 1, 2))
    bc = b.reshape(bsz, nc, chunk, nh, N_STATE)
    cc = c.reshape(bsz, nc, chunk, nh, N_STATE)
    a_cs = jnp.cumsum(ac, axis=-1)
    l_intra = jnp.exp(segsum(ac))
    y_diag = jnp.einsum('bclhn,bcshn,bhcls,bcshp->bclhp', cc, bc, l_intra, xc)
    decay_states = jnp.exp(a_cs[..., -1:] - a_cs)
    states = jnp.einsum('bclhn,bhcl,bclhp->bchpn', bc, decay_states, xc)
    states = jnp.concatenate([state0[:, None], states], axis=1)
    chunk_decay = jnp.exp(segsum(jnp.pad(a_cs[..., -1], ((0, 0), (0, 0), (1, 0)))))
    new_states = jnp.einsum('bhzc,bchpn->bzhpn', chunk_decay, states)
    states_in, final = new_states[:, :-1], new_states[:, -1]
    y_off = jnp.einsum('bclhn,bchpn,bhcl->bclhp', cc, states_in, jnp.exp(a_cs))
    return (y_diag + y_off).reshape(bsz, seqlen, nh, hp), final

def causal_dwconv(xpad, w):
    ch = xpad.shape[-1]
    return lax.conv_general_dilated(xpad, w[:, None, :].astype(xpad.dtype), window_strides=(1,),
                                    padding='VALID', dimension_numbers=('NWC', 'WIO', 'NWC'),
                                    feature_group_count=ch)

def diff_attention(q, k, v, q_pos0, lam, rel_bias):
    bsz, lq = q.shape[0], q.shape[1]
    lk = k.shape[1]
    blk = math.gcd(lq, Q_BLOCK)
    nblk = lq // blk
    kpos = jnp.arange(lk, dtype=jnp.int32)
    qb = jnp.moveaxis(q.reshape(bsz, nblk, blk, H_DIFF, 2, DH_DIFF), 1, 0)
    scale = DH_DIFF ** -0.5

    def one_block(args):
        q_blk, i = args
        qpos = q_pos0 + i * blk + jnp.arange(blk, dtype=jnp.int32)
        s = jnp.einsum('bqhmd,bkhmd->bhmqk', q_blk, k).astype(jnp.float32) * scale
        rel = qpos[:, None] - kpos[None, :]
        bias = jnp.moveaxis(rel_bias[t5_bucket(rel)], -1, 0).astype(jnp.float32)
        s = jnp.where(rel >= 0, s + bias[None, :, None], NEG_INF)
        pm = jax.nn.softmax(s, axis=-1)
        w = pm[:, :, 0] - lam * pm[:, :, 1]
        return jnp.einsum('bhqk,bkhe->bqhe', w.astype(v.dtype), v)

    o = lax.map(one_block, (qb, jnp.arange(nblk, dtype=jnp.int32)))
    return jnp.moveaxis(o, 0, 1).reshape(bsz, lq, H_DIFF, 2 * DH_DIFF)

def peer(xn, w_query, sub_keys, expert_u, expert_v):
    t = xn.shape[0]
    blk = math.gcd(t, PEER_BLOCK)
    xb = xn.reshape(t // blk, blk, D_MODEL)

    def one(xt):
        q = (xt @ w_query).reshape(blk, PEER_HEADS, 2, D_KEY // 2)
        s = jnp.einsum('thcd,cnd->thcn', q, sub_keys).astype(jnp.float32)
        s1, i1 = lax.top_k(s[:, :, 0], PEER_TOPK)
        s2, i2 = lax.top_k(s[:, :, 1], PEER_TOPK)
        cand = (s1[..., :, None] + s2[..., None, :]).reshape(blk, PEER_HEADS, PEER_TOPK * PEER_TOPK)
        cidx = (i1[..., :, None] * N_KEYS + i2[..., None, :]).reshape(blk, PEER_HEADS, PEER_TOPK * PEER_TOPK)
        sc, pos = lax.top_k(cand, PEER_TOPK)
        idx = jnp.take_along_axis(cidx, pos, axis=-1)
        g = jax.nn.softmax(sc, axis=-1)
        u = expert_u[idx]
        act = jax.nn.gelu(jnp.einsum('thkd,td->thk', u, xt).astype(jnp.float32), approximate=False)
        vv = expert_v[idx]
        return jnp.einsum('thk,thkd->td', (g * act).astype(vv.dtype), vv)

    return lax.map(one, xb).reshape(t, D_MODEL)

def decoder_layer(h, p_l, conv_buf, ssm0, past_k, past_v, pos0, lam_init,
                  g_mix, w_in, conv_w, conv_b, dt_bias, a_log, d_skip, g_ssm_norm,
                  lam_q1, lam_k1, lam_q2, lam_k2, g_diff_norm, rel_bias, w_out,
                  g_ffn, w_query, sub_keys, expert_u, expert_v, w_ple, w_ple_gate, g_ple):
    bsz, seqlen = h.shape[0], h.shape[1]
    a = rmsnorm(h, g_mix)
    proj = a @ w_in
    z, xbc, dt_raw, q, k, v = jnp.split(proj, SPLIT_AT, axis=-1)

    xpad = jnp.concatenate([conv_buf.astype(xbc.dtype), xbc], axis=1)
    conv_new = xpad[:, -(CONV_W - 1):]
    xc = jax.nn.silu(causal_dwconv(xpad, conv_w) + conv_b)
    xs, bm, cm = jnp.split(xc, (D_SSM, D_SSM + SSM_GROUPS * N_STATE), axis=-1)
    xs = xs.reshape(bsz, seqlen, H_SSM, P_SSM).astype(jnp.float32)
    bh = jnp.repeat(bm.reshape(bsz, seqlen, SSM_GROUPS, N_STATE), HEADS_PER_GROUP, axis=2).astype(jnp.float32)
    ch = jnp.repeat(cm.reshape(bsz, seqlen, SSM_GROUPS, N_STATE), HEADS_PER_GROUP, axis=2).astype(jnp.float32)
    dt = jax.nn.softplus(dt_raw.astype(jnp.float32) + dt_bias.astype(jnp.float32))
    adt = -jnp.exp(a_log.astype(jnp.float32)) * dt
    y, ssm_final = ssd_chunked(xs * dt[..., None], adt, bh, ch, ssm0.astype(jnp.float32),
                               math.gcd(seqlen, SSD_CHUNK))
    y = y + d_skip.astype(jnp.float32)[:, None] * xs
    y = y.reshape(bsz, seqlen, D_SSM) * jax.nn.silu(z.astype(jnp.float32))
    yg = y.reshape(bsz, seqlen, SSM_GROUPS, D_SSM // SSM_GROUPS)
    yg = yg * lax.rsqrt(jnp.mean(yg * yg, axis=-1, keepdims=True) + RMS_EPS)
    y_ssm = (yg.reshape(bsz, seqlen, D_SSM) * g_ssm_norm.astype(jnp.float32)).astype(h.dtype)

    q = q.reshape(bsz, seqlen, H_DIFF, 2, DH_DIFF)
    k = k.reshape(bsz, seqlen, H_DIFF, 2, DH_DIFF)
    v = v.reshape(bsz, seqlen, H_DIFF, 2 * DH_DIFF)
    if past_k is None:
        k_all, v_all = k, v
    else:
        k_all = jnp.concatenate([past_k.astype(k.dtype), k], axis=1)
        v_all = jnp.concatenate([past_v.astype(v.dtype), v], axis=1)
    lam = (jnp.exp(jnp.sum(lam_q1.astype(jnp.float32) * lam_k1.astype(jnp.float32)))
           - jnp.exp(jnp.sum(lam_q2.astype(jnp.float32) * lam_k2.astype(jnp.float32))) + lam_init)
    o = diff_attention(q, k_all, v_all, pos0, lam, rel_bias)
    o = rmsnorm(o, g_diff_norm) * (1.0 - lam_init)
    y_diff = o.reshape(bsz, seqlen, D_DIFF).astype(h.dtype)

    h = h + jnp.concatenate([y_ssm, y_diff], axis=-1) @ w_out
    m = rmsnorm(h, g_ffn)
    h = h + peer(m.reshape(bsz * seqlen, D_MODEL), w_query, sub_keys, expert_u, expert_v).reshape(bsz, seqlen, D_MODEL)
    h = h + (p_l @ w_ple) * jax.nn.sigmoid(rmsnorm(h, g_ple) @ w_ple_gate)
    return h, k, v, ssm_final.astype(ssm0.dtype), conv_new

def setup_inputs(seed: int = 0) -> dict:
    key = jax.random.key(seed)
    ks = jax.random.split(key, 40)
    f32 = jnp.float32
    n_pages = PAST_LEN // PAGE_SIZE
    n_pool = (DEC_BATCH * n_pages * 5) // 4

    def nrm(k, shape, s):
        return jax.random.normal(k, shape, f32) * s

    dt0 = jnp.exp(jax.random.uniform(ks[14], (DEPTH, H_SSM), f32) * (math.log(0.1) - math.log(0.001)) + math.log(0.001))
    return {
        'x_prompt': nrm(ks[0], (BATCH, SEQ, D_MODEL), 1.0),
        'x_sample': nrm(ks[1], (DEC_BATCH, DEC_SEQ, D_MODEL), 1.0),
        'cache_k': nrm(ks[2], (DEPTH, n_pool, PAGE_SIZE, H_DIFF, 2, DH_DIFF), 1.0),
        'cache_v': nrm(ks[3], (DEPTH, n_pool, PAGE_SIZE, H_DIFF, 2 * DH_DIFF), 1.0),
        'state_ssm': nrm(ks[4], (DEPTH, DEC_BATCH, H_SSM, P_SSM, N_STATE), 0.1),
        'state_conv': nrm(ks[5], (DEPTH, DEC_BATCH, CONV_W - 1, CONV_DIM), 1.0),
        'page_table': jax.random.permutation(ks[6], n_pool)[:DEC_BATCH * n_pages].reshape(DEC_BATCH, n_pages).astype(jnp.int32),
        'p_prompt': nrm(ks[7], (DEPTH, BATCH, SEQ, PLE_DIM), 1.0),
        'p_sample': nrm(ks[8], (DEPTH, DEC_BATCH, DEC_SEQ, PLE_DIM), 1.0),
        'g_mix': 1.0 + nrm(ks[9], (DEPTH, D_MODEL), 0.02),
        'w_in': nrm(ks[10], (DEPTH, D_MODEL, IN_COLS), D_MODEL ** -0.5),
        'conv_w': nrm(ks[11], (DEPTH, CONV_W, CONV_DIM), CONV_W ** -0.5),
        'conv_b': nrm(ks[12], (DEPTH, CONV_DIM), 0.02),
        'dt_bias': dt0 + jnp.log(-jnp.expm1(-dt0)),
        'a_log': jnp.log(jax.random.uniform(ks[15], (DEPTH, H_SSM), f32, 1.0, 16.0)),
        'd_skip': 1.0 + nrm(ks[16], (DEPTH, H_SSM), 0.02),
        'g_ssm_norm': 1.0 + nrm(ks[17], (DEPTH, D_SSM), 0.02),
        'lam_q1': nrm(ks[18], (DEPTH, DH_DIFF), 0.1),
        'lam_k1': nrm(ks[19], (DEPTH, DH_DIFF), 0.1),
        'lam_q2': nrm(ks[20], (DEPTH, DH_DIFF), 0.1),
        'lam_k2': nrm(ks[21], (DEPTH, DH_DIFF), 0.1),
        'g_diff_norm': 1.0 + nrm(ks[22], (DEPTH, 2 * DH_DIFF), 0.02),
        'rel_bias': nrm(ks[23], (N_BUCKETS, H_DIFF), 0.1),
        'w_out': nrm(ks[24], (DEPTH, D_MIX, D_MODEL), D_MIX ** -0.5),
        'g_ffn': 1.0 + nrm(ks[25], (DEPTH, D_MODEL), 0.02),
        'w_query': nrm(ks[26], (DEPTH, D_MODEL, PEER_HEADS * D_KEY), D_MODEL ** -0.5),
        'sub_keys': nrm(ks[27], (DEPTH, 2, N_KEYS, D_KEY // 2), (D_KEY // 2) ** -0.5),
        'expert_u': nrm(ks[28], (DEPTH, N_EXPERTS, D_MODEL), D_MODEL ** -0.5),
        'expert_v': nrm(ks[29], (DEPTH, N_EXPERTS, D_MODEL), 0.5),
        'w_ple': nrm(ks[30], (DEPTH, PLE_DIM, D_MODEL), PLE_DIM ** -0.5),
        'w_ple_gate': nrm(ks[31], (DEPTH, D_MODEL, D_MODEL), D_MODEL ** -0.5),
        'g_ple': 1.0 + nrm(ks[32], (DEPTH, D_MODEL), 0.02),
        'g_final': 1.0 + nrm(ks[33], (D_MODEL,), 0.02),
    }

def reference(x_prompt, x_sample, cache_k, cache_v, state_ssm, state_conv, page_table, p_prompt, p_sample,
              g_mix, w_in, conv_w, conv_b, dt_bias, a_log, d_skip, g_ssm_norm,
              lam_q1, lam_k1, lam_q2, lam_k2, g_diff_norm, rel_bias, w_out,
              g_ffn, w_query, sub_keys, expert_u, expert_v, w_ple, w_ple_gate, g_ple, g_final):
    dec_b = x_sample.shape[0]
    past_len = page_table.shape[1] * cache_k.shape[2]
    hp, hs = x_prompt, x_sample
    kp, vp, sp, cp = [], [], [], []
    ks_, vs_, ss_, cs_ = [], [], [], []
    for l in range(DEPTH):
        lam_init = 0.8 - 0.6 * math.exp(-0.3 * l)
        wl = dict(g_mix=g_mix[l], w_in=w_in[l], conv_w=conv_w[l], conv_b=conv_b[l], dt_bias=dt_bias[l],
                  a_log=a_log[l], d_skip=d_skip[l], g_ssm_norm=g_ssm_norm[l],
                  lam_q1=lam_q1[l], lam_k1=lam_k1[l], lam_q2=lam_q2[l], lam_k2=lam_k2[l],
                  g_diff_norm=g_diff_norm[l], rel_bias=rel_bias, w_out=w_out[l], g_ffn=g_ffn[l],
                  w_query=w_query[l], sub_keys=sub_keys[l], expert_u=expert_u[l], expert_v=expert_v[l],
                  w_ple=w_ple[l], w_ple_gate=w_ple_gate[l], g_ple=g_ple[l])
        conv0 = jnp.zeros((hp.shape[0], CONV_W - 1, CONV_DIM), hp.dtype)
        ssm0 = jnp.zeros((hp.shape[0], H_SSM, P_SSM, N_STATE), jnp.float32)
        hp, k_n, v_n, s_n, c_n = decoder_layer(hp, p_prompt[l], conv0, ssm0, None, None, 0, lam_init, **wl)
        kp.append(k_n); vp.append(v_n); sp.append(s_n); cp.append(c_n)
        past_k = cache_k[l][page_table].reshape(dec_b, past_len, H_DIFF, 2, DH_DIFF)
        past_v = cache_v[l][page_table].reshape(dec_b, past_len, H_DIFF, 2 * DH_DIFF)
        hs, k_n, v_n, s_n, c_n = decoder_layer(hs, p_sample[l], state_conv[l], state_ssm[l], past_k, past_v,
                                               past_len, lam_init, **wl)
        ks_.append(k_n); vs_.append(v_n); ss_.append(s_n); cs_.append(c_n)
    y_prompt = rmsnorm(hp, g_final)
    y_sample = rmsnorm(hs, g_final)
    return (y_prompt, y_sample, jnp.stack(kp), jnp.stack(vp), jnp.stack(sp), jnp.stack(cp),
            jnp.stack(ks_), jnp.stack(vs_), jnp.stack(ss_), jnp.stack(cs_))


_drawn_inputs = setup_inputs


def setup_inputs(seed=0):
    import zlib

    import numpy as np

    out = dict(_drawn_inputs(seed))
    spreads = {}
    factors = {'d_skip': 73.896,
     'g_diff_norm': 27.32,
     'g_ple': 200.0,
     'g_final': 22.716,
     'g_ssm_norm': 19.313,
     'g_ffn': 11.66}
    for name, (base, spread) in spreads.items():
        noise = np.random.default_rng([zlib.crc32(name.encode()), seed]).standard_normal(out[name].shape)
        drawn = base * np.exp(spread * noise) if base else spread * noise
        out[name] = jnp.asarray(drawn.astype(out[name].dtype))
    for name, factor in factors.items():
        out[name] = (out[name] * factor).astype(out[name].dtype)
    return out
```

```python
import math
from contextlib import ExitStack

import concourse.bass as bass
from concourse import mybir

F32 = mybir.dt.float32
I32 = mybir.dt.int32
U32 = mybir.dt.uint32
ALU = mybir.AluOpType
ACT = mybir.ActivationFunctionType
AX_X = mybir.AxisListType.X
ds = bass.ds

P = 128
D = 1024
KT = D // P
SEQ = 1024
PT = SEQ // P
NT = PT + 1
DEC_B, DEC_S = 8, 4
DEC = DEC_B * DEC_S
REP = P // DEC
D_SSM = 512
HS, PS, NS = 8, 64, 128
G = 2
CONV_W = 4
CONV_DIM = 1024
HD, DH = 4, 64
DV = 512
IN_COLS = 3080
C_Z, C_X, C_DT, C_Q, C_K, C_V = 0, 512, 1536, 1544, 2056, 2568
PAGES, PAGE = 16, 128
PAST = PAGES * PAGE
NEG = -1e30
EPS = 1e-6
LAM_INIT = 0.8 - 0.6 * math.exp(0.0)
X_OFF = PAST + DEC_S - 1
LINE = 3200
FAN = 2 * SEQ - 1
FAN_AT = X_OFF - (SEQ - 1)
KEYS = 128
PH, TOPK = 8, 16
SLOTS = PH * TOPK
PLE = 256


class Stage:

    def __init__(self, nc, ctx, tag):
        self.nc, self.ctx, self.tag, self.sems, self.pool_sems = nc, ctx, tag, {}, []

    def sb(self, name, shape, dt=F32):
        return self.ctx.enter_context(self.nc.sbuf_tensor(f"{self.tag}_{name}", shape, dt))

    def ps(self, name, shape, dt=F32):
        return self.ctx.enter_context(self.nc.psum_tensor(f"{self.tag}_{name}", shape, dt))

    def sem(self, name):
        s = self.ctx.enter_context(self.nc.semaphore(f"{self.tag}_{name}"))
        self.sems[name] = s
        return s

    def pool_sem(self, name):
        s = self.sem(name)
        self.pool_sems.append(s)
        return s

    def end_pass(self):
        nums = [s.num for s in self.sems.values()]
        if self.pool_sems:
            own = [s.num for s in self.pool_sems]
            self.nc.gpsimd.dma_reset(range(min(own), max(own) + 1))
        self.nc.multi_engine_barrier(list(self.nc.engines), sems_to_clear=range(min(nums), max(nums) + 1))


class Tally:

    def __init__(self, eng, sem):
        self.eng, self.sem, self.n = eng, sem, 0

    def did(self, ins):
        self.n += 1
        ins.then_inc(self.sem, 1)
        return self.n

    def settle(self):
        self.eng.wait_ge(self.sem, self.n)

    def step(self, ins):
        self.did(ins)
        self.settle()
        return self.n


def rows_of(vec, n=P):
    return vec.rearrange("(a n) -> a n", a=1).to_broadcast([n, vec.shape[0]])


def spread(vec, n=P):
    flat = vec.flatten()
    return bass.AP(flat.tensor, flat.offset, [[0, n], [1, flat.shape[-1]]])


def wide(ap, shape):
    return ap.unsqueeze(len(ap.shape)).to_broadcast(shape)


def tables(nc, t):
    with ExitStack() as ctx:
        st = Stage(nc, ctx, "tb")
        edges = st.sb("edges", [32, 2])
        rel = st.sb("rel", [32, HD])
        dist_i = st.sb("dist_i", [32, LINE], I32)
        dist = st.sb("dist", [32, LINE])
        hot = st.sb("hot", [32, LINE])
        below = st.sb("below", [HD, LINE])
        line = st.sb("line", [HD, LINE])
        ps = [st.ps(f"ps{k}", [HD, 512]) for k in range(2)]
        loaded, counted, v_done, line_mm, stored = (st.sem(n) for n in ("loaded", "counted", "v_done", "line_mm", "stored"))
        chunks = [(a, min(512, LINE - a)) for a in range(0, LINE, 512)]
        with nc.Block() as block:
            @block.sync
            def _(sp):
                sp.dma_start(edges[:], t["edges"]).then_inc(loaded, 16)
                sp.dma_start(rel[:], t["rel_bias"]).then_inc(loaded, 16)
                sp.wait_ge(v_done, 4 + len(chunks))
                sp.dma_start(t["line"], line[:]).then_inc(stored, 16)
                sp.wait_ge(stored, 16)
                for h in range(HD):
                    src = bass.AP(t["line"].tensor, h * LINE + FAN_AT, [[0, P], [1, FAN]])
                    sp.dma_start(t["fan"][h], src).then_inc(stored, 16)
                sp.wait_ge(stored, 16 * (1 + HD))

            @block.gpsimd
            def _(pool):
                pool.iota(dist_i[:], pattern=[[-1, LINE]], base=X_OFF, channel_multiplier=0).then_inc(counted, 1)

            @block.vector
            def _(dve):
                v = Tally(dve, v_done)
                dve.wait_ge(counted, 1)
                v.step(dve.tensor_copy(dist[:], dist_i[:]))
                dve.wait_ge(loaded, 32)
                v.did(dve.tensor_scalar(hot[:], dist[:], edges[:, 0:1], None, ALU.is_ge))
                v.step(dve.tensor_scalar(below[:], dist[0:HD, :], 0.0, NEG, ALU.is_lt, ALU.mult))
                v.step(dve.scalar_tensor_tensor(out=hot[:], in0=dist[:], scalar=edges[:, 1:2], in1=hot[:],
                                                op0=ALU.is_lt, op1=ALU.mult))
                for n, (a, w) in enumerate(chunks):
                    dve.wait_ge(line_mm, n + 1)
                    v.did(dve.tensor_tensor(line[:, a:a + w], ps[n % 2][:, 0:w], below[:, a:a + w], ALU.add))

            @block.tensor
            def _(pe):
                pe.wait_ge(v_done, 4)
                for n, (a, w) in enumerate(chunks):
                    if n >= 2:
                        pe.wait_ge(v_done, 4 + n - 1)
                    pe.matmul(ps[n % 2][:, 0:w], rel[:], hot[:, a:a + w], start=True, stop=True).then_inc(line_mm, 1)
        st.end_pass()


def root(act, out, ssq, n, eps):
    return act.activation(out, ssq, ACT.Sqrt, scale=1.0 / n, bias=eps)


def project(nc, t):
    with ExitStack() as ctx:
        st = Stage(nc, ctx, "pj")
        w = st.sb("w", [P, KT, IN_COLS])
        g = st.sb("g", [P, D])
        ident = st.sb("ident", [P, P])
        x = st.sb("x", [P, D])
        sq = st.sb("sq", [P, D])
        a = st.sb("a", [P, D])
        aT = st.sb("aT", [P, KT, P])
        ssq = st.sb("ssq", [P, 1])
        rs = st.sb("rs", [P, 1])
        eps = st.sb("eps", [P, 1])
        zero = st.sb("zero", [CONV_W - 1, CONV_DIM])
        zeroed = st.sem("zeroed")
        o_k, o_v, o_q, o_z = (st.sb(f"o_{n}", [P, 512]) for n in "kvqz")
        o_x = st.sb("o_x", [P, CONV_DIM])
        o_dt = st.sb("o_dt", [P, HS])
        o_kT = st.sb("o_kT", [P, 512])
        bank = [st.ps(f"bank{k}", [P, 512]) for k in range(4)]
        tr = [st.ps(f"tr{k}", [P, 4, P]) for k in range(2)]
        ktp = st.ps("ktp", [P, HD, P])
        loaded, x_in, squared, inverted, rooted, normed, turned, taken = (
            st.sem(n) for n in ("loaded", "x_in", "squared", "inverted", "rooted", "normed", "turned", "taken"))
        made, out_a, out_v, k_turned, k_taken, stored = (
            st.sem(n) for n in ("made", "out_a", "out_v", "k_turned", "k_taken", "stored"))
        w_in = t["w_in"].rearrange("(k p) n -> p k n", p=P)

        plan = [("k", C_K, 512, o_k[:]), ("v", C_V, 512, o_v[:]), ("q", C_Q, 512, o_q[:]),
                ("z", C_Z, 512, o_z[:]), ("x0", C_X, 512, o_x[:, 0:512]), ("x1", C_X + 512, 512, o_x[:, 512:]),
                ("dt", C_DT, HS, o_dt[:])]

        def norm_act(act):
            act.wait_ge(x_in, 16)
            act.activation(sq[:], x[:], ACT.Square, accum_out=ssq[:]).then_inc(squared, 1)
            act.wait_ge(squared, 1)
            root(act, rs[:], ssq[:], D, eps[:]).then_inc(rooted, 1)

        def norm_dve(dve):
            dve.wait_ge(rooted, 1)
            dve.reciprocal(rs[:], rs[:]).then_inc(inverted, 1)
            dve.wait_ge(inverted, 1)
            dve.scalar_tensor_tensor(out=a[:], in0=x[:], scalar=rs[:], in1=g[:], op0=ALU.mult,
                                     op1=ALU.mult).then_inc(normed, 1)

        def turn(pe):
            pe.wait_ge(normed, 1)
            for k in range(KT):
                last = pe.transpose(tr[k // 4][:, k % 4, :], a[:, k * P:(k + 1) * P], ident[:])
            last.then_inc(turned, 1)

        def take(act, dve=None):
            eng, half = (act, 0) if dve is None else (dve, 1)
            eng.wait_ge(turned, 1)
            if half:
                dve.tensor_copy(aT[:, 4:8, :], tr[1][:]).then_inc(taken, 1)
            else:
                act.activation(aT[:, 0:4, :], tr[0][:], ACT.Copy).then_inc(taken, 1)

        with nc.Block() as block:
            @block.sync
            def _(sp):
                sp.dma_start(x[:], t["x_all"][0:P, :]).then_inc(x_in, 16)
                sp.dma_start(ident[:], t["ident"]).then_inc(loaded, 16)
                sp.dma_start(g[:], spread(t["g_mix"])).then_inc(loaded, 16)
                for k in range(KT):
                    sp.dma_start(w[:, k, :], w_in[:, k, :]).then_inc(stored, 16)
                sp.wait_ge(zeroed, 1)
                sp.dma_start(t["xbc"][0:CONV_W - 1, :], zero[:]).then_inc(stored, 16)
                sp.wait_ge(stored, 16 * (KT + 1))

            @block.scalar
            def _(act):
                act.wait_ge(taken, 1)
                norm_act(act)
                take(act)

            @block.vector
            def _(dve):
                dve.memset(eps[:], EPS).then_inc(taken, 1)
                dve.memset(zero[:], 0.0).then_inc(zeroed, 1)
                dve.wait_ge(loaded, 32)
                norm_dve(dve)
                take(None, dve)

            @block.tensor
            def _(pe):
                pe.wait_ge(loaded, 32)
                turn(pe)
        st.end_pass()

        with nc.Fori(0, NT) as i:
            with nc.Block() as block:
                @block.sync
                def _(sp):
                    sp.dma_start(x[:], t["x_all"][ds((i + 1) * P, P), :]).then_inc(x_in, 16)
                    row = ds(i * P, P)
                    sp.wait_ge(out_a, 1)
                    sp.dma_start(t["k_all"][row, :], o_k[:]).then_inc(stored, 16)
                    sp.wait_ge(out_v, 1)
                    sp.dma_start(t["v_all"][row, :], o_v[:]).then_inc(stored, 16)
                    sp.wait_ge(out_a, 2)
                    sp.dma_start(t["qT"][row, :], o_q[:]).then_inc(stored, 16)
                    sp.wait_ge(k_taken, 1)
                    sp.dma_start(t["kT"][row, :], o_kT[:]).then_inc(stored, 16)
                    sp.wait_ge(out_v, 2)
                    sp.dma_start(t["z"][row, :], o_z[:]).then_inc(stored, 16)
                    sp.wait_ge(out_a, 3)
                    sp.wait_ge(out_v, 3)
                    sp.dma_start(t["xbc"][ds(i * P + CONV_W - 1, P), :], o_x[:]).then_inc(stored, 16)
                    sp.wait_ge(out_a, 4)
                    sp.dma_start(t["dt"][row, :], o_dt[:]).then_inc(stored, 16)
                    sp.wait_ge(stored, 16 * 7)

                @block.scalar
                def _(act):
                    norm_act(act)
                    for n in range(0, len(plan), 2):
                        act.wait_ge(made, n + 1)
                        name, _, cols, dest = plan[n]
                        act.activation(dest, bank[n % 4][:, 0:cols], ACT.Copy,
                                       scale=DH ** -0.5 if name == "q" else 1.0).then_inc(out_a, 1)
                    act.wait_ge(made, len(plan))
                    take(act)

                @block.vector
                def _(dve):
                    norm_dve(dve)
                    for n in range(1, len(plan), 2):
                        dve.wait_ge(made, n + 1)
                        _, _, cols, dest = plan[n]
                        dve.tensor_copy(dest, bank[n % 4][:, 0:cols]).then_inc(out_v, 1)
                        if n == 3:
                            dve.wait_ge(k_turned, 1)
                            dve.tensor_copy(o_kT[:], ktp[:].rearrange("p h q -> p (h q)")).then_inc(k_taken, 1)
                    dve.wait_ge(made, len(plan))
                    take(None, dve)

                @block.tensor
                def _(pe):
                    for n, (name, c0, cols, _) in enumerate(plan):
                        if n >= 4:
                            pe.wait_ge(out_a if n % 2 == 0 else out_v, (n - 4) // 2 + 1)
                        if name == "q":
                            for h in range(HD):
                                for k in range(KT):
                                    mm = pe.matmul(bank[n % 4][:, h * P:(h + 1) * P],
                                                   w[:, k, c0 + h * P:c0 + (h + 1) * P], aT[:, k, :],
                                                   start=(k == 0), stop=(k == KT - 1))
                        else:
                            for k in range(KT):
                                mm = pe.matmul(bank[n % 4][:, 0:cols], aT[:, k, :], w[:, k, c0:c0 + cols],
                                               start=(k == 0), stop=(k == KT - 1))
                        mm.then_inc(made, 1)
                        if n == 2:
                            pe.wait_ge(out_a, 1)
                            for h in range(HD):
                                mm = pe.transpose(ktp[:, h, :], o_k[:, h * P:(h + 1) * P], ident[:])
                            mm.then_inc(k_turned, 1)
                    turn(pe)
            st.end_pass()


def ssd(nc, t, sample):
    R, NB = (DEC, DEC_B) if sample else (P, 1)
    HALF = NS * 2
    with ExitStack() as ctx:
        st = Stage(nc, ctx, "ss" if sample else "sp")
        taps = st.sb("taps", [R, CONV_W, CONV_DIM])
        cbias = st.sb("cbias", [R, CONV_DIM])
        gn = st.sb("gn", [R, D_SSM])
        dskip = st.sb("dskip", [R, HS])
        dtb = st.sb("dtb", [R, HS])
        nega = st.sb("nega", [R, HS])
        cum = st.sb("cum", [R, R])
        same = st.sb("same", [R, R])
        own = st.sb("own", [R, NB])
        own_col = st.sb("own_col", [P, NB, R])
        ident = st.sb("ident", [P, P])
        ones = st.sb("ones", [R, P])
        eps = st.sb("eps", [P, 1])
        one = st.sb("one", [P, 1])
        xw = st.sb("xw", [R, CONV_W, CONV_DIM])
        xc = st.sb("xc", [R, CONV_DIM])
        z = st.sb("z", [R, D_SSM])
        dt = st.sb("dt", [R, HS])
        u, ea, ln, adt, acs, eac, dec = (st.sb(n, [R, HS]) for n in ("u", "ea", "ln", "adt", "acs", "eac", "dec"))
        adtm = st.sb("adtm", [R, NB, HS])
        adtr = st.sb("adtr", [R, HS, R])
        et = st.sb("et", [P, NB, HS])
        xdt = st.sb("xdt", [R, HS, PS])
        xdd = st.sb("xdd", [R, HS, PS])
        xdm = st.sb("xdm", [R, NB, D_SSM])
        bcT = st.sb("bcT", [P, 4, R])
        cTm = st.sb("cTm", [P, NB, G, R])
        gt = st.sb("gt", [R, G, R])
        el = st.sb("el", [R, HS, R])
        state = st.sb("state", [P, NB, D_SSM])
        y = st.sb("y", [R, D_SSM])
        skip = st.sb("skip", [R, D_SSM])
        ssq, rs = (st.sb(n, [R, G]) for n in ("ssq", "rs"))
        p_bc = st.ps("p_bc", [P, 4, P])
        p_sm = st.ps("p_sm", [P, 512])
        p_row = [st.ps(f"p_row{k}", [R, 4, P]) for k in range(2)]
        p_gt = st.ps("p_gt", [R, G, P])
        p_y = st.ps("p_y", [R, D_SSM])
        p_o = st.ps("p_o", [R, D_SSM])
        p_s = st.ps("p_s", [P, D_SSM])
        consts, loaded, z_in, v_done, a_done, stored = (
            st.sem(n) for n in ("consts", "loaded", "z_in", "v_done", "a_done", "stored"))
        (minus_abs, log_ready, adt_ready, summed, rows_up, convolved, acs_ready, less, decays, grown, activated,
         gate_ready, turned, bc_taken, scored, xdt_ready, own_ready, mixed, y_off, new_state, state_added, y_diag,
         y_ready, squared, rooted) = (
            st.sem(n) for n in (
                "minus_abs", "log_ready", "adt_ready", "summed", "rows_up", "convolved", "acs_ready", "less", "decays",
                "grown", "activated", "gate_ready", "turned", "bc_taken", "scored", "xdt_ready", "own_ready", "mixed",
                "y_off", "new_state", "state_added", "y_diag", "y_ready", "squared", "rooted"))
        n_const = 8

        with nc.Block() as block:
            @block.sync
            def _(sp):
                sp.dma_start(taps[:].rearrange("p w c -> p (w c)"), spread(t["conv_w"], R)).then_inc(consts, 16)
                sp.dma_start(cbias[:], spread(t["conv_b"], R)).then_inc(consts, 16)
                sp.dma_start(gn[:], spread(t["g_ssm_norm"], R)).then_inc(consts, 16)
                sp.dma_start(dskip[:], spread(t["d_skip"], R)).then_inc(consts, 16)
                sp.dma_start(dtb[:], spread(t["dt_bias"], R)).then_inc(consts, 16)
                sp.dma_start(nega[:], spread(t["a_log"], R)).then_inc(consts, 16)
                sp.dma_start(ident[:], t["ident"]).then_inc(consts, 16)
                sp.dma_start(cum[:], t["cum_s" if sample else "cum_p"]).then_inc(consts, 16)
                if sample:
                    sp.dma_start(same[:], t["same_s"]).then_inc(loaded, 16)
                    sp.dma_start(own[:], t["own_s"]).then_inc(loaded, 16)
                    sp.dma_start(own_col[:].rearrange("p b r -> p (b r)"), spread(t["own_cols"])).then_inc(loaded, 16)
                    sp.dma_start(state[:], t["ssm_in"].rearrange("b n c -> n b c")).then_inc(loaded, 16)
                    sp.wait_ge(loaded, 16 * 4)
                sp.wait_ge(consts, 16 * n_const)

            @block.scalar
            def _(act):
                act.wait_ge(consts, 16 * n_const)
                act.activation(nega[:], nega[:], ACT.Exp).then_inc(a_done, 1)

            @block.vector
            def _(dve):
                v = Tally(dve, v_done)
                v.did(dve.memset(eps[:], EPS))
                v.did(dve.memset(ones[:], 1.0))
                v.did(dve.memset(one[:], 1.0))
                if not sample:
                    v.did(dve.memset(same[:], 1.0))
                    v.did(dve.memset(own[:], 1.0))
                    v.did(dve.memset(state[:], 0.0))
                dve.wait_ge(a_done, 1)
                v.step(dve.tensor_scalar(nega[:], nega[:], -1.0, None, ALU.mult))
        st.end_pass()

        def one_pass(i):
            def heads(ap):
                return ap.rearrange("p (h c) -> p h c", h=HS)

            per_head = [R, HS, PS]
            row = ds(SEQ, R) if sample else ds(i * P, P)
            n_rows = CONV_W * (DEC_B if sample else 1)
            with nc.Block() as block:
                @block.sync
                def _(sp):
                    sp.dma_start(dt[:], t["dt"][row, :]).then_inc(z_in, 16)
                    sp.dma_start(z[:], t["z"][row, :]).then_inc(z_in, 16)
                    for k in range(CONV_W):
                        if sample:
                            for b in range(DEC_B):
                                sp.dma_start(xw[b * DEC_S:(b + 1) * DEC_S, k, :],
                                             t["xbc_s"][b, k:k + DEC_S, :]).then_inc(loaded, 16)
                        else:
                            sp.dma_start(xw[:, k, :], t["xbc"][ds(i * P + k, P), :]).then_inc(loaded, 16)
                    sp.wait_ge(y_ready, 3)
                    if sample:
                        for r in range(REP):
                            sp.dma_start(t["mix"][SEQ + r * R:SEQ + (r + 1) * R, 0:D_SSM], y[:]).then_inc(stored, 16)
                        sp.wait_ge(state_added, NB)
                        sp.dma_start(t["ssm_s"].rearrange("b n c -> n b c"), state[:]).then_inc(stored, 16)
                        sp.wait_ge(stored, 16 * (REP + 1))
                    else:
                        sp.dma_start(t["mix"][row, 0:D_SSM], y[:]).then_inc(stored, 16)
                        sp.wait_ge(stored, 16)

                @block.vector
                def _(dve):
                    v = Tally(dve, v_done)
                    dve.wait_ge(z_in, 32)
                    v.step(dve.tensor_tensor(u[:], dt[:], dtb[:], ALU.add))
                    dve.scalar_tensor_tensor(out=ea[:], in0=u[:], scalar=-1.0, in1=u[:], op0=ALU.mult,
                                             op1=ALU.min).then_inc(minus_abs, 1)
                    dve.wait_ge(log_ready, 2)
                    v.step(dve.scalar_tensor_tensor(out=dt[:], in0=u[:], scalar=0.0, in1=ln[:], op0=ALU.max, op1=ALU.add))
                    v.step(dve.tensor_tensor(adt[:], dt[:], nega[:], ALU.mult))
                    for b in range(NB):
                        v.did(dve.tensor_scalar(adtm[:, b, :], adt[:], own[:, b:b + 1], None, ALU.mult))
                    v.settle()
                    dve.tensor_copy(adtr[:], wide(adt[:], [R, HS, R])).then_inc(adt_ready, 1)
                    dve.wait_ge(loaded, 16 * n_rows)
                    for k in range(CONV_W):
                        v.did(dve.tensor_tensor(xw[:, k, :], xw[:, k, :], taps[:, k, :], ALU.mult))
                    v.settle()
                    v.did(dve.tensor_tensor(xw[:, 0, :], xw[:, 0, :], xw[:, 1, :], ALU.add))
                    v.step(dve.tensor_tensor(xw[:, 2, :], xw[:, 2, :], xw[:, 3, :], ALU.add))
                    v.step(dve.tensor_tensor(xw[:, 0, :], xw[:, 0, :], xw[:, 2, :], ALU.add))
                    dve.tensor_tensor(xw[:, 0, :], xw[:, 0, :], cbias[:], ALU.add).then_inc(convolved, 1)
                    dve.wait_ge(summed, 1)
                    v.step(dve.tensor_copy(acs[:], p_sm[:R, 0:HS]))
                    dve.tensor_tensor(dec[:], p_sm[:R, HS:2 * HS], acs[:], ALU.subtract).then_inc(acs_ready, 1)
                    dve.wait_ge(rows_up, 1)
                    for k in range(2):
                        v.did(dve.tensor_tensor(el[:, 4 * k:4 * k + 4, :], p_row[k][:, :, 0:R],
                                                wide(acs[:, 4 * k:4 * k + 4], [R, 4, R]), ALU.subtract))
                    v.settle()
                    dve.tensor_scalar(el[:], el[:], 0.0, None, ALU.min).then_inc(less, 1)
                    dve.wait_ge(activated, 1)
                    xs = heads(xc[:, 0:D_SSM])
                    dve.tensor_tensor(xdt[:], xs, wide(dt[:], per_head), ALU.mult).then_inc(xdt_ready, 1)
                    dve.wait_ge(xdt_ready, 1)
                    dve.wait_ge(decays, 3)
                    v.step(dve.tensor_tensor(xdd[:], xdt[:], wide(dec[:], per_head), ALU.mult))
                    dve.wait_ge(bc_taken, 1)
                    for b in range(NB):
                        v.did(dve.tensor_scalar(xdm[:, b, :], xdd[:].rearrange("p h c -> p (h c)"),
                                                own[:, b:b + 1], None, ALU.mult))
                        if sample:
                            v.did(dve.tensor_tensor(cTm[:, b], bcT[:, 2:4, :],
                                                    own_col[:, b:b + 1, :].to_broadcast([P, G, R]), ALU.mult))
                    v.settle()
                    dve.tensor_tensor(heads(skip[:]), xs, wide(dskip[:], per_head), ALU.mult).then_inc(own_ready, 1)
                    dve.wait_ge(scored, 1)
                    v.step(dve.tensor_tensor(gt[:], p_gt[:, :, 0:R],
                                             cum[:].unsqueeze(1).to_broadcast([R, G, R]), ALU.mult))
                    dve.wait_ge(grown, 1)
                    for g in range(G):
                        dve.tensor_tensor(el[:, 4 * g:4 * g + 4, :], el[:, 4 * g:4 * g + 4, :],
                                          gt[:, g:g + 1, :].to_broadcast([R, 4, R]), ALU.mult).then_inc(mixed, 1)
                    dve.wait_ge(y_off, 1)
                    v.step(dve.tensor_tensor(heads(y[:]), heads(p_o[:]), wide(eac[:], per_head), ALU.mult))
                    dve.wait_ge(y_diag, 1)
                    v.step(dve.tensor_tensor(y[:], y[:], p_y[:], ALU.add))
                    dve.wait_ge(own_ready, 1)
                    v.step(dve.tensor_tensor(y[:], y[:], skip[:], ALU.add))
                    dve.wait_ge(gate_ready, 1)
                    dve.tensor_tensor(y[:], y[:], z[:], ALU.mult).then_inc(y_ready, 1)
                    for b in range(NB):
                        sb = state[:, b, :]
                        v.step(dve.tensor_tensor(heads(sb), heads(sb), wide(et[:, b, :], [P, HS, PS]), ALU.mult))
                        dve.wait_ge(new_state, b + 1)
                        dve.tensor_tensor(sb, sb, p_s[:], ALU.add).then_inc(state_added, 1)
                    dve.wait_ge(rooted, 1)
                    v.step(dve.reciprocal(rs[:], rs[:]))
                    for g in range(G):
                        part = slice(g * HALF, (g + 1) * HALF)
                        dve.scalar_tensor_tensor(out=y[:, part], in0=y[:, part], scalar=rs[:, g:g + 1], in1=gn[:, part],
                                                 op0=ALU.mult, op1=ALU.mult).then_inc(y_ready, 1)

                @block.scalar
                def _(act):
                    act.wait_ge(minus_abs, 1)
                    act.activation(ea[:], ea[:], ACT.Exp).then_inc(log_ready, 1)
                    act.wait_ge(log_ready, 1)
                    act.activation(ln[:], ea[:], ACT.Ln, bias=one[:R]).then_inc(log_ready, 1)
                    act.wait_ge(acs_ready, 1)
                    act.activation(dec[:], dec[:], ACT.Exp).then_inc(decays, 1)
                    act.activation(eac[:], acs[:], ACT.Exp).then_inc(decays, 1)
                    act.activation(et[:].rearrange("p b h -> p (b h)"), p_sm[:, 2 * HS:2 * HS + NB * HS],
                                   ACT.Exp).then_inc(decays, 1)
                    act.wait_ge(less, 1)
                    act.activation(el[:], el[:], ACT.Exp).then_inc(grown, 1)
                    act.wait_ge(convolved, 1)
                    act.activation(xc[:], xw[:, 0, :], ACT.Silu).then_inc(activated, 1)
                    act.activation(z[:], z[:], ACT.Silu).then_inc(gate_ready, 1)
                    act.wait_ge(turned, 1)
                    act.activation(bcT[:], p_bc[:, :, 0:R], ACT.Copy).then_inc(bc_taken, 1)
                    act.wait_ge(y_ready, 1)
                    act.wait_ge(mixed, G)
                    for g in range(G):
                        part = slice(g * HALF, (g + 1) * HALF)
                        act.activation(skip[:, part], y[:, part], ACT.Square,
                                       accum_out=ssq[:, g:g + 1]).then_inc(squared, 1)
                    act.wait_ge(squared, G)
                    root(act, rs[:], ssq[:], HALF, eps[:R]).then_inc(rooted, 1)

                @block.tensor
                def _(pe):
                    pe.wait_ge(adt_ready, 1)
                    pe.matmul(p_sm[:R, 0:HS], cum[:], adt[:], start=True, stop=True)
                    pe.matmul(p_sm[:R, HS:2 * HS], same[:], adt[:], start=True, stop=True)
                    pe.matmul(p_sm[:, 2 * HS:2 * HS + NB * HS], ones[:], adtm[:].rearrange("p b h -> p (b h)"),
                              start=True, stop=True).then_inc(summed, 1)
                    for h in range(HS):
                        mm = pe.matmul(p_row[h // 4][:, h % 4, 0:R], adtr[:, h, :], cum[:], start=True, stop=True)
                    mm.then_inc(rows_up, 1)
                    pe.wait_ge(activated, 1)
                    for k in range(4):
                        mm = pe.transpose(p_bc[:, k, 0:R], xc[:, D_SSM + k * NS:D_SSM + (k + 1) * NS], ident[:R, :R])
                    mm.then_inc(turned, 1)
                    pe.wait_ge(bc_taken, 1)
                    for g in range(G):
                        mm = pe.matmul(p_gt[:, g, 0:R], bcT[:, g, :], bcT[:, 2 + g, :], start=True, stop=True)
                    mm.then_inc(scored, 1)
                    pe.wait_ge(own_ready, 1)
                    for g in range(G):
                        for b in range(NB):
                            c = cTm[:, b, g, :] if sample else bcT[:, 2 + g, :]
                            mm = pe.matmul(p_o[:, g * HALF:(g + 1) * HALF], c, state[:, b, g * HALF:(g + 1) * HALF],
                                           start=(b == 0), stop=(b == NB - 1))
                    mm.then_inc(y_off, 1)
                    for b in range(NB):
                        if b:
                            pe.wait_ge(state_added, b)
                        for g in range(G):
                            part = slice(g * HALF, (g + 1) * HALF)
                            mm = pe.matmul(p_s[:, part], xc[:, D_SSM + g * NS:D_SSM + (g + 1) * NS], xdm[:, b, part],
                                           start=True, stop=True)
                        mm.then_inc(new_state, 1)
                        if b == 0:
                            for h in range(HS):
                                pe.wait_ge(mixed, h // 4 + 1)
                                mm = pe.matmul(p_y[:, h * PS:(h + 1) * PS], el[:, h, :], xdt[:, h, :],
                                               start=True, stop=True)
                            mm.then_inc(y_diag, 1)
            st.end_pass()

        if sample:
            one_pass(None)
        else:
            with nc.Fori(0, PT) as i:
                one_pass(i)
            with nc.Block() as block:
                @block.sync
                def _(sp):
                    sp.dma_start(t["ssm_p"], state[:, 0, :]).then_inc(stored, 16)
                    sp.wait_ge(stored, 16)
            st.end_pass()


def between(nc, t, copies):
    with ExitStack() as ctx:
        st = Stage(nc, ctx, "cp")
        stored = st.sem("stored")
        with nc.Block() as block:
            @block.sync
            def _(sp):
                for dst, src in copies:
                    sp.dma_start(dst, src).then_inc(stored, 16)
                sp.wait_ge(stored, 16 * len(copies))
        st.end_pass()


def split_conv(nc, t):
    new = t["xbc"][CONV_W - 1 + SEQ:CONV_W - 1 + SEQ + DEC, :].rearrange("(b s) c -> b s c", s=DEC_S)
    between(nc, t, [(t["xbc_s"][:, 0:CONV_W - 1, :], t["state_conv"]), (t["xbc_s"][:, CONV_W - 1:, :], new),
                    (t["conv_p"], t["xbc"][SEQ:SEQ + CONV_W - 1, :]), (t["conv_s"], new[:, 1:, :])])


def lambdas(act, dve, v, lq, prod, sums, lam, ready, back):
    if dve is not None:
        for m in range(2):
            v.did(dve.tensor_tensor(prod[:, m, :], lq[:, 2 * m, :], lq[:, 2 * m + 1, :], ALU.mult))
        v.settle()
        dve.tensor_reduce(sums[:], prod[:], AX_X, ALU.add).then_inc(ready, 1)
        dve.wait_ge(back, 1)
        dve.scalar_tensor_tensor(out=lam[:], in0=sums[:, 0:1], scalar=LAM_INIT, in1=sums[:, 1:2], op0=ALU.add,
                                 op1=ALU.subtract).then_inc(ready, 1)
    else:
        act.wait_ge(ready, 1)
        act.activation(sums[:], sums[:], ACT.Exp).then_inc(back, 1)


def attend_prompt(nc, t):
    with ExitStack() as ctx:
        st = Stage(nc, ctx, "ap")
        kT = st.sb("kT", [P, HD, SEQ])
        val = st.sb("val", [P, PT, DV])
        ident = st.sb("ident", [P, P])
        gd = st.sb("gd", [P, 2 * DH])
        lq = st.sb("lq", [P, 4, DH])
        prod = st.sb("prod", [P, 2, DH])
        sums = st.sb("sums", [P, 2])
        lam = st.sb("lam", [P, 1])
        eps = st.sb("eps", [P, 1])
        qT = st.sb("qT", [P, HD, P])
        bias = st.sb("bias", [P, HD, SEQ])
        s = [st.sb(f"s{k}", [P, SEQ]) for k in range(4)]
        mx = st.sb("mx", [P, 2 * HD])
        total = st.sb("total", [P, 2 * HD])
        inv = st.sb("inv", [P, 2 * HD])
        wT = [st.sb(f"wT{k}", [P, PT, P]) for k in range(2)]
        o = st.sb("o", [P, HD, 2 * DH])
        sq = st.sb("sq", [P, 2 * DH])
        ssq, rs = (st.sb(n, [P, HD]) for n in ("ssq", "rs"))
        p_s = [st.ps(f"p_s{k}", [P, SEQ]) for k in range(2)]
        p_t = [st.ps(f"p_t{k}", [P, 4, P]) for k in range(2)]
        p_o = st.ps("p_o", [P, HD, P])
        consts, q_in, b_in, v_done, stored = (st.sem(n) for n in ("consts", "q_in", "b_in", "v_done", "stored"))
        (lam_ready, lam_back, scored, maxed, grown, weighed, turned, taken_a, taken_v, mixed, o_ready, squared, rooted,
         o_done) = (
            st.sem(n) for n in (
                "lam_ready", "lam_back", "scored", "maxed", "grown", "weighed", "turned", "taken_a", "taken_v", "mixed",
                "o_ready", "squared", "rooted", "o_done"))

        with nc.Block() as block:
            @block.sync
            def _(sp):
                sp.dma_start(ident[:], t["ident"]).then_inc(consts, 16)
                sp.dma_start(gd[:], spread(t["g_diff_norm"])).then_inc(consts, 16)
                for n in range(4):
                    sp.dma_start(lq[:, n, :], spread(t["lam"][n])).then_inc(consts, 16)
                for j in range(PT):
                    sp.dma_start(kT[:, :, j * P:(j + 1) * P],
                                 t["kT"][j * P:(j + 1) * P, :].rearrange("p (h k) -> p h k", h=HD)).then_inc(q_in, 16)
                    sp.dma_start(val[:, j, :], t["v_all"][j * P:(j + 1) * P, :]).then_inc(q_in, 16)
                sp.wait_ge(q_in, 16 * 2 * PT)

            @block.scalar
            def _(act):
                lambdas(act, None, None, lq, prod, sums, lam, lam_ready, lam_back)

            @block.vector
            def _(dve):
                v = Tally(dve, v_done)
                v.did(dve.memset(eps[:], EPS))
                dve.wait_ge(consts, 16 * 6)
                v.did(dve.tensor_scalar(gd[:], gd[:], 1.0 - LAM_INIT, None, ALU.mult))
                lambdas(None, dve, v, lq, prod, sums, lam, lam_ready, lam_back)
        st.end_pass()

        with nc.Fori(0, PT) as i:
            with nc.Block() as block:
                @block.sync
                def _(sp):
                    sp.dma_start(qT[:].rearrange("p h q -> p (h q)"), t["qT"][ds(i * P, P), :]).then_inc(q_in, 16)
                    for h in range(HD):
                        sp.dma_start(bias[:, h, :], bass.AP(
                            t["fan"].tensor, h * P * FAN + SEQ - 1 - i * P, [[FAN - 1, P], [1, SEQ]])).then_inc(b_in, 16)
                    sp.wait_ge(o_done, 1 + HD)
                    sp.dma_start(t["mix"][ds(i * P, P), D_SSM:], o[:].rearrange("p h e -> p (h e)")).then_inc(stored, 16)
                    sp.wait_ge(stored, 16)

                @block.tensor
                def _(pe):
                    def scores(n):
                        h, m = n // 2, n % 2
                        if n >= 2:
                            pe.wait_ge(maxed, n - 1)
                        part = slice(m * DH, (m + 1) * DH)
                        for c in range(0, SEQ, 512):
                            mm = pe.matmul(p_s[n % 2][:, c:c + 512], qT[part, h, :], kT[part, h, c:c + 512],
                                           start=True, stop=True)
                        mm.then_inc(scored, 1)

                    def values(h):
                        pe.wait_ge(weighed, h + 1)
                        for half in range(2):
                            if h:
                                pe.wait_ge(taken_v if half else taken_a, h)
                            for j in range(4):
                                c = (4 * half + j) * P
                                mm = pe.transpose(p_t[half][:, j, :], s[2 * (h % 2)][:, c:c + P], ident[:])
                            mm.then_inc(turned, 1)
                        for j in range(PT):
                            if j % 4 == 0:
                                pe.wait_ge(taken_v if j else taken_a, h + 1)
                            mm = pe.matmul(p_o[:, h, :], wT[h % 2][:, j, :], val[:, j, h * P:(h + 1) * P],
                                           start=(j == 0), stop=(j == PT - 1))
                        mm.then_inc(mixed, 1)

                    pe.wait_ge(q_in, 16)
                    for n in range(2 * HD):
                        scores(n)
                        if n >= 3 and n % 2:
                            values(n // 2 - 1)
                    values(HD - 1)

                @block.vector
                def _(dve):
                    v = Tally(dve, v_done)

                    def weigh(h):
                        a, b = s[2 * (h % 2)], s[2 * (h % 2) + 1]
                        dve.wait_ge(grown, 2 * h + 2)
                        v.step(dve.reciprocal(inv[:, 2 * h:2 * h + 2], total[:, 2 * h:2 * h + 2]))
                        v.step(dve.tensor_tensor(inv[:, 2 * h + 1:2 * h + 2], inv[:, 2 * h + 1:2 * h + 2], lam[:], ALU.mult))
                        v.step(dve.tensor_scalar(b[:], b[:], inv[:, 2 * h + 1:2 * h + 2], None, ALU.mult))
                        dve.scalar_tensor_tensor(out=a[:], in0=a[:], scalar=inv[:, 2 * h:2 * h + 1], in1=b[:],
                                                 op0=ALU.mult, op1=ALU.subtract).then_inc(weighed, 1)

                    def take(h):
                        dve.wait_ge(turned, 2 * h + 2)
                        if h >= 2:
                            dve.wait_ge(mixed, h - 1)
                        dve.tensor_copy(wT[h % 2][:, 4:8, :], p_t[1][:]).then_inc(taken_v, 1)

                    dve.wait_ge(b_in, 16 * HD)
                    for n in range(2 * HD):
                        h = n // 2
                        dve.wait_ge(scored, n + 1)
                        if h >= 2:
                            dve.wait_ge(turned, 2 * (h - 1))
                        dve.tensor_tensor_reduce(out=s[n % 4][:], in0=p_s[n % 2][:], in1=bias[:, h, :], scale=1.0,
                                                 scalar=NEG, op0=ALU.add, op1=ALU.max,
                                                 accum_out=mx[:, n:n + 1]).then_inc(maxed, 1)
                        dve.wait_ge(maxed, n + 1)
                        dve.tensor_scalar(mx[:, n:n + 1], mx[:, n:n + 1], -1.0, None, ALU.mult).then_inc(o_ready, 1)
                        if n >= 3 and n % 2:
                            weigh(n // 2 - 1)
                            take(n // 2 - 1)
                    weigh(HD - 1)
                    take(HD - 1)
                    dve.wait_ge(mixed, HD)
                    dve.tensor_copy(o[:], p_o[:]).then_inc(o_done, 1)
                    dve.wait_ge(rooted, 1)
                    v.step(dve.reciprocal(rs[:], rs[:]))
                    for h in range(HD):
                        dve.scalar_tensor_tensor(out=o[:, h, :], in0=o[:, h, :], scalar=rs[:, h:h + 1], in1=gd[:],
                                                 op0=ALU.mult, op1=ALU.mult).then_inc(o_done, 1)

                @block.scalar
                def _(act):
                    def take(h):
                        act.wait_ge(turned, 2 * h + 1)
                        if h >= 2:
                            act.wait_ge(mixed, h - 1)
                        act.activation(wT[h % 2][:, 0:4, :], p_t[0][:], ACT.Copy).then_inc(taken_a, 1)

                    for n in range(2 * HD):
                        act.wait_ge(o_ready, n + 1)
                        act.activation(s[n % 4][:], s[n % 4][:], ACT.Exp, bias=mx[:, n:n + 1],
                                       accum_out=total[:, n:n + 1]).then_inc(grown, 1)
                        if n >= 3 and n % 2:
                            take(n // 2 - 1)
                    take(HD - 1)
                    act.wait_ge(o_done, 1)
                    for h in range(HD):
                        if h:
                            act.wait_ge(squared, h)
                        act.activation(sq[:], o[:, h, :], ACT.Square, accum_out=ssq[:, h:h + 1]).then_inc(squared, 1)
                    act.wait_ge(squared, HD)
                    root(act, rs[:], ssq[:], 2 * DH, eps[:]).then_inc(rooted, 1)
            st.end_pass()


def attend_sample(nc, t):
    NR, NW = 2 * HD * DEC_S, HD * DEC_S
    NKEY = PAST + DEC_S
    with ExitStack() as ctx:
        st = Stage(nc, ctx, "as")
        kT = [st.sb(f"kT{k}", [P, PAGES, HD * PAGE]) for k in range(2)]
        val = [st.sb(f"val{k}", [P, PAGES, DV]) for k in range(2)]
        kN = [st.sb(f"kN{k}", [P, HD, DEC_S]) for k in range(2)]
        vN = [st.sb(f"vN{k}", [DEC_S, DV]) for k in range(2)]
        pages = st.sb("pages", [1, PAGES * (DEC_B + 1)], I32)
        qT = st.sb("qT", [P, HD, DEC])
        qm = st.sb("qm", [P, HD, DEC_B, NR])
        bias = st.sb("bias", [NR, NKEY])
        sel = st.sb("sel", [NR, NW])
        lq = st.sb("lq", [P, 4, DH])
        prod = st.sb("prod", [P, 2, DH])
        sums = st.sb("sums", [P, 2])
        lam = st.sb("lam", [P, 1])
        sign = st.sb("sign", [NR, 2])
        coef = st.sb("coef", [NR, 1])
        eps = st.sb("eps", [P, 1])
        gd = st.sb("gd", [DEC, 2 * DH])
        ident = st.sb("ident", [P, P])
        s = st.sb("s", [NR, NKEY])
        mx, total, inv = (st.sb(n, [NR, 1]) for n in ("mx", "total", "inv"))
        mix = st.sb("mix", [NR, NW])
        qc = [st.sb(f"qc{k}", [P, HD, NR]) for k in range(2)]
        wT = st.sb("wT", [P, PAGES + 1, NW])
        oT = st.sb("oT", [P, HD, DEC])
        o = st.sb("o", [DEC, HD, 2 * DH])
        sq = st.sb("sq", [DEC, 2 * DH])
        ssq, rs = (st.sb(n, [DEC, HD]) for n in ("ssq", "rs"))
        p_s = st.ps("p_s", [NR, PAST])
        p_n = st.ps("p_n", [NR, DEC_S])
        p_w = st.ps("p_w", [P, PAGES + 1, NW])
        p_o = st.ps("p_o", [P, HD, DEC_S])
        p_t = st.ps("p_t", [DEC, HD, P])
        consts, v_done, stored, first = (st.sem(n) for n in ("consts", "v_done", "stored", "first"))
        k_in = [st.sem(f"k_in{k}") for k in range(2)]
        v_in = [st.sem(f"v_in{k}") for k in range(2)]
        (lam_ready, lam_back, scored, maxed, neg_ready, grown, mix_ready, weighed, w_taken, mixed, o_taken, turned,
         squared, rooted, o_done) = (
            st.sem(n) for n in (
                "lam_ready", "lam_back", "scored", "maxed", "neg_ready", "grown", "mix_ready", "weighed", "w_taken",
                "mixed", "o_taken", "turned", "squared", "rooted", "o_done"))
        k_pool = t["cache_kT"]
        v_pool = t["cache_v"]
        N_POOL = k_pool.shape[0]

        def fetch_keys(eng, b, slot):
            for p in range(PAGES):
                page = eng.value_load(pages[0:1, ds(b * PAGES + p, 1)], min_val=0, max_val=N_POOL - 1)
                eng.dma_start(kT[slot][:, p, :], k_pool[ds(page, 1), :, :].rearrange("a p n -> p (a n)")).then_inc(
                    k_in[slot], 16)

        def fetch_values(eng, b, slot):
            for p in range(PAGES):
                page = eng.value_load(pages[0:1, ds(b * PAGES + p, 1)], min_val=0, max_val=N_POOL - 1)
                eng.dma_start(val[slot][:, p, :], v_pool[ds(page, 1), :, :].rearrange("a p n -> p (a n)")).then_inc(
                    v_in[slot], 16)

        def fetch_new(eng, b, slot):
            kt = t["kT"][SEQ:SEQ + P, :].rearrange("p (h q) -> p h q", h=HD)
            eng.dma_start(kN[slot][:], kt[:, :, ds(b * DEC_S, DEC_S)]).then_inc(k_in[slot], 16)
            eng.dma_start(vN[slot][:], t["v_all"][ds(SEQ + b * DEC_S, DEC_S), :]).then_inc(v_in[slot], 16)

        with nc.Block() as block:
            @block.sync
            def _(sp):
                sp.dma_start(pages[:], t["pages"]).then_inc(first, 16)
                sp.dma_start(ident[:], t["ident"]).then_inc(consts, 16)
                sp.dma_start(gd[:], spread(t["g_diff_norm"], DEC)).then_inc(consts, 16)
                for n in range(4):
                    sp.dma_start(lq[:, n, :], spread(t["lam"][n])).then_inc(consts, 16)
                sp.dma_start(sel[:], t["sel_w"]).then_inc(consts, 16)
                sp.dma_start(sign[:], t["sign_w"]).then_inc(consts, 16)
                sp.dma_start(qT[:], t["qT"][SEQ:SEQ + P, :].rearrange("p (h q) -> p h q", h=HD)[:, :, 0:DEC]).then_inc(
                    consts, 16)
                for m in range(2):
                    for tok in range(DEC_S):
                        r = m * NW + tok
                        sp.dma_start(bias[r:r + NW - DEC_S + 1:DEC_S, :],
                                     bass.AP(t["line"].tensor, X_OFF - PAST - tok, [[LINE, HD], [1, NKEY]])).then_inc(
                            consts, 16)
                sp.wait_ge(first, 16)
                fetch_keys(sp, 0, 0)
                fetch_new(sp, 0, 0)
                sp.wait_ge(consts, 16 * (9 + 2 * HD))
                sp.wait_ge(k_in[0], 16 * (PAGES + 1))

            @block.scalar
            def _(act):
                act.wait_ge(first, 16)
                fetch_values(act, 0, 0)
                lambdas(act, None, None, lq, prod, sums, lam, lam_ready, lam_back)
                act.wait_ge(v_in[0], 16 * (PAGES + 1))

            @block.vector
            def _(dve):
                v = Tally(dve, v_done)
                v.did(dve.memset(eps[:], EPS))
                v.did(dve.memset(qm[:], 0.0))
                dve.wait_ge(consts, 16 * (9 + 2 * HD))
                v.did(dve.tensor_scalar(gd[:], gd[:], 1.0 - LAM_INIT, None, ALU.mult))
                lambdas(None, dve, v, lq, prod, sums, lam, lam_ready, lam_back)
                dve.wait_ge(lam_ready, 2)
                v.settle()
                v.step(dve.scalar_tensor_tensor(out=coef[:], in0=sign[:, 1:2], scalar=lam[0:NR, :], in1=sign[:, 0:1],
                                                op0=ALU.mult, op1=ALU.add))
                for m in range(2):
                    for h in range(HD):
                        r = (m * HD + h) * DEC_S
                        part = slice(m * DH, (m + 1) * DH)
                        v.did(dve.tensor_copy(qm[part, h, :, r:r + DEC_S],
                                              qT[part, h, :].rearrange("p (b s) -> p b s", s=DEC_S)))
                v.settle()
        st.end_pass()

        with nc.Fori(0, DEC_B // 2) as i:
            with nc.Block() as block:
                @block.sync
                def _(sp):
                    fetch_keys(sp, 2 * i + 1, 1)
                    fetch_new(sp, 2 * i + 1, 1)
                    sp.wait_ge(scored, 1)
                    sp.wait_ge(mixed, 1)
                    fetch_keys(sp, 2 * i + 2, 0)
                    fetch_new(sp, 2 * i + 2, 0)
                    sp.wait_ge(k_in[0], 16 * (PAGES + 1))
                    sp.wait_ge(v_in[0], 16 * (PAGES + 1))

                @block.tensor
                def _(pe):
                    for k in range(2):
                        if k:
                            pe.wait_ge(k_in[1], 16 * (PAGES + 1))
                            pe.wait_ge(maxed, 2)
                        pe.wait_ge(w_taken, 2 * k + 1)
                        for c in range(PAGES // 4):
                            for h in range(HD):
                                pe.matmul(p_s[:, c * 512:(c + 1) * 512], qc[k][:, h, :],
                                          kT[k][:, 4 * c:4 * c + 4, h * PAGE:(h + 1) * PAGE],
                                          start=(h == 0), stop=(h == HD - 1))
                        for h in range(HD):
                            mm = pe.matmul(p_n[:], qc[k][:, h, :], kN[k][:, h, :], start=(h == 0), stop=(h == HD - 1))
                        mm.then_inc(scored, 1)
                        pe.wait_ge(mix_ready, k + 1)
                        for p in range(PAGES):
                            pe.matmul(p_w[:, p, :], s[:, p * PAGE:(p + 1) * PAGE], mix[:], start=True, stop=True)
                        pe.matmul(p_w[0:DEC_S, PAGES, :], s[:, PAST:], mix[:], start=True, stop=True).then_inc(weighed, 1)
                        pe.wait_ge(w_taken, 2 * k + 2)
                        if k:
                            pe.wait_ge(v_in[1], 16 * (PAGES + 1))
                            pe.wait_ge(o_taken, 1)
                        for h in range(HD):
                            cols = slice(h * DEC_S, (h + 1) * DEC_S)
                            for p in range(PAGES):
                                pe.matmul(p_o[:, h, :], val[k][:, p, h * P:(h + 1) * P], wT[:, p, cols],
                                          start=(p == 0), stop=False)
                            mm = pe.matmul(p_o[:, h, :], vN[k][:, h * P:(h + 1) * P], wT[0:DEC_S, PAGES, cols],
                                           start=False, stop=True)
                        mm.then_inc(mixed, 1)

                @block.vector
                def _(dve):
                    v = Tally(dve, v_done)
                    for k in range(2):
                        if k:
                            dve.wait_ge(scored, 1)
                        dve.tensor_copy(qc[k][:], qm[:, :, ds(2 * i + k, 1), :].rearrange("p h a r -> p h (a r)")).then_inc(
                            w_taken, 1)
                        dve.wait_ge(scored, k + 1)
                        if k:
                            dve.wait_ge(weighed, 1)
                        dve.tensor_tensor_reduce(out=s[:, 0:PAST], in0=p_s[:], in1=bias[:, 0:PAST], scale=1.0,
                                                 scalar=NEG, op0=ALU.add, op1=ALU.max, accum_out=mx[:]).then_inc(maxed, 1)
                        dve.wait_ge(maxed, 2 * k + 1)
                        dve.tensor_tensor_reduce(out=s[:, PAST:], in0=p_n[:], in1=bias[:, PAST:], scale=1.0,
                                                 scalar=mx[:], op0=ALU.add, op1=ALU.max, accum_out=inv[:]).then_inc(maxed, 1)
                        dve.wait_ge(maxed, 2 * k + 2)
                        dve.tensor_scalar(mx[:], inv[:], -1.0, None, ALU.mult).then_inc(neg_ready, 1)
                        dve.wait_ge(grown, k + 1)
                        v.step(dve.reciprocal(inv[:], total[:]))
                        v.step(dve.tensor_tensor(inv[:], inv[:], coef[:], ALU.mult))
                        dve.tensor_scalar(mix[:], sel[:], inv[:], None, ALU.mult).then_inc(mix_ready, 1)
                        dve.wait_ge(weighed, k + 1)
                        if k:
                            dve.wait_ge(mixed, 1)
                        v.did(dve.tensor_copy(wT[:, 0:PAGES, :], p_w[:, 0:PAGES, :]))
                        v.settle()
                        dve.tensor_copy(wT[0:DEC_S, PAGES, :], p_w[0:DEC_S, PAGES, :]).then_inc(w_taken, 1)
                        dve.wait_ge(mixed, k + 1)
                        dve.tensor_copy(oT[:, :, ds((2 * i + k) * DEC_S, DEC_S)], p_o[:]).then_inc(o_taken, 1)

                @block.scalar
                def _(act):
                    fetch_values(act, 2 * i + 1, 1)
                    for k in range(2):
                        act.wait_ge(neg_ready, k + 1)
                        act.activation(s[:], s[:], ACT.Exp, bias=mx[:], accum_out=total[:]).then_inc(grown, 1)
                        if k == 0:
                            act.wait_ge(mixed, 1)
                            fetch_values(act, 2 * i + 2, 0)
                    act.wait_ge(v_in[1], 16 * (PAGES + 1))
            st.end_pass()

        with nc.Block() as block:
            @block.tensor
            def _(pe):
                for h in range(HD):
                    mm = pe.transpose(p_t[:, h, :], oT[:, h, :], ident[:])
                mm.then_inc(turned, 1)

            @block.scalar
            def _(act):
                act.wait_ge(o_done, 1)
                for h in range(HD):
                    if h:
                        act.wait_ge(squared, h)
                    act.activation(sq[:], o[:, h, :], ACT.Square, accum_out=ssq[:, h:h + 1]).then_inc(squared, 1)
                act.wait_ge(squared, HD)
                root(act, rs[:], ssq[:], 2 * DH, eps[:DEC]).then_inc(rooted, 1)

            @block.vector
            def _(dve):
                v = Tally(dve, v_done)
                dve.wait_ge(turned, 1)
                dve.tensor_copy(o[:], p_t[:]).then_inc(o_done, 1)
                dve.wait_ge(rooted, 1)
                v.step(dve.reciprocal(rs[:], rs[:]))
                for h in range(HD):
                    dve.scalar_tensor_tensor(out=o[:, h, :], in0=o[:, h, :], scalar=rs[:, h:h + 1], in1=gd[:],
                                             op0=ALU.mult, op1=ALU.mult).then_inc(o_done, 1)

            @block.sync
            def _(sp):
                sp.wait_ge(o_done, 1 + HD)
                for r in range(REP):
                    sp.dma_start(t["mix"][SEQ + r * DEC:SEQ + (r + 1) * DEC, D_SSM:],
                                 o[:].rearrange("p h e -> p (h e)")).then_inc(stored, 16)
                sp.wait_ge(stored, 16 * REP)
        st.end_pass()


def experts(nc, t):
    RING = 14
    GRP = TOPK
    with ExitStack() as ctx:
        st = Stage(nc, ctx, "ex")
        wo = st.sb("wo", [P, KT, D])
        wq = st.sb("wq", [P, KT, 2 * PH * KEYS])
        keysT = st.sb("keysT", [P, 2, KEYS])
        ident = st.sb("ident", [P, P])
        fold = st.sb("fold", [P, DEC])
        g = st.sb("g", [P, D])
        eps = st.sb("eps", [P, 1])
        iota_i = st.sb("iota_i", [P, TOPK], I32)
        iota = st.sb("iota", [P, TOPK])
        ring = st.sb("ring", [P, RING, D])
        m_cur = st.sb("m_cur", [P, D])
        idx_cur = st.sb("idx_cur", [P, SLOTS], I32)
        gate_cur = st.sb("gate_cur", [P, SLOTS])
        dots = st.sb("dots", [P, SLOTS])
        act_out = st.sb("act_out", [P, SLOTS])
        coef = st.sb("coef", [P, SLOTS])
        diag = st.sb("diag", [P, 4, P])
        h1_cur = st.sb("h1_cur", [P, D])
        h1 = st.sb("h1", [P, D])
        m = st.sb("m", [P, D])
        aT = st.sb("aT", [P, KT, P])
        ssq, rs = (st.sb(n, [P, 1]) for n in ("ssq", "rs"))
        qT = [st.sb(f"qT{k}", [P, 4, P]) for k in range(2)]
        s = st.sb("s", [P, 4, KEYS])
        s_less = st.sb("s_less", [P, 4, KEYS])
        top = st.sb("top", [P, 4, TOPK])
        top_i = st.sb("top_i", [P, 4, TOPK], U32)
        top_f = st.sb("top_f", [P, 4, TOPK])
        cand = st.sb("cand", [P, 2, TOPK, TOPK])
        cand_less = st.sb("cand_less", [P, 2, TOPK * TOPK])
        best = st.sb("best", [P, 2, TOPK])
        pos = st.sb("pos", [P, 2 * TOPK], U32)
        side_i = st.sb("side_i", [P, 2, 2 * TOPK], U32)
        side = st.sb("side", [P, 2, 2 * TOPK])
        hot = st.sb("hot", [P, 2, 2 * TOPK, TOPK])
        pick = st.sb("pick", [P, 2, 2 * TOPK])
        idx_f = st.sb("idx_f", [P, 2 * TOPK])
        neg = st.sb("neg", [P, 2])
        total = st.sb("total", [P, 2])
        idx_next = st.sb("idx_next", [P, SLOTS], I32)
        gate_next = st.sb("gate_next", [P, SLOTS])
        acc = [st.ps(f"acc{k}", [P, 512]) for k in range(2)]
        pt = [st.ps(f"pt{k}", [P, 512]) for k in range(2)]
        pq = [st.ps(f"pq{k}", [P, 4, P]) for k in range(2)]
        pk = [st.ps(f"pk{k}", [P, 4, KEYS]) for k in range(2)]
        consts, v_done, h_done, copied, h1_in, stored = (
            st.sem(n) for n in ("consts", "v_done", "h_done", "copied", "h1_in", "stored"))
        u_used, v_used, gelu_done, coef_ready, diag_ready, folded, h2_ready = (
            st.sem(n) for n in ("u_used", "v_used", "gelu_done", "coef_ready", "diag_ready", "folded", "h2_ready"))
        (x_in, f_turned, f_taken_a, f_taken_v, projected, h1_ready, squared, rooted, m_ready, q_made, q_taken, s_made,
         s_taken, ranked, grown) = (
            st.sem(n) for n in (
                "x_in", "f_turned", "f_taken_a", "f_taken_v", "projected", "h1_ready", "squared", "rooted", "m_ready",
                "q_made", "q_taken", "s_made", "s_taken", "ranked", "grown"))
        came = [st.pool_sem(f"came{k}") for k in range(RING)]

        class Front:

            def __init__(self, tile):
                self.row = tile

            def sync(self, sp):
                sp.dma_start(m[:], t["mix"][self.row, :]).then_inc(x_in, 16)
                sp.dma_start(h1[:], t["x_all"][self.row, :]).then_inc(x_in, 16)
                sp.wait_ge(h1_ready, 2)
                sp.dma_start(t["h1"][self.row, :], h1[:]).then_inc(stored, 16)

            @staticmethod
            def tensor(pe, piece):
                if piece in (0, 1):
                    pe.wait_ge(x_in, 32) if piece == 0 else pe.wait_ge(m_ready, 1)
                    for k in range(KT):
                        mm = pe.transpose(pt[k // 4][:, (k % 4) * P:(k % 4 + 1) * P], m[:, k * P:(k + 1) * P], ident[:])
                    mm.then_inc(f_turned, 1)
                if piece == 0:
                    pe.wait_ge(f_taken_a, 1)
                    pe.wait_ge(f_taken_v, 1)
                    for n in range(2):
                        for k in range(KT):
                            mm = pe.matmul(pt[n][:], aT[:, k, :], wo[:, k, n * 512:(n + 1) * 512],
                                           start=(k == 0), stop=(k == KT - 1))
                        mm.then_inc(projected, 1)
                if piece >= 1:
                    n = piece - 1
                    if n == 0:
                        pe.wait_ge(f_taken_a, 2)
                        pe.wait_ge(f_taken_v, 2)
                    if n < 4:
                        if n >= 2:
                            pe.wait_ge(q_taken, n - 1)
                        for j in range(4):
                            c = (4 * n + j) * KEYS
                            for k in range(KT):
                                mm = pe.matmul(pq[n % 2][:, j, :], wq[:, k, c:c + KEYS], aT[:, k, :],
                                               start=(k == 0), stop=(k == KT - 1))
                        mm.then_inc(q_made, 1)
                        pe.wait_ge(q_taken, n + 1)
                        if n >= 2:
                            pe.wait_ge(s_taken, n - 1)
                        for j in range(4):
                            mm = pe.matmul(pk[n % 2][:, j, :], qT[n % 2][:, j, :], keysT[:, j % 2, :], start=True, stop=True)
                        mm.then_inc(s_made, 1)

            @staticmethod
            def scalar(act, piece):
                if piece in (0, 1):
                    act.wait_ge(f_turned, piece + 1)
                    act.activation(aT[:, 0:4, :].rearrange("p k q -> p (k q)"), pt[0][:], ACT.Copy).then_inc(f_taken_a, 1)
                if piece == 0:
                    act.wait_ge(h1_ready, 2)
                    act.activation(m[:], h1[:], ACT.Square, accum_out=ssq[:]).then_inc(squared, 1)
                    act.wait_ge(squared, 1)
                    root(act, rs[:], ssq[:], D, eps[:]).then_inc(rooted, 1)
                if 1 <= piece < 5:
                    n = piece - 1
                    act.wait_ge(q_made, n + 1)
                    if n >= 2:
                        act.wait_ge(s_made, n - 1)
                    act.activation(qT[n % 2][:], pq[n % 2][:], ACT.Copy).then_inc(q_taken, 1)
                if 2 <= piece < 6:
                    n = piece - 2
                    act.wait_ge(ranked, n + 1)
                    for h in range(2):
                        c = (2 * n + h) * TOPK
                        act.activation(gate_next[:, c:c + TOPK], best[:, h, :], ACT.Exp, bias=neg[:, h:h + 1],
                                       accum_out=total[:, h:h + 1]).then_inc(grown, 1)

            @staticmethod
            def vector(dve, v, piece):
                if piece in (0, 1):
                    dve.wait_ge(f_turned, piece + 1)
                    dve.tensor_copy(aT[:, 4:8, :].rearrange("p k q -> p (k q)"), pt[1][:]).then_inc(f_taken_v, 1)
                if piece == 0:
                    for n in range(2):
                        dve.wait_ge(projected, n + 1)
                        part = slice(n * 512, (n + 1) * 512)
                        dve.tensor_tensor(h1[:, part], h1[:, part], pt[n][:], ALU.add).then_inc(h1_ready, 1)
                    dve.wait_ge(rooted, 1)
                    v.step(dve.reciprocal(rs[:], rs[:]))
                    dve.scalar_tensor_tensor(out=m[:], in0=h1[:], scalar=rs[:], in1=g[:], op0=ALU.mult,
                                             op1=ALU.mult).then_inc(m_ready, 1)
                if 2 <= piece < 6:
                    n = piece - 2
                    dve.wait_ge(s_made, n + 1)
                    dve.tensor_copy(s[:], pk[n % 2][:]).then_inc(s_taken, 1)
                    dve.wait_ge(s_taken, n + 1)
                    for j in range(4):
                        v.did(dve.max(top[:, j, 0:8], s[:, j, :]))
                    v.settle()
                    for j in range(4):
                        v.did(dve.max_index(top_i[:, j, 0:8], top[:, j, 0:8], s[:, j, :]))
                        v.did(dve.match_replace(s_less[:, j, :], top[:, j, 0:8], s[:, j, :], NEG))
                    v.settle()
                    for j in range(4):
                        v.did(dve.max(top[:, j, 8:16], s_less[:, j, :]))
                    v.settle()
                    for j in range(4):
                        v.did(dve.max_index(top_i[:, j, 8:16], top[:, j, 8:16], s_less[:, j, :]))
                    for h in range(2):
                        v.did(dve.tensor_tensor(cand[:, h], wide(top[:, 2 * h, :], [P, TOPK, TOPK]),
                                                top[:, 2 * h + 1:2 * h + 2, :].to_broadcast([P, TOPK, TOPK]), ALU.add))
                    v.settle()
                    v.did(dve.tensor_copy(top_f[:], top_i[:]))
                    flat = [cand[:, h].rearrange("p a b -> p (a b)") for h in range(2)]
                    for h in range(2):
                        v.did(dve.max(best[:, h, 0:8], flat[h]))
                    v.settle()
                    for h in range(2):
                        v.did(dve.max_index(pos[:, h * TOPK:h * TOPK + 8], best[:, h, 0:8], flat[h]))
                        v.did(dve.match_replace(cand_less[:, h, :], best[:, h, 0:8], flat[h], NEG))
                    v.settle()
                    for h in range(2):
                        v.did(dve.max(best[:, h, 8:16], cand_less[:, h, :]))
                    v.did(dve.tensor_scalar(neg[:], best[:, :, 0], -1.0, None, ALU.mult))
                    v.settle()
                    for h in range(2):
                        last = dve.max_index(pos[:, h * TOPK + 8:(h + 1) * TOPK], best[:, h, 8:16], cand_less[:, h, :])
                        v.did(last)
                    v.settle()
                    dve.tensor_scalar(side_i[:, 0, :], pos[:], 4, None, ALU.logical_shift_right).then_inc(ranked, 1)
                    v.did(dve.tensor_scalar(side_i[:, 1, :], pos[:], TOPK - 1, None, ALU.bitwise_and))
                    dve.wait_ge(ranked, n + 1)
                    v.settle()
                    v.step(dve.tensor_copy(side[:], side_i[:]))
                    for c in range(2):
                        v.did(dve.tensor_tensor(hot[:, c], wide(side[:, c, :], [P, 2 * TOPK, TOPK]),
                                                iota[:].unsqueeze(1).to_broadcast([P, 2 * TOPK, TOPK]), ALU.is_equal))
                    v.settle()
                    for c in range(2):
                        for h in range(2):
                            part = hot[:, c, h * TOPK:(h + 1) * TOPK, :]
                            v.did(dve.tensor_tensor(part, part,
                                                    top_f[:, 2 * h + c:2 * h + c + 1, :].to_broadcast([P, TOPK, TOPK]),
                                                    ALU.mult))
                    v.settle()
                    v.step(dve.tensor_reduce(pick[:], hot[:], AX_X, ALU.add))
                    v.step(dve.scalar_tensor_tensor(out=idx_f[:], in0=pick[:, 0, :], scalar=float(KEYS), in1=pick[:, 1, :],
                                                    op0=ALU.mult, op1=ALU.add))
                    c0 = 2 * n * TOPK
                    v.did(dve.tensor_copy(idx_next[:, c0:c0 + 2 * TOPK], idx_f[:]))
                    dve.wait_ge(grown, 2 * n + 2)
                    v.step(dve.reciprocal(total[:], total[:]))
                    for h in range(2):
                        c = c0 + h * TOPK
                        v.did(dve.tensor_scalar(gate_next[:, c:c + TOPK], gate_next[:, c:c + TOPK], total[:, h:h + 1],
                                                None, ALU.mult))
                    v.settle()

        def items(n_grp):
            out = []
            for q in range(n_grp + 1):
                out += [("u", q * GRP + j) for j in range(GRP)] if q < n_grp else []
                out += [("v", (q - 1) * GRP + j) for j in range(GRP)] if q else []
            return out

        class Gather:
            def __init__(self, n_grp):
                self.n_grp, self.order = n_grp, items(n_grp)
                self.at = {it: n for n, it in enumerate(self.order)}

            def start(self, dve, v, sample):
                if sample:
                    for r in range(REP):
                        rows, cols = slice(r * DEC, (r + 1) * DEC), slice(2 * r * TOPK, 2 * (r + 1) * TOPK)
                        v.did(dve.tensor_copy(idx_cur[rows, 0:2 * TOPK], idx_next[rows, cols]))
                        v.did(dve.tensor_copy(gate_cur[rows, 0:2 * TOPK], gate_next[rows, cols]))
                else:
                    v.did(dve.tensor_copy(idx_cur[:], idx_next[:]))
                    v.did(dve.tensor_copy(gate_cur[:], gate_next[:]))
                v.settle()
                dve.tensor_copy(m_cur[:], m[:]).then_inc(copied, 1)

            def landed(self, eng, it):
                n = self.at[it]
                eng.wait_ge(came[n % RING], 16 * (n // RING + 1))

            def pool(self, pool):
                pool.wait_ge(copied, 1)
                for n, (kind, slot) in enumerate(self.order):
                    if n >= RING:
                        k0, s0 = self.order[n - RING]
                        pool.wait_ge(u_used if k0 == "u" else v_used, s0 + 1)
                    table = t["expert_u"] if kind == "u" else t["expert_v"]
                    pool.indirect_dma_start(ring[:, n % RING, :], None, table,
                                            bass.IndirectOffsetOnAxis(idx_cur[:, slot:slot + 1], 0)).then_inc(
                        came[n % RING], 16)

            def vector(self, dve, q):
                if q == 0:
                    dve.wait_ge(copied, 1)
                if q < self.n_grp:
                    for slot in range(q * GRP, (q + 1) * GRP):
                        self.landed(dve, ("u", slot))
                        u = ring[:, self.at[("u", slot)] % RING, :]
                        dve.tensor_tensor_reduce(out=u, in0=u, in1=m_cur[:], scale=1.0, scalar=0.0, op0=ALU.mult,
                                                 op1=ALU.add, accum_out=dots[:, slot:slot + 1]).then_inc(u_used, 1)
                if q:
                    cols = slice((q - 1) * GRP, q * GRP)
                    dve.wait_ge(gelu_done, q)
                    dve.tensor_tensor(coef[:, cols], act_out[:, cols], gate_cur[:, cols], ALU.mult).then_inc(coef_ready, 1)

            def scalar(self, act, q):
                if q < self.n_grp:
                    cols = slice(q * GRP, (q + 1) * GRP)
                    act.wait_ge(u_used, (q + 1) * GRP)
                    act.activation(act_out[:, cols], dots[:, cols], ACT.Gelu).then_inc(gelu_done, 1)
                if q:
                    act.wait_ge(coef_ready, q)
                    for slot in range((q - 1) * GRP, q * GRP):
                        if slot >= 4:
                            act.wait_ge(v_used, slot - 3)
                        act.activation(diag[:, slot % 4, :], ident[:], ACT.Copy,
                                       scale=coef[:, slot:slot + 1]).then_inc(diag_ready, 1)

            def tensor(self, pe, q):
                if q:
                    for slot in range((q - 1) * GRP, q * GRP):
                        pe.wait_ge(diag_ready, slot + 1)
                        self.landed(pe, ("v", slot))
                        row = self.at[("v", slot)] % RING
                        for n in range(2):
                            mm = pe.matmul(acc[n][:], diag[:, slot % 4, :], ring[:, row, n * 512:(n + 1) * 512],
                                           start=(slot == 0), stop=(slot == self.n_grp * GRP - 1))
                        mm.then_inc(v_used, 1)

        front = Front(slice(0, P))
        with nc.Block() as block:
            @block.sync
            def _(sp):
                front.sync(sp)
                sp.wait_ge(stored, 16)
                sp.wait_ge(consts, 16 * (5 + 2 * KT))

            @block.gpsimd
            def _(pool):
                pool.iota(iota_i[:], pattern=[[1, TOPK]], base=0, channel_multiplier=0).then_inc(copied, 1)

            @block.scalar
            def _(act):
                act.dma_start(ident[:], t["ident"]).then_inc(consts, 16)
                act.dma_start(g[:], spread(t["g_ffn"])).then_inc(consts, 16)
                act.dma_start(fold[:], t["fold"]).then_inc(consts, 16)
                act.dma_start(keysT[:, 0, :], t["keysT"][:, 0, :]).then_inc(consts, 16)
                act.dma_start(keysT[:, 1, :], t["keysT"][:, 1, :]).then_inc(consts, 16)
                for k in range(KT):
                    act.dma_start(wo[:, k, :], t["w_out"][k * P:(k + 1) * P, :]).then_inc(consts, 16)
                for k in range(KT):
                    act.dma_start(wq[:, k, :], t["w_query"][k * P:(k + 1) * P, :]).then_inc(consts, 16)
                for piece in range(6):
                    front.scalar(act, piece)

            @block.vector
            def _(dve):
                v = Tally(dve, v_done)
                v.did(dve.memset(eps[:], EPS))
                dve.wait_ge(copied, 1)
                v.step(dve.tensor_copy(iota[:], iota_i[:]))
                for piece in range(6):
                    front.vector(dve, v, piece)

            @block.tensor
            def _(pe):
                pe.wait_ge(consts, 16 * (5 + 2 * KT))
                for piece in range(5):
                    front.tensor(pe, piece)
        st.end_pass()

        gather = Gather(SLOTS // GRP)
        with nc.Fori(0, NT - 1) as k:
            front = Front(ds((k + 1) * P, P))
            with nc.Block() as block:
                @block.sync
                def _(sp):
                    sp.dma_start(h1_cur[:], t["h1"][ds(k * P, P), :]).then_inc(h1_in, 16)
                    sp.wait_ge(copied, 1)
                    front.sync(sp)
                    sp.wait_ge(h2_ready, 2)
                    sp.dma_start(t["h2"][ds(k * P, P), :], h1_cur[:]).then_inc(stored, 16)
                    sp.wait_ge(stored, 32)

                @block.gpsimd
                def _(pool):
                    gather.pool(pool)

                @block.scalar
                def _(act):
                    for q in range(gather.n_grp + 1):
                        gather.scalar(act, q)
                        if 1 <= q < 7:
                            front.scalar(act, q - 1)

                @block.vector
                def _(dve):
                    v = Tally(dve, v_done)
                    gather.start(dve, v, False)
                    for q in range(gather.n_grp + 1):
                        gather.vector(dve, q)
                        if 1 <= q < 7:
                            front.vector(dve, v, q - 1)
                    dve.wait_ge(h1_in, 16)
                    dve.wait_ge(v_used, SLOTS)
                    for n in range(2):
                        part = slice(n * 512, (n + 1) * 512)
                        dve.tensor_tensor(h1_cur[:, part], h1_cur[:, part], acc[n][:], ALU.add).then_inc(h2_ready, 1)

                @block.tensor
                def _(pe):
                    for q in range(gather.n_grp + 1):
                        gather.tensor(pe, q)
                        if 1 <= q < 6:
                            front.tensor(pe, q - 1)
            st.end_pass()

        last = Gather(2 * TOPK // GRP)
        with nc.Block() as block:
            @block.sync
            def _(sp):
                sp.dma_start(h1_cur[0:DEC, :], t["h1"][SEQ:SEQ + DEC, :]).then_inc(h1_in, 16)
                sp.wait_ge(h2_ready, 2)
                for r in range(2 * REP):
                    sp.dma_start(t["h2"][SEQ + r * DEC:SEQ + (r + 1) * DEC, :], h1_cur[0:DEC, :]).then_inc(stored, 16)
                sp.wait_ge(stored, 16 * 2 * REP)

            @block.gpsimd
            def _(pool):
                last.pool(pool)

            @block.scalar
            def _(act):
                for q in range(last.n_grp + 1):
                    last.scalar(act, q)

            @block.vector
            def _(dve):
                v = Tally(dve, v_done)
                last.start(dve, v, True)
                for q in range(last.n_grp + 1):
                    last.vector(dve, q)
                dve.wait_ge(v_used, 2 * TOPK)
                for n in range(2):
                    part = slice(n * 512, (n + 1) * 512)
                    dve.tensor_copy(h1[:, part], acc[n][:]).then_inc(h1_ready, 1)
                dve.wait_ge(h1_in, 16)
                for n in range(2):
                    part = slice(n * 512, (n + 1) * 512)
                    dve.wait_ge(folded, n + 1)
                    dve.tensor_tensor(h1_cur[0:DEC, part], h1_cur[0:DEC, part], pt[n][0:DEC, :], ALU.add).then_inc(
                        h2_ready, 1)

            @block.tensor
            def _(pe):
                for q in range(last.n_grp + 1):
                    last.tensor(pe, q)
                for n in range(2):
                    pe.wait_ge(h1_ready, n + 1)
                    pe.matmul(pt[n][0:DEC, :], fold[:], h1[:, n * 512:(n + 1) * 512], start=True, stop=True).then_inc(
                        folded, 1)
        st.end_pass()


def finish(nc, t):
    with ExitStack() as ctx:
        st = Stage(nc, ctx, "fi")
        wg = st.sb("wg", [P, KT, D])
        wp = st.sb("wp", [P, PLE // P, D])
        g1 = st.sb("g1", [P, D])
        g2 = st.sb("g2", [P, D])
        ident = st.sb("ident", [P, P])
        eps = st.sb("eps", [P, 1])
        x = st.sb("x", [P, D])
        h = st.sb("h", [P, D])
        a = st.sb("a", [P, D])
        aT = st.sb("aT", [P, KT, P])
        pT = st.sb("pT", [P, PLE // P, P])
        ssq, rs, ssq2, rs2 = (st.sb(n, [P, 1]) for n in ("ssq", "rs", "ssq2", "rs2"))
        sig = st.sb("sig", [P, D])
        sq = st.sb("sq", [P, D])
        y = st.sb("y", [P, D])
        pg = [st.ps(f"pg{k}", [P, 512]) for k in range(2)]
        pp = [st.ps(f"pp{k}", [P, 512]) for k in range(2)]
        tr = [st.ps(f"tr{k}", [P, 512]) for k in range(2)]
        (consts, x_in, p_in, squared, rooted, inverted, normed, turned, taken, h_taken, gated, added, sig_ready, e_ready,
         h3_ready, squared2, rooted2, y_ready, v_done, stored) = (
            st.sem(n) for n in (
                "consts", "x_in", "p_in", "squared", "rooted", "inverted", "normed", "turned", "taken", "h_taken", "gated",
                "added", "sig_ready", "e_ready", "h3_ready", "squared2", "rooted2", "y_ready", "v_done", "stored"))

        def norm_act(act):
            act.wait_ge(x_in, 16)
            act.activation(sq[:], x[:], ACT.Square, accum_out=ssq[:]).then_inc(squared, 1)
            act.wait_ge(squared, 1)
            root(act, rs[:], ssq[:], D, eps[:]).then_inc(rooted, 1)

        def norm_dve(dve):
            dve.wait_ge(rooted, 1)
            dve.reciprocal(rs[:], rs[:]).then_inc(inverted, 1)
            dve.wait_ge(inverted, 1)
            dve.scalar_tensor_tensor(out=a[:], in0=x[:], scalar=rs[:], in1=g1[:], op0=ALU.mult,
                                     op1=ALU.mult).then_inc(normed, 1)

        def turn(pe):
            pe.wait_ge(normed, 1)
            for k in range(KT):
                last = pe.transpose(tr[k // 4][:, (k % 4) * P:(k % 4 + 1) * P], a[:, k * P:(k + 1) * P], ident[:])
            last.then_inc(turned, 1)

        def take_act(act):
            act.wait_ge(turned, 1)
            act.activation(aT[:, 0:4, :].rearrange("p k q -> p (k q)"), tr[0][:], ACT.Copy).then_inc(taken, 1)

        def take_dve(dve):
            dve.wait_ge(turned, 1)
            dve.tensor_copy(aT[:, 4:8, :].rearrange("p k q -> p (k q)"), tr[1][:]).then_inc(taken, 1)
            dve.tensor_copy(h[:], x[:]).then_inc(h_taken, 1)

        with nc.Block() as block:
            @block.sync
            def _(sp):
                sp.dma_start(x[:], t["h2"][0:P, :]).then_inc(x_in, 16)
                sp.dma_start(g1[:], spread(t["g_ple"])).then_inc(consts, 16)
                sp.dma_start(g2[:], spread(t["g_final"])).then_inc(consts, 16)
                sp.dma_start(ident[:], t["ident"]).then_inc(consts, 16)
                for k in range(KT):
                    sp.dma_start(wg[:, k, :], t["w_ple_gate"][k * P:(k + 1) * P, :]).then_inc(stored, 16)
                for k in range(PLE // P):
                    sp.dma_start(wp[:, k, :], t["w_ple"][k * P:(k + 1) * P, :]).then_inc(stored, 16)
                sp.wait_ge(stored, 16 * (KT + PLE // P))

            @block.scalar
            def _(act):
                act.wait_ge(v_done, 1)
                norm_act(act)
                take_act(act)

            @block.vector
            def _(dve):
                dve.memset(eps[:], EPS).then_inc(v_done, 1)
                dve.wait_ge(consts, 48)
                norm_dve(dve)
                take_dve(dve)

            @block.tensor
            def _(pe):
                pe.wait_ge(consts, 48)
                turn(pe)
        st.end_pass()

        with nc.Fori(0, NT) as i:
            with nc.Block() as block:
                @block.sync
                def _(sp):
                    sp.dma_start(pT[:].rearrange("p k q -> p (k q)"), t["pT"][ds(i * P, P), :]).then_inc(p_in, 16)
                    sp.dma_start(x[:], t["h2"][ds((i + 1) * P, P), :]).then_inc(x_in, 16)
                    sp.wait_ge(y_ready, 1)
                    sp.dma_start(t["y"][ds(i * P, P), :], y[:]).then_inc(stored, 16)
                    sp.wait_ge(stored, 16)

                @block.tensor
                def _(pe):
                    for n in range(2):
                        for k in range(KT):
                            mm = pe.matmul(pg[n][:], aT[:, k, :], wg[:, k, n * 512:(n + 1) * 512],
                                           start=(k == 0), stop=(k == KT - 1))
                        mm.then_inc(gated, 1)
                    pe.wait_ge(p_in, 16)
                    for n in range(2):
                        for k in range(PLE // P):
                            mm = pe.matmul(pp[n][:], pT[:, k, :], wp[:, k, n * 512:(n + 1) * 512],
                                           start=(k == 0), stop=(k == PLE // P - 1))
                        mm.then_inc(added, 1)
                    turn(pe)

                @block.scalar
                def _(act):
                    norm_act(act)
                    for n in range(2):
                        act.wait_ge(gated, n + 1)
                        act.activation(sig[:, n * 512:(n + 1) * 512], pg[n][:], ACT.Sigmoid).then_inc(sig_ready, 1)
                    act.wait_ge(h3_ready, 2)
                    act.activation(sq[:], y[:], ACT.Square, accum_out=ssq2[:]).then_inc(squared2, 1)
                    act.wait_ge(squared2, 1)
                    root(act, rs2[:], ssq2[:], D, eps[:]).then_inc(rooted2, 1)
                    take_act(act)

                @block.vector
                def _(dve):
                    v = Tally(dve, v_done)
                    norm_dve(dve)
                    for n in range(2):
                        part = slice(n * 512, (n + 1) * 512)
                        dve.wait_ge(sig_ready, n + 1)
                        dve.wait_ge(added, n + 1)
                        v.step(dve.tensor_tensor(sig[:, part], sig[:, part], pp[n][:], ALU.mult))
                        dve.tensor_tensor(y[:, part], h[:, part], sig[:, part], ALU.add).then_inc(h3_ready, 1)
                    dve.wait_ge(rooted2, 1)
                    v.step(dve.reciprocal(rs2[:], rs2[:]))
                    dve.scalar_tensor_tensor(out=y[:], in0=y[:], scalar=rs2[:], in1=g2[:], op0=ALU.mult,
                                             op1=ALU.mult).then_inc(y_ready, 1)
                    take_dve(dve)
            st.end_pass()


_SCRATCH = {
    "line": (HD, LINE), "fan": (HD, P, FAN), "qT": (NT * P, DV), "kT": (NT * P, DV), "z": (NT * P, D_SSM),
    "xbc": (CONV_W - 1 + NT * P, CONV_DIM), "xbc_s": (DEC_B, CONV_W - 1 + DEC_S, CONV_DIM), "dt": (NT * P, HS),
    "mix": (NT * P, D), "h1": (NT * P, D), "h2": ((NT + 1) * P, D),
}
_OUTPUTS = {
    "y": (NT * P, D), "k_all": (NT * P, DV), "v_all": (NT * P, DV), "ssm_p": (NS, D_SSM),
    "ssm_s": (DEC_B, NS, D_SSM), "conv_p": (CONV_W - 1, CONV_DIM), "conv_s": (DEC_B, CONV_W - 1, CONV_DIM),
}


def program(nc, t):
    tables(nc, t)
    project(nc, t)
    split_conv(nc, t)
    ssd(nc, t, sample=False)
    ssd(nc, t, sample=True)
    attend_prompt(nc, t)
    attend_sample(nc, t)
    experts(nc, t)
    finish(nc, t)


def _constants(np):
    f = np.float32
    low = [b if b <= 16 else math.ceil(16 * 8 ** ((b - 16) / 16)) for b in range(32)]
    seq = np.kron(np.eye(DEC_B, dtype=f), np.ones((DEC_S, DEC_S), f))
    own = np.kron(np.eye(DEC_B, dtype=f), np.ones((DEC_S, 1), f))
    pair = np.eye(HD * DEC_S, dtype=f)
    return {
        "edges": np.array(list(zip(low, low[1:] + [10 ** 9])), f),
        "ident": np.eye(P, dtype=f),
        "cum_p": np.triu(np.ones((P, P), f)), "cum_s": np.triu(seq), "same_s": seq,
        "own_s": own, "own_cols": np.ascontiguousarray(own.T),
        "sel_w": np.concatenate([pair, pair]),
        "sign_w": np.repeat(np.array([[1, 0], [0, -1]], f), HD * DEC_S, axis=0),
        "fold": np.tile(np.eye(DEC, dtype=f), (REP, 1)),
    }


def _layout(np, i):
    def tiled(prompt, sample, width):
        s = sample.reshape(DEC, width)
        return np.concatenate([prompt.reshape(SEQ, width)] + [s] * REP)

    x = tiled(i["x_prompt"], i["x_sample"], D)
    p = tiled(i["p_prompt"], i["p_sample"], PLE)
    n_pool = i["cache_k"].shape[1]
    pages = i["page_table"]
    out = {
        "x_all": np.concatenate([x, x[SEQ:]]),
        "pT": p.reshape(NT, P, PLE // P, P).transpose(0, 3, 2, 1).reshape(NT * P, PLE),
        "cache_kT": i["cache_k"].reshape(n_pool, PAGE, HD, 2 * DH).transpose(0, 3, 2, 1).reshape(n_pool, P, HD * PAGE),
        "cache_v": i["cache_v"].reshape(n_pool, PAGE, DV),
        "ssm_in": i["state_ssm"].reshape(DEC_B, D_SSM, NS).transpose(0, 2, 1),
        "state_conv": i["state_conv"][0],
        "pages": np.concatenate([pages, pages[-1:]]).reshape(1, -1),
        "keysT": i["sub_keys"][0].transpose(2, 0, 1),
        "lam": np.stack([i[n][0] for n in ("lam_q1", "lam_k1", "lam_q2", "lam_k2")]),
        "rel_bias": i["rel_bias"], "g_final": i["g_final"],
    }
    for n in ("g_mix", "w_in", "conv_w", "conv_b", "dt_bias", "a_log", "d_skip", "g_ssm_norm", "g_diff_norm", "w_out",
              "g_ffn", "w_query", "expert_u", "expert_v", "w_ple", "w_ple_gate", "g_ple"):
        out[n] = i[n][0]
    return out


def kernel(**inputs):
    import numpy as np
    import concourse.bacc as bacc
    from concourse.bass_utils import run_bass_kernel_spmd

    nc = bacc.Bacc("TRN2", target_bir_lowering=False, num_devices=1)
    data = {**_layout(np, {k: np.asarray(v) for k, v in inputs.items()}), **_constants(np)}
    arrays, t = {}, {}
    for name, a in data.items():
        a = np.ascontiguousarray(a)
        arrays[f"in_{name}"] = a
        t[name] = nc.dram_tensor(f"in_{name}", a.shape, mybir.dt.from_np(a.dtype), kind="ExternalInput").ap()
    for name, shape in _SCRATCH.items():
        t[name] = nc.dram_tensor(f"mid_{name}", shape, F32, kind="Internal").ap()
    for name, shape in _OUTPUTS.items():
        t[name] = nc.dram_tensor(f"out_{name}", shape, F32, kind="ExternalOutput").ap()
    program(nc, t)
    r = run_bass_kernel_spmd(nc, [arrays], core_ids=[0]).results[0]
    y, k, v = r["out_y"], r["out_k_all"], r["out_v_all"]
    s = slice(SEQ, SEQ + DEC)
    ssm_p = r["out_ssm_p"].T.reshape(1, 1, HS, PS, NS)
    ssm_s = r["out_ssm_s"].transpose(0, 2, 1).reshape(1, DEC_B, HS, PS, NS)
    return (y[:SEQ].reshape(1, SEQ, D), y[s].reshape(DEC_B, DEC_S, D),
            k[:SEQ].reshape(1, 1, SEQ, HD, 2, DH), v[:SEQ].reshape(1, 1, SEQ, HD, 2 * DH),
            np.ascontiguousarray(ssm_p), r["out_conv_p"].reshape(1, 1, CONV_W - 1, CONV_DIM),
            k[s].reshape(1, DEC_B, DEC_S, HD, 2, DH), v[s].reshape(1, DEC_B, DEC_S, HD, 2 * DH),
            np.ascontiguousarray(ssm_s), r["out_conv_s"].reshape(1, DEC_B, CONV_W - 1, CONV_DIM))
```

```python
import math
from contextlib import ExitStack

import concourse.bass as bass
from concourse import mybir

F32 = mybir.dt.float32
I32 = mybir.dt.int32
U32 = mybir.dt.uint32
ALU = mybir.AluOpType
ACT = mybir.ActivationFunctionType
AX_X = mybir.AxisListType.X
ds = bass.ds

P = 128
D = 1024
KT = D // P
SEQ = 1024
PT = SEQ // P
NT = PT + 1
DEC_B, DEC_S = 8, 4
DEC = DEC_B * DEC_S
REP = P // DEC
D_SSM = 512
HS, PS, NS = 8, 64, 128
G = 2
CONV_W = 4
CONV_DIM = 1024
HD, DH = 4, 64
DV = 512
IN_COLS = 3080
C_Z, C_X, C_DT, C_Q, C_K, C_V = 0, 512, 1536, 1544, 2056, 2568
PAGES, PAGE = 16, 128
PAST = PAGES * PAGE
NEG = -1e30
EPS = 1e-6
LAM_INIT = 0.8 - 0.6 * math.exp(0.0)
X_OFF = PAST + DEC_S - 1
LINE = 3200
FAN = 2 * SEQ - 1
FAN_AT = X_OFF - (SEQ - 1)
KEYS = 128
PH, TOPK = 8, 16
SLOTS = PH * TOPK
PLE = 256


class Stage:

    def __init__(self, nc, ctx, tag):
        self.nc, self.ctx, self.tag, self.sems, self.pool_sems = nc, ctx, tag, {}, []

    def sb(self, name, shape, dt=F32):
        return self.ctx.enter_context(self.nc.sbuf_tensor(f"{self.tag}_{name}", shape, dt))

    def ps(self, name, shape, dt=F32):
        return self.ctx.enter_context(self.nc.psum_tensor(f"{self.tag}_{name}", shape, dt))

    def sem(self, name):
        s = self.ctx.enter_context(self.nc.semaphore(f"{self.tag}_{name}"))
        self.sems[name] = s
        return s

    def pool_sem(self, name):
        s = self.sem(name)
        self.pool_sems.append(s)
        return s

    def end_pass(self):
        nums = [s.num for s in self.sems.values()]
        if self.pool_sems:
            own = [s.num for s in self.pool_sems]
            self.nc.gpsimd.dma_reset(range(min(own), max(own) + 1))
        self.nc.multi_engine_barrier(list(self.nc.engines), sems_to_clear=range(min(nums), max(nums) + 1))


class Tally:

    def __init__(self, eng, sem):
        self.eng, self.sem, self.n = eng, sem, 0

    def did(self, ins):
        self.n += 1
        ins.then_inc(self.sem, 1)
        return self.n

    def settle(self):
        self.eng.wait_ge(self.sem, self.n)

    def step(self, ins):
        self.did(ins)
        self.settle()
        return self.n


def rows_of(vec, n=P):
    return vec.rearrange("(a n) -> a n", a=1).to_broadcast([n, vec.shape[0]])


def spread(vec, n=P):
    flat = vec.flatten()
    return bass.AP(flat.tensor, flat.offset, [[0, n], [1, flat.shape[-1]]])


def wide(ap, shape):
    return ap.unsqueeze(len(ap.shape)).to_broadcast(shape)


def tables(nc, t):
    with ExitStack() as ctx:
        st = Stage(nc, ctx, "tb")
        edges = st.sb("edges", [32, 2])
        rel = st.sb("rel", [32, HD])
        dist_i = st.sb("dist_i", [32, LINE], I32)
        dist = st.sb("dist", [32, LINE])
        hot = st.sb("hot", [32, LINE])
        below = st.sb("below", [HD, LINE])
        line = st.sb("line", [HD, LINE])
        ps = [st.ps(f"ps{k}", [HD, 512]) for k in range(2)]
        loaded, counted, v_done, line_mm, stored = (st.sem(n) for n in ("loaded", "counted", "v_done", "line_mm", "stored"))
        chunks = [(a, min(512, LINE - a)) for a in range(0, LINE, 512)]
        with nc.Block() as block:
            @block.sync
            def _(sp):
                sp.dma_start(edges[:], t["edges"]).then_inc(loaded, 16)
                sp.dma_start(rel[:], t["rel_bias"]).then_inc(loaded, 16)
                sp.wait_ge(v_done, 4 + len(chunks))
                sp.dma_start(t["line"], line[:]).then_inc(stored, 16)
                sp.wait_ge(stored, 16)
                for h in range(HD):
                    src = bass.AP(t["line"].tensor, h * LINE + FAN_AT, [[0, P], [1, FAN]])
                    sp.dma_start(t["fan"][h], src).then_inc(stored, 16)
                sp.wait_ge(stored, 16 * (1 + HD))

            @block.gpsimd
            def _(pool):
                pool.iota(dist_i[:], pattern=[[-1, LINE]], base=X_OFF, channel_multiplier=0).then_inc(counted, 1)

            @block.vector
            def _(dve):
                v = Tally(dve, v_done)
                dve.wait_ge(counted, 1)
                v.step(dve.tensor_copy(dist[:], dist_i[:]))
                dve.wait_ge(loaded, 32)
                v.did(dve.tensor_scalar(hot[:], dist[:], edges[:, 0:1], None, ALU.is_ge))
                v.step(dve.tensor_scalar(below[:], dist[0:HD, :], 0.0, NEG, ALU.is_lt, ALU.mult))
                v.step(dve.scalar_tensor_tensor(out=hot[:], in0=dist[:], scalar=edges[:, 1:2], in1=hot[:],
                                                op0=ALU.is_lt, op1=ALU.mult))
                for n, (a, w) in enumerate(chunks):
                    dve.wait_ge(line_mm, n + 1)
                    v.did(dve.tensor_tensor(line[:, a:a + w], ps[n % 2][:, 0:w], below[:, a:a + w], ALU.add))

            @block.tensor
            def _(pe):
                pe.wait_ge(v_done, 4)
                for n, (a, w) in enumerate(chunks):
                    if n >= 2:
                        pe.wait_ge(v_done, 4 + n - 1)
                    pe.matmul(ps[n % 2][:, 0:w], rel[:], hot[:, a:a + w], start=True, stop=True).then_inc(line_mm, 1)
        st.end_pass()


def root(act, out, ssq, n, eps):
    return act.activation(out, ssq, ACT.Sqrt, scale=1.0 / n, bias=eps)


def project(nc, t):
    with ExitStack() as ctx:
        st = Stage(nc, ctx, "pj")
        w = st.sb("w", [P, KT, IN_COLS])
        g = st.sb("g", [P, D])
        ident = st.sb("ident", [P, P])
        x = st.sb("x", [P, D])
        sq = st.sb("sq", [P, D])
        a = st.sb("a", [P, D])
        aT = st.sb("aT", [P, KT, P])
        ssq = st.sb("ssq", [P, 1])
        rs = st.sb("rs", [P, 1])
        eps = st.sb("eps", [P, 1])
        zero = st.sb("zero", [CONV_W - 1, CONV_DIM])
        zeroed = st.sem("zeroed")
        o_k, o_v, o_q, o_z = (st.sb(f"o_{n}", [P, 512]) for n in "kvqz")
        o_x = st.sb("o_x", [P, CONV_DIM])
        o_dt = st.sb("o_dt", [P, HS])
        o_kT = st.sb("o_kT", [P, 512])
        bank = [st.ps(f"bank{k}", [P, 512]) for k in range(4)]
        tr = [st.ps(f"tr{k}", [P, 4, P]) for k in range(2)]
        ktp = st.ps("ktp", [P, HD, P])
        loaded, x_in, squared, inverted, rooted, normed, turned, taken = (
            st.sem(n) for n in ("loaded", "x_in", "squared", "inverted", "rooted", "normed", "turned", "taken"))
        made, out_a, out_v, k_turned, k_taken, stored = (
            st.sem(n) for n in ("made", "out_a", "out_v", "k_turned", "k_taken", "stored"))
        w_in = t["w_in"].rearrange("(k p) n -> p k n", p=P)

        plan = [("k", C_K, 512, o_k[:]), ("v", C_V, 512, o_v[:]), ("q", C_Q, 512, o_q[:]),
                ("z", C_Z, 512, o_z[:]), ("x0", C_X, 512, o_x[:, 0:512]), ("x1", C_X + 512, 512, o_x[:, 512:]),
                ("dt", C_DT, HS, o_dt[:])]

        def norm_act(act):
            act.wait_ge(x_in, 16)
            act.activation(sq[:], x[:], ACT.Square, accum_out=ssq[:]).then_inc(squared, 1)
            act.wait_ge(squared, 1)
            root(act, rs[:], ssq[:], D, eps[:]).then_inc(rooted, 1)

        def norm_dve(dve):
            dve.wait_ge(rooted, 1)
            dve.reciprocal(rs[:], rs[:]).then_inc(inverted, 1)
            dve.wait_ge(inverted, 1)
            dve.scalar_tensor_tensor(out=a[:], in0=x[:], scalar=rs[:], in1=g[:], op0=ALU.mult,
                                     op1=ALU.mult).then_inc(normed, 1)

        def turn(pe):
            pe.wait_ge(normed, 1)
            for k in range(KT):
                last = pe.transpose(tr[k // 4][:, k % 4, :], a[:, k * P:(k + 1) * P], ident[:])
            last.then_inc(turned, 1)

        def take(act, dve=None):
            eng, half = (act, 0) if dve is None else (dve, 1)
            eng.wait_ge(turned, 1)
            if half:
                dve.tensor_copy(aT[:, 4:8, :], tr[1][:]).then_inc(taken, 1)
            else:
                act.activation(aT[:, 0:4, :], tr[0][:], ACT.Copy).then_inc(taken, 1)

        with nc.Block() as block:
            @block.sync
            def _(sp):
                sp.dma_start(x[:], t["x_all"][0:P, :]).then_inc(x_in, 16)
                sp.dma_start(ident[:], t["ident"]).then_inc(loaded, 16)
                sp.dma_start(g[:], spread(t["g_mix"])).then_inc(loaded, 16)
                for k in range(KT):
                    sp.dma_start(w[:, k, :], w_in[:, k, :]).then_inc(stored, 16)
                sp.wait_ge(zeroed, 1)
                sp.dma_start(t["xbc"][0:CONV_W - 1, :], zero[:]).then_inc(stored, 16)
                sp.wait_ge(stored, 16 * (KT + 1))

            @block.scalar
            def _(act):
                act.wait_ge(taken, 1)
                norm_act(act)
                take(act)

            @block.vector
            def _(dve):
                dve.memset(eps[:], EPS).then_inc(taken, 1)
                dve.memset(zero[:], 0.0).then_inc(zeroed, 1)
                dve.wait_ge(loaded, 32)
                norm_dve(dve)
                take(None, dve)

            @block.tensor
            def _(pe):
                pe.wait_ge(loaded, 32)
                turn(pe)
        st.end_pass()

        with nc.Fori(0, NT) as i:
            with nc.Block() as block:
                @block.sync
                def _(sp):
                    sp.dma_start(x[:], t["x_all"][ds((i + 1) * P, P), :]).then_inc(x_in, 16)
                    row = ds(i * P, P)
                    sp.wait_ge(out_a, 1)
                    sp.dma_start(t["k_all"][row, :], o_k[:]).then_inc(stored, 16)
                    sp.wait_ge(out_v, 1)
                    sp.dma_start(t["v_all"][row, :], o_v[:]).then_inc(stored, 16)
                    sp.wait_ge(out_a, 2)
                    sp.dma_start(t["qT"][row, :], o_q[:]).then_inc(stored, 16)
                    sp.wait_ge(k_taken, 1)
                    sp.dma_start(t["kT"][row, :], o_kT[:]).then_inc(stored, 16)
                    sp.wait_ge(out_v, 2)
                    sp.dma_start(t["z"][row, :], o_z[:]).then_inc(stored, 16)
                    sp.wait_ge(out_a, 3)
                    sp.wait_ge(out_v, 3)
                    sp.dma_start(t["xbc"][ds(i * P + CONV_W - 1, P), :], o_x[:]).then_inc(stored, 16)
                    sp.wait_ge(out_a, 4)
                    sp.dma_start(t["dt"][row, :], o_dt[:]).then_inc(stored, 16)
                    sp.wait_ge(stored, 16 * 7)

                @block.scalar
                def _(act):
                    norm_act(act)
                    for n in range(0, len(plan), 2):
                        act.wait_ge(made, n + 1)
                        name, _, cols, dest = plan[n]
                        act.activation(dest, bank[n % 4][:, 0:cols], ACT.Copy,
                                       scale=DH ** -0.5 if name == "q" else 1.0).then_inc(out_a, 1)
                    act.wait_ge(made, len(plan))
                    take(act)

                @block.vector
                def _(dve):
                    norm_dve(dve)
                    for n in range(1, len(plan), 2):
                        dve.wait_ge(made, n + 1)
                        _, _, cols, dest = plan[n]
                        dve.tensor_copy(dest, bank[n % 4][:, 0:cols]).then_inc(out_v, 1)
                        if n == 3:
                            dve.wait_ge(k_turned, 1)
                            dve.tensor_copy(o_kT[:], ktp[:].rearrange("p h q -> p (h q)")).then_inc(k_taken, 1)
                    dve.wait_ge(made, len(plan))
                    take(None, dve)

                @block.tensor
                def _(pe):
                    for n, (name, c0, cols, _) in enumerate(plan):
                        if n >= 4:
                            pe.wait_ge(out_a if n % 2 == 0 else out_v, (n - 4) // 2 + 1)
                        if name == "q":
                            for h in range(HD):
                                for k in range(KT):
                                    mm = pe.matmul(bank[n % 4][:, h * P:(h + 1) * P],
                                                   w[:, k, c0 + h * P:c0 + (h + 1) * P], aT[:, k, :],
                                                   start=(k == 0), stop=(k == KT - 1))
                        else:
                            for k in range(KT):
                                mm = pe.matmul(bank[n % 4][:, 0:cols], aT[:, k, :], w[:, k, c0:c0 + cols],
                                               start=(k == 0), stop=(k == KT - 1))
                        mm.then_inc(made, 1)
                        if n == 2:
                            pe.wait_ge(out_a, 1)
                            for h in range(HD):
                                mm = pe.transpose(ktp[:, h, :], o_k[:, h * P:(h + 1) * P], ident[:])
                            mm.then_inc(k_turned, 1)
                    turn(pe)
            st.end_pass()


def ssd(nc, t, sample):
    R, NB = (DEC, DEC_B) if sample else (P, 1)
    HALF = NS * 2
    with ExitStack() as ctx:
        st = Stage(nc, ctx, "ss" if sample else "sp")
        taps = st.sb("taps", [R, CONV_W, CONV_DIM])
        cbias = st.sb("cbias", [R, CONV_DIM])
        gn = st.sb("gn", [R, D_SSM])
        dskip = st.sb("dskip", [R, HS])
        dtb = st.sb("dtb", [R, HS])
        nega = st.sb("nega", [R, HS])
        cum = st.sb("cum", [R, R])
        same = st.sb("same", [R, R])
        own = st.sb("own", [R, NB])
        own_col = st.sb("own_col", [P, NB, R])
        ident = st.sb("ident", [P, P])
        ones = st.sb("ones", [R, P])
        eps = st.sb("eps", [P, 1])
        one = st.sb("one", [P, 1])
        xw = st.sb("xw", [R, CONV_W, CONV_DIM])
        xc = st.sb("xc", [R, CONV_DIM])
        z = st.sb("z", [R, D_SSM])
        dt = st.sb("dt", [R, HS])
        u, ea, ln, adt, acs, eac, dec = (st.sb(n, [R, HS]) for n in ("u", "ea", "ln", "adt", "acs", "eac", "dec"))
        adtm = st.sb("adtm", [R, NB, HS])
        adtr = st.sb("adtr", [R, HS, R])
        et = st.sb("et", [P, NB, HS])
        xdt = st.sb("xdt", [R, HS, PS])
        xdd = st.sb("xdd", [R, HS, PS])
        xdm = st.sb("xdm", [R, NB, D_SSM])
        bcT = st.sb("bcT", [P, 4, R])
        cTm = st.sb("cTm", [P, NB, G, R])
        gt = st.sb("gt", [R, G, R])
        el = st.sb("el", [R, HS, R])
        state = st.sb("state", [P, NB, D_SSM])
        y = st.sb("y", [R, D_SSM])
        skip = st.sb("skip", [R, D_SSM])
        ssq, rs = (st.sb(n, [R, G]) for n in ("ssq", "rs"))
        p_bc = st.ps("p_bc", [P, 4, P])
        p_sm = st.ps("p_sm", [P, 512])
        p_row = [st.ps(f"p_row{k}", [R, 4, P]) for k in range(2)]
        p_gt = st.ps("p_gt", [R, G, P])
        p_y = st.ps("p_y", [R, D_SSM])
        p_o = st.ps("p_o", [R, D_SSM])
        p_s = st.ps("p_s", [P, D_SSM])
        consts, loaded, z_in, v_done, a_done, stored = (
            st.sem(n) for n in ("consts", "loaded", "z_in", "v_done", "a_done", "stored"))
        (minus_abs, log_ready, adt_ready, summed, rows_up, convolved, acs_ready, less, decays, grown, activated,
         gate_ready, turned, bc_taken, scored, xdt_ready, own_ready, mixed, y_off, new_state, state_added, y_diag,
         y_ready, squared, rooted) = (
            st.sem(n) for n in (
                "minus_abs", "log_ready", "adt_ready", "summed", "rows_up", "convolved", "acs_ready", "less", "decays",
                "grown", "activated", "gate_ready", "turned", "bc_taken", "scored", "xdt_ready", "own_ready", "mixed",
                "y_off", "new_state", "state_added", "y_diag", "y_ready", "squared", "rooted"))
        n_const = 8

        with nc.Block() as block:
            @block.sync
            def _(sp):
                sp.dma_start(taps[:].rearrange("p w c -> p (w c)"), spread(t["conv_w"], R)).then_inc(consts, 16)
                sp.dma_start(cbias[:], spread(t["conv_b"], R)).then_inc(consts, 16)
                sp.dma_start(gn[:], spread(t["g_ssm_norm"], R)).then_inc(consts, 16)
                sp.dma_start(dskip[:], spread(t["d_skip"], R)).then_inc(consts, 16)
                sp.dma_start(dtb[:], spread(t["dt_bias"], R)).then_inc(consts, 16)
                sp.dma_start(nega[:], spread(t["a_log"], R)).then_inc(consts, 16)
                sp.dma_start(ident[:], t["ident"]).then_inc(consts, 16)
                sp.dma_start(cum[:], t["cum_s" if sample else "cum_p"]).then_inc(consts, 16)
                if sample:
                    sp.dma_start(same[:], t["same_s"]).then_inc(loaded, 16)
                    sp.dma_start(own[:], t["own_s"]).then_inc(loaded, 16)
                    sp.dma_start(own_col[:].rearrange("p b r -> p (b r)"), spread(t["own_cols"])).then_inc(loaded, 16)
                    sp.dma_start(state[:], t["ssm_in"].rearrange("b n c -> n b c")).then_inc(loaded, 16)
                    sp.wait_ge(loaded, 16 * 4)
                sp.wait_ge(consts, 16 * n_const)

            @block.scalar
            def _(act):
                act.wait_ge(consts, 16 * n_const)
                act.activation(nega[:], nega[:], ACT.Exp).then_inc(a_done, 1)

            @block.vector
            def _(dve):
                v = Tally(dve, v_done)
                v.did(dve.memset(eps[:], EPS))
                v.did(dve.memset(ones[:], 1.0))
                v.did(dve.memset(one[:], 1.0))
                if not sample:
                    v.did(dve.memset(same[:], 1.0))
                    v.did(dve.memset(own[:], 1.0))
                    v.did(dve.memset(state[:], 0.0))
                dve.wait_ge(a_done, 1)
                v.step(dve.tensor_scalar(nega[:], nega[:], -1.0, None, ALU.mult))
        st.end_pass()

        def one_pass(i):
            def heads(ap):
                return ap.rearrange("p (h c) -> p h c", h=HS)

            per_head = [R, HS, PS]
            row = ds(SEQ, R) if sample else ds(i * P, P)
            n_rows = CONV_W * (DEC_B if sample else 1)
            with nc.Block() as block:
                @block.sync
                def _(sp):
                    sp.dma_start(dt[:], t["dt"][row, :]).then_inc(z_in, 16)
                    sp.dma_start(z[:], t["z"][row, :]).then_inc(z_in, 16)
                    for k in range(CONV_W):
                        if sample:
                            for b in range(DEC_B):
                                sp.dma_start(xw[b * DEC_S:(b + 1) * DEC_S, k, :],
                                             t["xbc_s"][b, k:k + DEC_S, :]).then_inc(loaded, 16)
                        else:
                            sp.dma_start(xw[:, k, :], t["xbc"][ds(i * P + k, P), :]).then_inc(loaded, 16)
                    sp.wait_ge(y_ready, 3)
                    if sample:
                        for r in range(REP):
                            sp.dma_start(t["mix"][SEQ + r * R:SEQ + (r + 1) * R, 0:D_SSM], y[:]).then_inc(stored, 16)
                        sp.wait_ge(state_added, NB)
                        sp.dma_start(t["ssm_s"].rearrange("b n c -> n b c"), state[:]).then_inc(stored, 16)
                        sp.wait_ge(stored, 16 * (REP + 1))
                    else:
                        sp.dma_start(t["mix"][row, 0:D_SSM], y[:]).then_inc(stored, 16)
                        sp.wait_ge(stored, 16)

                @block.vector
                def _(dve):
                    v = Tally(dve, v_done)
                    dve.wait_ge(z_in, 32)
                    v.step(dve.tensor_tensor(u[:], dt[:], dtb[:], ALU.add))
                    dve.scalar_tensor_tensor(out=ea[:], in0=u[:], scalar=-1.0, in1=u[:], op0=ALU.mult,
                                             op1=ALU.min).then_inc(minus_abs, 1)
                    dve.wait_ge(log_ready, 2)
                    v.step(dve.scalar_tensor_tensor(out=dt[:], in0=u[:], scalar=0.0, in1=ln[:], op0=ALU.max, op1=ALU.add))
                    v.step(dve.tensor_tensor(adt[:], dt[:], nega[:], ALU.mult))
                    for b in range(NB):
                        v.did(dve.tensor_scalar(adtm[:, b, :], adt[:], own[:, b:b + 1], None, ALU.mult))
                    v.settle()
                    dve.tensor_copy(adtr[:], wide(adt[:], [R, HS, R])).then_inc(adt_ready, 1)
                    dve.wait_ge(loaded, 16 * n_rows)
                    for k in range(CONV_W):
                        v.did(dve.tensor_tensor(xw[:, k, :], xw[:, k, :], taps[:, k, :], ALU.mult))
                    v.settle()
                    v.did(dve.tensor_tensor(xw[:, 0, :], xw[:, 0, :], xw[:, 1, :], ALU.add))
                    v.step(dve.tensor_tensor(xw[:, 2, :], xw[:, 2, :], xw[:, 3, :], ALU.add))
                    v.step(dve.tensor_tensor(xw[:, 0, :], xw[:, 0, :], xw[:, 2, :], ALU.add))
                    dve.tensor_tensor(xw[:, 0, :], xw[:, 0, :], cbias[:], ALU.add).then_inc(convolved, 1)
                    dve.wait_ge(summed, 1)
                    v.step(dve.tensor_copy(acs[:], p_sm[:R, 0:HS]))
                    dve.tensor_tensor(dec[:], p_sm[:R, HS:2 * HS], acs[:], ALU.subtract).then_inc(acs_ready, 1)
                    dve.wait_ge(rows_up, 1)
                    for k in range(2):
                        v.did(dve.tensor_tensor(el[:, 4 * k:4 * k + 4, :], p_row[k][:, :, 0:R],
                                                wide(acs[:, 4 * k:4 * k + 4], [R, 4, R]), ALU.subtract))
                    v.settle()
                    dve.tensor_scalar(el[:], el[:], 0.0, None, ALU.min).then_inc(less, 1)
                    dve.wait_ge(activated, 1)
                    xs = heads(xc[:, 0:D_SSM])
                    dve.tensor_tensor(xdt[:], xs, wide(dt[:], per_head), ALU.mult).then_inc(xdt_ready, 1)
                    dve.wait_ge(xdt_ready, 1)
                    dve.wait_ge(decays, 3)
                    v.step(dve.tensor_tensor(xdd[:], xdt[:], wide(dec[:], per_head), ALU.mult))
                    dve.wait_ge(bc_taken, 1)
                    for b in range(NB):
                        v.did(dve.tensor_scalar(xdm[:, b, :], xdd[:].rearrange("p h c -> p (h c)"),
                                                own[:, b:b + 1], None, ALU.mult))
                        if sample:
                            v.did(dve.tensor_tensor(cTm[:, b], bcT[:, 2:4, :],
                                                    own_col[:, b:b + 1, :].to_broadcast([P, G, R]), ALU.mult))
                    v.settle()
                    dve.tensor_tensor(heads(skip[:]), xs, wide(dskip[:], per_head), ALU.mult).then_inc(own_ready, 1)
                    dve.wait_ge(scored, 1)
                    v.step(dve.tensor_tensor(gt[:], p_gt[:, :, 0:R],
                                             cum[:].unsqueeze(1).to_broadcast([R, G, R]), ALU.mult))
                    dve.wait_ge(grown, 1)
                    for g in range(G):
                        dve.tensor_tensor(el[:, 4 * g:4 * g + 4, :], el[:, 4 * g:4 * g + 4, :],
                                          gt[:, g:g + 1, :].to_broadcast([R, 4, R]), ALU.mult).then_inc(mixed, 1)
                    dve.wait_ge(y_off, 1)
                    v.step(dve.tensor_tensor(heads(y[:]), heads(p_o[:]), wide(eac[:], per_head), ALU.mult))
                    dve.wait_ge(y_diag, 1)
                    v.step(dve.tensor_tensor(y[:], y[:], p_y[:], ALU.add))
                    dve.wait_ge(own_ready, 1)
                    v.step(dve.tensor_tensor(y[:], y[:], skip[:], ALU.add))
                    dve.wait_ge(gate_ready, 1)
                    dve.tensor_tensor(y[:], y[:], z[:], ALU.mult).then_inc(y_ready, 1)
                    for b in range(NB):
                        sb = state[:, b, :]
                        v.step(dve.tensor_tensor(heads(sb), heads(sb), wide(et[:, b, :], [P, HS, PS]), ALU.mult))
                        dve.wait_ge(new_state, b + 1)
                        dve.tensor_tensor(sb, sb, p_s[:], ALU.add).then_inc(state_added, 1)
                    dve.wait_ge(rooted, 1)
                    v.step(dve.reciprocal(rs[:], rs[:]))
                    for g in range(G):
                        part = slice(g * HALF, (g + 1) * HALF)
                        dve.scalar_tensor_tensor(out=y[:, part], in0=y[:, part], scalar=rs[:, g:g + 1], in1=gn[:, part],
                                                 op0=ALU.mult, op1=ALU.mult).then_inc(y_ready, 1)

                @block.scalar
                def _(act):
                    act.wait_ge(minus_abs, 1)
                    act.activation(ea[:], ea[:], ACT.Exp).then_inc(log_ready, 1)
                    act.wait_ge(log_ready, 1)
                    act.activation(ln[:], ea[:], ACT.Ln, bias=one[:R]).then_inc(log_ready, 1)
                    act.wait_ge(acs_ready, 1)
                    act.activation(dec[:], dec[:], ACT.Exp).then_inc(decays, 1)
                    act.activation(eac[:], acs[:], ACT.Exp).then_inc(decays, 1)
                    act.activation(et[:].rearrange("p b h -> p (b h)"), p_sm[:, 2 * HS:2 * HS + NB * HS],
                                   ACT.Exp).then_inc(decays, 1)
                    act.wait_ge(less, 1)
                    act.activation(el[:], el[:], ACT.Exp).then_inc(grown, 1)
                    act.wait_ge(convolved, 1)
                    act.activation(xc[:], xw[:, 0, :], ACT.Silu).then_inc(activated, 1)
                    act.activation(z[:], z[:], ACT.Silu).then_inc(gate_ready, 1)
                    act.wait_ge(turned, 1)
                    act.activation(bcT[:], p_bc[:, :, 0:R], ACT.Copy).then_inc(bc_taken, 1)
                    act.wait_ge(y_ready, 1)
                    act.wait_ge(mixed, G)
                    for g in range(G):
                        part = slice(g * HALF, (g + 1) * HALF)
                        act.activation(skip[:, part], y[:, part], ACT.Square,
                                       accum_out=ssq[:, g:g + 1]).then_inc(squared, 1)
                    act.wait_ge(squared, G)
                    root(act, rs[:], ssq[:], HALF, eps[:R]).then_inc(rooted, 1)

                @block.tensor
                def _(pe):
                    pe.wait_ge(adt_ready, 1)
                    pe.matmul(p_sm[:R, 0:HS], cum[:], adt[:], start=True, stop=True)
                    pe.matmul(p_sm[:R, HS:2 * HS], same[:], adt[:], start=True, stop=True)
                    pe.matmul(p_sm[:, 2 * HS:2 * HS + NB * HS], ones[:], adtm[:].rearrange("p b h -> p (b h)"),
                              start=True, stop=True).then_inc(summed, 1)
                    for h in range(HS):
                        mm = pe.matmul(p_row[h // 4][:, h % 4, 0:R], adtr[:, h, :], cum[:], start=True, stop=True)
                    mm.then_inc(rows_up, 1)
                    pe.wait_ge(activated, 1)
                    for k in range(4):
                        mm = pe.transpose(p_bc[:, k, 0:R], xc[:, D_SSM + k * NS:D_SSM + (k + 1) * NS], ident[:R, :R])
                    mm.then_inc(turned, 1)
                    pe.wait_ge(bc_taken, 1)
                    for g in range(G):
                        mm = pe.matmul(p_gt[:, g, 0:R], bcT[:, g, :], bcT[:, 2 + g, :], start=True, stop=True)
                    mm.then_inc(scored, 1)
                    pe.wait_ge(own_ready, 1)
                    for g in range(G):
                        for b in range(NB):
                            c = cTm[:, b, g, :] if sample else bcT[:, 2 + g, :]
                            mm = pe.matmul(p_o[:, g * HALF:(g + 1) * HALF], c, state[:, b, g * HALF:(g + 1) * HALF],
                                           start=(b == 0), stop=(b == NB - 1))
                    mm.then_inc(y_off, 1)
                    for b in range(NB):
                        if b:
                            pe.wait_ge(state_added, b)
                        for g in range(G):
                            part = slice(g * HALF, (g + 1) * HALF)
                            mm = pe.matmul(p_s[:, part], xc[:, D_SSM + g * NS:D_SSM + (g + 1) * NS], xdm[:, b, part],
                                           start=True, stop=True)
                        mm.then_inc(new_state, 1)
                        if b == 0:
                            for h in range(HS):
                                pe.wait_ge(mixed, h // 4 + 1)
                                mm = pe.matmul(p_y[:, h * PS:(h + 1) * PS], el[:, h, :], xdt[:, h, :],
                                               start=True, stop=True)
                            mm.then_inc(y_diag, 1)
            st.end_pass()

        if sample:
            one_pass(None)
        else:
            with nc.Fori(0, PT) as i:
                one_pass(i)
            with nc.Block() as block:
                @block.sync
                def _(sp):
                    sp.dma_start(t["ssm_p"], state[:, 0, :]).then_inc(stored, 16)
                    sp.wait_ge(stored, 16)
            st.end_pass()


def between(nc, t, copies):
    with ExitStack() as ctx:
        st = Stage(nc, ctx, "cp")
        stored = st.sem("stored")
        with nc.Block() as block:
            @block.sync
            def _(sp):
                for dst, src in copies:
                    sp.dma_start(dst, src).then_inc(stored, 16)
                sp.wait_ge(stored, 16 * len(copies))
        st.end_pass()


def split_conv(nc, t):
    new = t["xbc"][CONV_W - 1 + SEQ:CONV_W - 1 + SEQ + DEC, :].rearrange("(b s) c -> b s c", s=DEC_S)
    between(nc, t, [(t["xbc_s"][:, 0:CONV_W - 1, :], t["state_conv"]), (t["xbc_s"][:, CONV_W - 1:, :], new),
                    (t["conv_p"], t["xbc"][SEQ:SEQ + CONV_W - 1, :]), (t["conv_s"], new[:, 1:, :])])


def lambdas(act, dve, v, lq, prod, sums, lam, ready, back):
    if dve is not None:
        for m in range(2):
            v.did(dve.tensor_tensor(prod[:, m, :], lq[:, 2 * m, :], lq[:, 2 * m + 1, :], ALU.mult))
        v.settle()
        dve.tensor_reduce(sums[:], prod[:], AX_X, ALU.add).then_inc(ready, 1)
        dve.wait_ge(back, 1)
        dve.scalar_tensor_tensor(out=lam[:], in0=sums[:, 0:1], scalar=LAM_INIT, in1=sums[:, 1:2], op0=ALU.add,
                                 op1=ALU.subtract).then_inc(ready, 1)
    else:
        act.wait_ge(ready, 1)
        act.activation(sums[:], sums[:], ACT.Exp).then_inc(back, 1)


def attend_prompt(nc, t):
    with ExitStack() as ctx:
        st = Stage(nc, ctx, "ap")
        kT = st.sb("kT", [P, HD, SEQ])
        qT = st.sb("qT", [P, HD, SEQ])
        val = st.sb("val", [P, PT, DV])
        bias = st.sb("bias", [P, HD, SEQ])
        k_cur, q_cur, b_cur = (st.sb(n, [P, SEQ]) for n in ("k_cur", "q_cur", "b_cur"))
        v_cur = st.sb("v_cur", [P, PT, P])
        ident = st.sb("ident", [P, P])
        gd = st.sb("gd", [P, 2 * DH])
        lq = st.sb("lq", [P, 4, DH])
        prod = st.sb("prod", [P, 2, DH])
        sums = st.sb("sums", [P, 2])
        lam = st.sb("lam", [P, 1])
        neg_lam = st.sb("neg_lam", [P, 1])
        eps = st.sb("eps", [P, 1])
        AHEAD = 3
        s = [[st.sb(f"s{k}{m}", [P, SEQ]) for m in range(2)] for k in range(AHEAD)]
        mx = st.sb("mx", [P, 2 * PT])
        total = st.sb("total", [P, 2 * PT])
        inv = st.sb("inv", [P, 2 * PT])
        ratio = st.sb("ratio", [P, PT])
        wT = [st.sb(f"wT{k}", [P, PT, P]) for k in range(2)]
        o = st.sb("o", [P, PT, HD, P])
        sq = st.sb("sq", [P, 2 * DH])
        ssq_cur = st.sb("ssq_cur", [P, PT])
        ssq, rs = (st.sb(n, [P, HD, PT]) for n in ("ssq", "rs"))
        p_s = [st.ps(f"p_s{k}", [P, SEQ]) for k in range(2)]
        p_t = [st.ps(f"p_t{k}", [P, 4, P]) for k in range(2)]
        p_o = [st.ps(f"p_o{k}", [P, P]) for k in range(2)]
        consts, k_in, q_in, val_in, b_in, v_done, stored = (
            st.sem(n) for n in ("consts", "k_in", "q_in", "val_in", "b_in", "v_done", "stored"))
        (lam_ready, lam_back, cur_v, cur_a, scored, maxed, neg_ready, grown, weighed, turned_a, turned_v, taken_a,
         taken_v, mixed, o_taken, squared, rooted, o_done) = (
            st.sem(n) for n in (
                "lam_ready", "lam_back", "cur_v", "cur_a", "scored", "maxed", "neg_ready", "grown", "weighed",
                "turned_a", "turned_v", "taken_a", "taken_v", "mixed", "o_taken", "squared", "rooted", "o_done"))

        with nc.Block() as block:
            @block.sync
            def _(sp):
                for j in range(PT):
                    cols = slice(j * P, (j + 1) * P)
                    sp.dma_start(kT[:, :, cols], t["kT"][cols, :].rearrange("p (h k) -> p h k", h=HD)).then_inc(k_in, 16)
                    sp.dma_start(qT[:, :, cols], t["qT"][cols, :].rearrange("p (h k) -> p h k", h=HD)).then_inc(q_in, 16)
                sp.wait_ge(k_in, 16 * PT)
                sp.wait_ge(q_in, 16 * PT)

            @block.scalar
            def _(act):
                for n in range(4):
                    act.dma_start(lq[:, n, :], spread(t["lam"][n])).then_inc(consts, 16)
                act.dma_start(ident[:], t["ident"]).then_inc(consts, 16)
                act.dma_start(gd[:], spread(t["g_diff_norm"])).then_inc(consts, 16)
                for h in range(HD):
                    act.dma_start(bias[:, h, :], bass.AP(t["fan"].tensor, h * P * FAN + SEQ - 1 - (PT - 1) * P,
                                                         [[FAN - 1, P], [1, SEQ]])).then_inc(b_in, 16)
                for j in range(PT):
                    act.dma_start(val[:, j, :], t["v_all"][j * P:(j + 1) * P, :]).then_inc(val_in, 16)
                lambdas(act, None, None, lq, prod, sums, lam, lam_ready, lam_back)
                act.wait_ge(b_in, 16 * HD)
                act.wait_ge(val_in, 16 * PT)

            @block.vector
            def _(dve):
                v = Tally(dve, v_done)
                v.did(dve.memset(eps[:], EPS))
                dve.wait_ge(consts, 16 * 6)
                v.did(dve.tensor_scalar(gd[:], gd[:], 1.0 - LAM_INIT, None, ALU.mult))
                lambdas(None, dve, v, lq, prod, sums, lam, lam_ready, lam_back)
                dve.wait_ge(lam_ready, 2)
                v.step(dve.tensor_scalar(neg_lam[:], lam[:], -1.0, None, ALU.mult))
        st.end_pass()

        with nc.Fori(0, HD) as h:
            with nc.Block() as block:
                @block.tensor
                def _(pe):
                    def scores(u):
                        i = PT - 1 - u
                        width = (i + 1) * P
                        for m in range(2):
                            n = 2 * u + m
                            if n >= 2:
                                pe.wait_ge(maxed, n - 1)
                            part = slice(m * DH, (m + 1) * DH)
                            for c in range(0, width, 512):
                                end = min(c + 512, width)
                                mm = pe.matmul(p_s[m][:, c:end], q_cur[part, i * P:(i + 1) * P], k_cur[part, c:end],
                                               start=True, stop=True)
                            mm.then_inc(scored, 1)

                    def turn(u):
                        i = PT - 1 - u
                        pe.wait_ge(weighed, u + 1)
                        if i >= 4:
                            if u:
                                pe.wait_ge(taken_v, u)
                            for j in range(4, i + 1):
                                mm = pe.transpose(p_t[1][:, j - 4, :], s[u % AHEAD][0][:, j * P:(j + 1) * P], ident[:])
                            mm.then_inc(turned_v, 1)
                        if u:
                            pe.wait_ge(taken_a, u)
                        for j in range(min(4, i + 1)):
                            mm = pe.transpose(p_t[0][:, j, :], s[u % AHEAD][0][:, j * P:(j + 1) * P], ident[:])
                        mm.then_inc(turned_a, 1)

                    def mix(u):
                        i = PT - 1 - u
                        if u >= 2:
                            pe.wait_ge(o_taken, u - 1)
                        pe.wait_ge(taken_a, u + 1)
                        for j in range(i + 1):
                            if j == 4:
                                pe.wait_ge(taken_v, u + 1)
                            mm = pe.matmul(p_o[u % 2][:], wT[u % 2][:, j, :], v_cur[:, j, :], start=(j == 0),
                                           stop=(j == i))
                        mm.then_inc(mixed, 1)

                    pe.wait_ge(cur_v, 1)
                    pe.wait_ge(cur_a, 1)
                    for u in range(AHEAD):
                        scores(u)
                    for u in range(PT):
                        turn(u)
                        if u + AHEAD < PT:
                            scores(u + AHEAD)
                        if u == 0:
                            pe.wait_ge(cur_a, 2)
                        mix(u)

                @block.vector
                def _(dve):
                    v = Tally(dve, v_done)

                    def soften(u):
                        i = PT - 1 - u
                        width = (i + 1) * P
                        if u >= AHEAD:
                            dve.wait_ge(turned_a, u - AHEAD + 1)
                        for m in range(2):
                            n = 2 * u + m
                            dve.wait_ge(scored, n + 1)
                            dve.tensor_tensor_reduce(out=s[u % AHEAD][m][:, 0:width], in0=p_s[m][:, 0:width],
                                                     in1=b_cur[:, SEQ - width:], scale=1.0, scalar=NEG, op0=ALU.add,
                                                     op1=ALU.max, accum_out=mx[:, n:n + 1]).then_inc(maxed, 1)
                            dve.wait_ge(maxed, n + 1)
                            dve.tensor_scalar(mx[:, n:n + 1], mx[:, n:n + 1], -1.0, None, ALU.mult).then_inc(neg_ready, 1)

                    def weigh(u):
                        width = (PT - u) * P
                        a, b = (s[u % AHEAD][m][:, 0:width] for m in range(2))
                        dve.wait_ge(grown, 2 * u + 2)
                        v.step(dve.reciprocal(inv[:, 2 * u:2 * u + 2], total[:, 2 * u:2 * u + 2]))
                        v.step(dve.scalar_tensor_tensor(out=ratio[:, u:u + 1], in0=total[:, 2 * u:2 * u + 1],
                                                        scalar=inv[:, 2 * u + 1:2 * u + 2], in1=neg_lam[:], op0=ALU.mult,
                                                        op1=ALU.mult))
                        dve.scalar_tensor_tensor(out=a, in0=b, scalar=ratio[:, u:u + 1], in1=a, op0=ALU.mult,
                                                 op1=ALU.add).then_inc(weighed, 1)

                    def take(u):
                        i = PT - 1 - u
                        if i >= 4:
                            dve.wait_ge(turned_v, u + 1)
                            if u >= 2:
                                dve.wait_ge(mixed, u - 1)
                            dve.tensor_copy(wT[u % 2][:, 4:i + 1, :], p_t[1][:, 0:i - 3, :]).then_inc(taken_v, 1)

                    def out(u):
                        dve.wait_ge(mixed, u + 1)
                        dve.tensor_scalar(o[:, PT - 1 - u, ds(h, 1), :].rearrange("p a e -> p (a e)"), p_o[u % 2][:],
                                          inv[:, 2 * u:2 * u + 1], None, ALU.mult).then_inc(o_taken, 1)

                    dve.tensor_copy(q_cur[:], qT[:, ds(h, 1), :].rearrange("p a k -> p (a k)")).then_inc(cur_v, 1)
                    v.did(dve.tensor_copy(b_cur[:], bias[:, ds(h, 1), :].rearrange("p a k -> p (a k)")))
                    v.settle()
                    soften(0)
                    soften(1)
                    for u in range(PT):
                        weigh(u)
                        if u + 2 < PT:
                            soften(u + 2)
                        take(u)
                        if u:
                            out(u - 1)
                    out(PT - 1)

                @block.scalar
                def _(act):
                    def grow(u):
                        width = (PT - u) * P
                        for m in range(2):
                            n = 2 * u + m
                            act.wait_ge(neg_ready, n + 1)
                            part = s[u % AHEAD][m][:, 0:width]
                            act.activation(part, part, ACT.Exp, bias=mx[:, n:n + 1],
                                           accum_out=total[:, n:n + 1]).then_inc(grown, 1)

                    def take(u):
                        n = min(4, PT - u)
                        act.wait_ge(turned_a, u + 1)
                        if u >= 2:
                            act.wait_ge(mixed, u - 1)
                        act.activation(wT[u % 2][:, 0:n, :], p_t[0][:, 0:n, :], ACT.Copy).then_inc(taken_a, 1)

                    def square(u):
                        act.wait_ge(o_taken, u + 1)
                        if u:
                            act.wait_ge(squared, u)
                        i = PT - 1 - u
                        act.activation(sq[:], o[:, i, ds(h, 1), :].rearrange("p a e -> p (a e)"), ACT.Square,
                                       accum_out=ssq_cur[:, i:i + 1]).then_inc(squared, 1)

                    act.activation(k_cur[:], kT[:, ds(h, 1), :].rearrange("p a k -> p (a k)"), ACT.Copy).then_inc(cur_a, 1)
                    act.activation(v_cur[:], val[:, :, ds(h * P, P)], ACT.Copy).then_inc(cur_a, 1)
                    grow(0)
                    grow(1)
                    for u in range(PT):
                        if u + 2 < PT:
                            grow(u + 2)
                        take(u)
                        if u:
                            square(u - 1)
                    square(PT - 1)
                    act.wait_ge(squared, PT)
                    act.activation(ssq[:, ds(h, 1), :].rearrange("p a i -> p (a i)"), ssq_cur[:], ACT.Copy)
            st.end_pass()

        with nc.Block() as block:
            @block.scalar
            def _(act):
                root(act, rs[:], ssq[:], 2 * DH, eps[:]).then_inc(rooted, 1)

            @block.vector
            def _(dve):
                v = Tally(dve, v_done)
                dve.wait_ge(rooted, 1)
                v.step(dve.reciprocal(rs[:], rs[:]))
                for i in range(PT):
                    v.step(dve.tensor_tensor(o[:, i], o[:, i], wide(rs[:, :, i], [P, HD, P]), ALU.mult))
                    dve.tensor_tensor(o[:, i], o[:, i], gd[:].unsqueeze(1).to_broadcast([P, HD, P]), ALU.mult).then_inc(
                        o_done, 1)

            @block.sync
            def _(sp):
                for i in range(PT):
                    sp.wait_ge(o_done, i + 1)
                    sp.dma_start(t["mix"][i * P:(i + 1) * P, D_SSM:], o[:, i].rearrange("p h e -> p (h e)")).then_inc(
                        stored, 16)
                sp.wait_ge(stored, 16 * PT)
        st.end_pass()


def attend_sample(nc, t):
    NR, NW = 2 * HD * DEC_S, HD * DEC_S
    NKEY = PAST + DEC_S
    with ExitStack() as ctx:
        st = Stage(nc, ctx, "as")
        kT = [st.sb(f"kT{k}", [P, PAGES, HD * PAGE]) for k in range(2)]
        val = [st.sb(f"val{k}", [P, PAGES, DV]) for k in range(2)]
        kN = [st.sb(f"kN{k}", [P, HD, DEC_S]) for k in range(2)]
        vN = [st.sb(f"vN{k}", [DEC_S, DV]) for k in range(2)]
        pages = st.sb("pages", [1, PAGES * DEC_B], I32)
        qT = st.sb("qT", [P, HD, DEC])
        qm = st.sb("qm", [P, HD, DEC_B, NR])
        bias = st.sb("bias", [NR, NKEY])
        sel = st.sb("sel", [NR, NW])
        lq = st.sb("lq", [P, 4, DH])
        prod = st.sb("prod", [P, 2, DH])
        sums = st.sb("sums", [P, 2])
        lam = st.sb("lam", [P, 1])
        sign = st.sb("sign", [NR, 2])
        coef = st.sb("coef", [NR, 1])
        eps = st.sb("eps", [P, 1])
        gd = st.sb("gd", [DEC, 2 * DH])
        s = [st.sb(f"s{k}", [NR, NKEY]) for k in range(2)]
        mx, top, total, inv = (st.sb(n, [NR, 1]) for n in ("mx", "top", "total", "inv"))
        mix = [st.sb(f"mix{k}", [NR, NW]) for k in range(2)]
        qc = [st.sb(f"qc{k}", [P, HD, NR]) for k in range(2)]
        wT = st.sb("wT", [P, PAGES + 1, NW])
        o_all = st.sb("o_all", [NW, DEC_B, DV])
        o = st.sb("o", [DEC, HD, 2 * DH])
        sq = st.sb("sq", [DEC, 2 * DH])
        ssq, rs = (st.sb(n, [DEC, HD]) for n in ("ssq", "rs"))
        p_s = st.ps("p_s", [NR, PAST])
        p_n = st.ps("p_n", [NR, DEC_S])
        p_w = st.ps("p_w", [P, PAGES + 1, NW])
        p_o = st.ps("p_o", [NW, DV])
        consts, v_done, stored, first = (st.sem(n) for n in ("consts", "v_done", "stored", "first"))
        k_in = [st.sem(f"k_in{k}") for k in range(2)]
        v_in = [st.pool_sem(f"v_in{k}") for k in range(2)]
        (lam_ready, lam_back, q_ready, scored, maxed, neg_ready, grown, mix_ready, weighed, w_taken, mixed, o_taken,
         squared, rooted, o_done) = (
            st.sem(n) for n in (
                "lam_ready", "lam_back", "q_ready", "scored", "maxed", "neg_ready", "grown", "mix_ready", "weighed",
                "w_taken", "mixed", "o_taken", "squared", "rooted", "o_done"))
        k_pool = t["cache_kT"]
        v_pool = t["cache_v"]
        N_POOL = k_pool.shape[0]
        FETCHED = 16 * (PAGES + 1)

        def fetch_keys(eng, b, slot):
            for p in range(PAGES):
                page = eng.value_load(pages[0:1, ds(b * PAGES + p, 1)], min_val=0, max_val=N_POOL - 1)
                eng.dma_start(kT[slot][:, p, :], k_pool[ds(page, 1), :, :].rearrange("a p n -> p (a n)")).then_inc(
                    k_in[slot], 16)
            kt = t["kT"][SEQ:SEQ + P, :].rearrange("p (h q) -> p h q", h=HD)
            eng.dma_start(kN[slot][:], kt[:, :, ds(b * DEC_S, DEC_S)]).then_inc(k_in[slot], 16)

        def fetch_values(eng, b, slot):
            for p in range(PAGES):
                page = eng.value_load(pages[0:1, ds(b * PAGES + p, 1)], min_val=0, max_val=N_POOL - 1)
                eng.dma_start(val[slot][:, p, :], v_pool[ds(page, 1), :, :].rearrange("a p n -> p (a n)")).then_inc(
                    v_in[slot], 16)
            eng.dma_start(vN[slot][:], t["v_all"][ds(SEQ + b * DEC_S, DEC_S), :]).then_inc(v_in[slot], 16)

        def make_scores(pe, k):
            for c in range(PAGES // 4):
                for h in range(HD):
                    pe.matmul(p_s[:, c * 512:(c + 1) * 512], qc[k][:, h, :],
                              kT[k][:, 4 * c:4 * c + 4, h * PAGE:(h + 1) * PAGE], start=(h == 0), stop=(h == HD - 1))
            for h in range(HD):
                mm = pe.matmul(p_n[:], qc[k][:, h, :], kN[k][:, h, :], start=(h == 0), stop=(h == HD - 1))
            mm.then_inc(scored, 1)

        def soften(dve, v, k, n):
            dve.wait_ge(scored, n + 1)
            dve.tensor_tensor_reduce(out=s[k][:, 0:PAST], in0=p_s[:], in1=bias[:, 0:PAST], scale=1.0, scalar=NEG,
                                     op0=ALU.add, op1=ALU.max, accum_out=mx[:]).then_inc(maxed, 1)
            dve.wait_ge(maxed, 2 * n + 1)
            dve.tensor_tensor_reduce(out=s[k][:, PAST:], in0=p_n[:], in1=bias[:, PAST:], scale=1.0, scalar=mx[:],
                                     op0=ALU.add, op1=ALU.max, accum_out=top[:]).then_inc(maxed, 1)
            dve.wait_ge(maxed, 2 * n + 2)
            dve.tensor_scalar(mx[:], top[:], -1.0, None, ALU.mult).then_inc(neg_ready, 1)
            dve.wait_ge(grown, n + 1)
            v.step(dve.reciprocal(inv[:], total[:]))
            v.step(dve.tensor_tensor(inv[:], inv[:], coef[:], ALU.mult))
            dve.tensor_scalar(mix[k][:], sel[:], inv[:], None, ALU.mult).then_inc(mix_ready, 1)

        def grow(act, k, n):
            act.wait_ge(neg_ready, n + 1)
            act.activation(s[k][:], s[k][:], ACT.Exp, bias=mx[:], accum_out=total[:]).then_inc(grown, 1)

        def queries(dve, b, k):
            dve.tensor_copy(qc[k][:], qm[:, :, ds(b, 1), :].rearrange("p h a r -> p h (a r)")).then_inc(q_ready, 1)

        with nc.Block() as block:
            @block.sync
            def _(sp):
                sp.dma_start(pages[:], t["pages"]).then_inc(first, 16)
                sp.wait_ge(first, 16)
                fetch_keys(sp, 0, 0)
                fetch_keys(sp, 1, 1)
                sp.wait_ge(k_in[1], FETCHED)

            @block.gpsimd
            def _(pool):
                pool.wait_ge(first, 16)
                fetch_values(pool, 0, 0)
                pool.wait_ge(v_in[0], FETCHED)

            @block.scalar
            def _(act):
                act.dma_start(qT[:], t["qT"][SEQ:SEQ + P, :].rearrange("p (h q) -> p h q", h=HD)[:, :, 0:DEC]).then_inc(
                    consts, 16)
                for n in range(4):
                    act.dma_start(lq[:, n, :], spread(t["lam"][n])).then_inc(consts, 16)
                act.dma_start(sel[:], t["sel_w"]).then_inc(consts, 16)
                act.dma_start(sign[:], t["sign_w"]).then_inc(consts, 16)
                for m in range(2):
                    for tok in range(DEC_S):
                        r = m * NW + tok
                        act.dma_start(bias[r:r + NW - DEC_S + 1:DEC_S, :],
                                      bass.AP(t["line"].tensor, X_OFF - PAST - tok, [[LINE, HD], [1, NKEY]])).then_inc(
                            consts, 16)
                act.dma_start(gd[:], spread(t["g_diff_norm"], DEC)).then_inc(consts, 16)
                act.wait_ge(consts, 16 * (8 + 2 * HD))
                lambdas(act, None, None, lq, prod, sums, lam, lam_ready, lam_back)
                grow(act, 0, 0)

            @block.vector
            def _(dve):
                v = Tally(dve, v_done)
                v.did(dve.memset(eps[:], EPS))
                v.did(dve.memset(qm[:], 0.0))
                dve.wait_ge(consts, 16 * (8 + 2 * HD))
                v.did(dve.tensor_scalar(gd[:], gd[:], 1.0 - LAM_INIT, None, ALU.mult))
                v.settle()
                for m in range(2):
                    for h in range(HD):
                        r = (m * HD + h) * DEC_S
                        part = slice(m * DH, (m + 1) * DH)
                        v.did(dve.tensor_copy(qm[part, h, :, r:r + DEC_S],
                                              qT[part, h, :].rearrange("p (b s) -> p b s", s=DEC_S)))
                v.settle()
                queries(dve, 0, 0)
                lambdas(None, dve, v, lq, prod, sums, lam, lam_ready, lam_back)
                dve.wait_ge(lam_ready, 2)
                v.step(dve.scalar_tensor_tensor(out=coef[:], in0=sign[:, 1:2], scalar=lam[0:NR, :], in1=sign[:, 0:1],
                                                op0=ALU.mult, op1=ALU.add))
                soften(dve, v, 0, 0)

            @block.tensor
            def _(pe):
                pe.wait_ge(q_ready, 1)
                pe.wait_ge(k_in[0], FETCHED)
                make_scores(pe, 0)
        st.end_pass()

        def two_sequences(i, last):
            ahead = 1 if last else 2
            with nc.Block() as block:
                @block.sync
                def _(sp):
                    if not last:
                        fetch_keys(sp, 2 * i + 2, 0)
                        sp.wait_ge(scored, 1)
                        fetch_keys(sp, 2 * i + 3, 1)
                        sp.wait_ge(k_in[1], FETCHED)

                @block.tensor
                def _(pe):
                    for j in range(2):
                        if j < ahead:
                            pe.wait_ge(q_ready, j + 1)
                            if j:
                                pe.wait_ge(k_in[0], FETCHED)
                                pe.wait_ge(maxed, 2)
                            make_scores(pe, 1 - j)
                        if j:
                            pe.wait_ge(mix_ready, 1)
                            pe.wait_ge(w_taken, 2)
                        for p in range(PAGES):
                            pe.matmul(p_w[:, p, :], s[j][:, p * PAGE:(p + 1) * PAGE], mix[j][:], start=True, stop=True)
                        pe.matmul(p_w[0:DEC_S, PAGES, :], s[j][:, PAST:], mix[j][:], start=True, stop=True).then_inc(
                            weighed, 1)
                        pe.wait_ge(w_taken, 2 * j + 2)
                        if j:
                            pe.wait_ge(v_in[1], FETCHED)
                            pe.wait_ge(o_taken, 1)
                        for p in range(PAGES):
                            pe.matmul(p_o[:], wT[:, p, :], val[j][:, p, :], start=(p == 0), stop=False)
                        pe.matmul(p_o[:], wT[0:DEC_S, PAGES, :], vN[j][:], start=False, stop=True).then_inc(mixed, 1)

                @block.vector
                def _(dve):
                    v = Tally(dve, v_done)
                    for j in range(ahead):
                        queries(dve, 2 * i + 1 + j, 1 - j)
                    for j in range(2):
                        if j < ahead:
                            if j:
                                dve.wait_ge(weighed, 1)
                            soften(dve, v, 1 - j, j)
                        dve.wait_ge(weighed, j + 1)
                        if j:
                            dve.wait_ge(mixed, 1)
                        dve.tensor_copy(wT[:, 0:PAGES, :], p_w[:, 0:PAGES, :]).then_inc(w_taken, 1)
                        dve.tensor_copy(wT[0:DEC_S, PAGES, :], p_w[0:DEC_S, PAGES, :]).then_inc(w_taken, 1)
                        dve.wait_ge(mixed, j + 1)
                        dve.tensor_copy(o_all[:, ds(2 * i + j, 1), :].rearrange("p a e -> p (a e)"), p_o[:]).then_inc(o_taken, 1)

                @block.scalar
                def _(act):
                    for j in range(ahead):
                        grow(act, 1 - j, j)

                @block.gpsimd
                def _(pool):
                    fetch_values(pool, 2 * i + 1, 1)
                    if not last:
                        pool.wait_ge(mixed, 1)
                        fetch_values(pool, 2 * i + 2, 0)
                        pool.wait_ge(v_in[0], FETCHED)
            st.end_pass()

        with nc.Fori(0, DEC_B // 2 - 1) as i:
            two_sequences(i, False)
        two_sequences(DEC_B // 2 - 1, True)

        with nc.Block() as block:
            @block.scalar
            def _(act):
                act.wait_ge(first, 16)
                for h in range(HD):
                    if h:
                        act.wait_ge(squared, h)
                    act.activation(sq[:], o[:, h, :], ACT.Square, accum_out=ssq[:, h:h + 1]).then_inc(squared, 1)
                act.wait_ge(squared, HD)
                root(act, rs[:], ssq[:], 2 * DH, eps[:DEC]).then_inc(rooted, 1)

            @block.vector
            def _(dve):
                v = Tally(dve, v_done)
                dve.wait_ge(first, 16)
                dve.wait_ge(rooted, 1)
                v.step(dve.reciprocal(rs[:], rs[:]))
                for h in range(HD):
                    dve.scalar_tensor_tensor(out=o[:, h, :], in0=o[:, h, :], scalar=rs[:, h:h + 1], in1=gd[:],
                                             op0=ALU.mult, op1=ALU.mult).then_inc(o_done, 1)

            @block.sync
            def _(sp):
                flat = o[:].rearrange("p h e -> p (h e)")
                for h in range(HD):
                    cols = slice(h * P, (h + 1) * P)
                    sp.dma_start(t["mix"][SEQ:SEQ + DEC, D_SSM + h * P:D_SSM + (h + 1) * P].rearrange(
                        "(b s) e -> s b e", s=DEC_S), o_all[h * DEC_S:(h + 1) * DEC_S, :, cols]).then_inc(consts, 16)
                sp.wait_ge(consts, 16 * HD)
                sp.dma_start(flat, t["mix"][SEQ:SEQ + DEC, D_SSM:]).then_inc(first, 16)
                sp.wait_ge(o_done, HD)
                for r in range(REP):
                    sp.dma_start(t["mix"][SEQ + r * DEC:SEQ + (r + 1) * DEC, D_SSM:], flat).then_inc(stored, 16)
                sp.wait_ge(stored, 16 * REP)
        st.end_pass()


def experts(nc, t):
    RING = 15
    DIAGS = 8
    GRP = 8
    COEF_LAG = GRP + 1
    LAG = GRP + 3
    with ExitStack() as ctx:
        st = Stage(nc, ctx, "ex")
        wo = st.sb("wo", [P, KT, D])
        wq = st.sb("wq", [P, KT, 2 * PH * KEYS])
        keysT = st.sb("keysT", [P, 2, KEYS])
        ident = st.sb("ident", [P, P])
        fold = st.sb("fold", [P, DEC])
        g = st.sb("g", [P, D])
        eps = st.sb("eps", [P, 1])
        iota_i = st.sb("iota_i", [P, TOPK], I32)
        iota = st.sb("iota", [P, TOPK])
        ring = st.sb("ring", [P, RING, D])
        m_cur = st.sb("m_cur", [P, D])
        idx_cur = st.sb("idx_cur", [P, SLOTS], I32)
        gate_cur = st.sb("gate_cur", [P, SLOTS])
        dots = st.sb("dots", [P, SLOTS])
        act_out = st.sb("act_out", [P, SLOTS])
        coef = st.sb("coef", [P, SLOTS])
        diag = st.sb("diag", [P, DIAGS, P])
        h1_cur = st.sb("h1_cur", [P, D])
        h1 = st.sb("h1", [P, D])
        m = st.sb("m", [P, D])
        aT = st.sb("aT", [P, KT, P])
        ssq, rs = (st.sb(n, [P, 1]) for n in ("ssq", "rs"))
        qT = [st.sb(f"qT{k}", [P, 4, P]) for k in range(2)]
        s = st.sb("s", [P, 4, KEYS])
        s_less = st.sb("s_less", [P, 4, KEYS])
        top = st.sb("top", [P, 4, TOPK])
        top_i = st.sb("top_i", [P, 4, TOPK], U32)
        top_f = st.sb("top_f", [P, 4, TOPK])
        cand = st.sb("cand", [P, 2, TOPK, TOPK])
        cand_less = st.sb("cand_less", [P, 2, TOPK * TOPK])
        best = st.sb("best", [P, 2, TOPK])
        pos = st.sb("pos", [P, 2 * TOPK], U32)
        side_i = st.sb("side_i", [P, 2, 2 * TOPK], U32)
        side = st.sb("side", [P, 2, 2 * TOPK])
        hot = st.sb("hot", [P, 2, 2 * TOPK, TOPK])
        pick = st.sb("pick", [P, 2, 2 * TOPK])
        idx_f = st.sb("idx_f", [P, 2 * TOPK])
        neg = st.sb("neg", [P, 2])
        total = st.sb("total", [P, 2])
        idx_next = st.sb("idx_next", [P, SLOTS], I32)
        gate_next = st.sb("gate_next", [P, SLOTS])
        acc = [st.ps(f"acc{k}", [P, 512]) for k in range(2)]
        pt = [st.ps(f"pt{k}", [P, 512]) for k in range(2)]
        pq = [st.ps(f"pq{k}", [P, 4, P]) for k in range(2)]
        pk = [st.ps(f"pk{k}", [P, 4, KEYS]) for k in range(2)]
        consts, v_done, h_done, copied, h1_in, stored = (
            st.sem(n) for n in ("consts", "v_done", "h_done", "copied", "h1_in", "stored"))
        u_used, v_used, gelu_done, coef_ready, diag_ready, folded, h2_ready = (
            st.sem(n) for n in ("u_used", "v_used", "gelu_done", "coef_ready", "diag_ready", "folded", "h2_ready"))
        (x_in, f_turned, f_taken_a, f_taken_v, projected, h1_ready, squared, rooted, m_ready, q_made, q_taken, s_made,
         s_taken, ranked, grown) = (
            st.sem(n) for n in (
                "x_in", "f_turned", "f_taken_a", "f_taken_v", "projected", "h1_ready", "squared", "rooted", "m_ready",
                "q_made", "q_taken", "s_made", "s_taken", "ranked", "grown"))
        came = [st.pool_sem(f"came{k}") for k in range(RING)]

        def pause(steps):
            return (None for _ in range(steps))

        class Front:

            def __init__(self, row):
                self.row = row

            def sync(self, sp):
                sp.dma_start(m[:], t["mix"][self.row, :]).then_inc(x_in, 16)
                sp.dma_start(h1[:], t["x_all"][self.row, :]).then_inc(x_in, 16)
                sp.wait_ge(h1_ready, 2)
                sp.dma_start(t["h1"][self.row, :], h1[:]).then_inc(stored, 16)

            @staticmethod
            def tensor(pe):
                def turn():
                    for k in range(KT):
                        mm = pe.transpose(pt[k // 4][:, (k % 4) * P:(k % 4 + 1) * P], m[:, k * P:(k + 1) * P], ident[:])
                    mm.then_inc(f_turned, 1)

                pe.wait_ge(x_in, 32)
                turn()
                yield from pause(4)
                pe.wait_ge(f_taken_a, 1)
                pe.wait_ge(f_taken_v, 1)
                for n in range(2):
                    for k in range(KT):
                        mm = pe.matmul(pt[n][:], aT[:, k, :], wo[:, k, n * 512:(n + 1) * 512],
                                       start=(k == 0), stop=(k == KT - 1))
                        if k % 2:
                            if k == KT - 1:
                                mm.then_inc(projected, 1)
                            yield
                yield from pause(7)
                pe.wait_ge(m_ready, 1)
                turn()
                yield from pause(4)
                pe.wait_ge(f_taken_a, 2)
                pe.wait_ge(f_taken_v, 2)
                for n in range(5):
                    if n < 4:
                        if n >= 2:
                            pe.wait_ge(q_taken, n - 1)
                        for j in range(4):
                            c = (4 * n + j) * KEYS
                            for k in range(KT):
                                mm = pe.matmul(pq[n % 2][:, j, :], wq[:, k, c:c + KEYS], aT[:, k, :],
                                               start=(k == 0), stop=(k == KT - 1))
                            if j == 3:
                                mm.then_inc(q_made, 1)
                            yield
                    if n:
                        pe.wait_ge(q_taken, n)
                        if n >= 3:
                            pe.wait_ge(s_taken, n - 2)
                        for j in range(4):
                            mm = pe.matmul(pk[(n - 1) % 2][:, j, :], qT[(n - 1) % 2][:, j, :], keysT[:, j % 2, :],
                                           start=True, stop=True)
                        mm.then_inc(s_made, 1)
                        yield from pause(11)

            @staticmethod
            def scalar(act):
                def take(n):
                    act.wait_ge(f_turned, n)
                    act.activation(aT[:, 0:4, :].rearrange("p k q -> p (k q)"), pt[0][:], ACT.Copy).then_inc(f_taken_a, 1)

                def take_queries(n):
                    act.wait_ge(q_made, n + 1)
                    if n >= 2:
                        act.wait_ge(s_made, n - 1)
                    act.activation(qT[n % 2][:], pq[n % 2][:], ACT.Copy).then_inc(q_taken, 1)

                yield from pause(2)
                take(1)
                yield from pause(13)
                act.wait_ge(h1_ready, 2)
                act.activation(m[:], h1[:], ACT.Square, accum_out=ssq[:]).then_inc(squared, 1)
                act.wait_ge(squared, 1)
                root(act, rs[:], ssq[:], D, eps[:]).then_inc(rooted, 1)
                yield from pause(6)
                take(2)
                yield from pause(7)
                for n in range(5):
                    if n < 4:
                        take_queries(n)
                    yield from pause(12 if n < 4 else 14)
                    if n:
                        act.wait_ge(ranked, n)
                        for h in range(2):
                            c = (2 * (n - 1) + h) * TOPK
                            act.activation(gate_next[:, c:c + TOPK], best[:, h, :], ACT.Exp, bias=neg[:, h:h + 1],
                                           accum_out=total[:, h:h + 1]).then_inc(grown, 1)

            @staticmethod
            def vector(dve, v):
                def take(n):
                    dve.wait_ge(f_turned, n)
                    dve.tensor_copy(aT[:, 4:8, :].rearrange("p k q -> p (k q)"), pt[1][:]).then_inc(f_taken_v, 1)

                def divide(n):
                    dve.wait_ge(grown, 2 * n + 2)
                    v.step(dve.reciprocal(total[:], total[:]))
                    for h in range(2):
                        c = (2 * n + h) * TOPK
                        v.did(dve.tensor_scalar(gate_next[:, c:c + TOPK], gate_next[:, c:c + TOPK], total[:, h:h + 1],
                                                None, ALU.mult))
                    v.settle()

                yield from pause(2)
                take(1)
                yield from pause(11)
                for n in range(2):
                    dve.wait_ge(projected, n + 1)
                    part = slice(n * 512, (n + 1) * 512)
                    dve.tensor_tensor(h1[:, part], h1[:, part], pt[n][:], ALU.add).then_inc(h1_ready, 1)
                yield from pause(4)
                dve.wait_ge(rooted, 1)
                v.step(dve.reciprocal(rs[:], rs[:]))
                dve.scalar_tensor_tensor(out=m[:], in0=h1[:], scalar=rs[:], in1=g[:], op0=ALU.mult,
                                         op1=ALU.mult).then_inc(m_ready, 1)
                yield from pause(4)
                take(2)
                yield from pause(12)
                for n in range(4):
                    dve.wait_ge(s_made, n + 1)
                    dve.tensor_copy(s[:], pk[n % 2][:]).then_inc(s_taken, 1)
                    dve.wait_ge(s_taken, n + 1)
                    for j in range(4):
                        v.did(dve.max(top[:, j, 0:8], s[:, j, :]))
                    yield
                    v.settle()
                    for j in range(4):
                        v.did(dve.match_replace(s_less[:, j, :], top[:, j, 0:8], s[:, j, :], NEG))
                    yield
                    v.settle()
                    for j in range(4):
                        v.did(dve.max(top[:, j, 8:16], s_less[:, j, :]))
                    yield
                    for j in range(4):
                        v.did(dve.max_index(top_i[:, j, 0:8], top[:, j, 0:8], s[:, j, :]))
                    yield
                    v.settle()
                    for j in range(4):
                        v.did(dve.max_index(top_i[:, j, 8:16], top[:, j, 8:16], s_less[:, j, :]))
                    yield
                    for h in range(2):
                        v.did(dve.tensor_tensor(cand[:, h], wide(top[:, 2 * h, :], [P, TOPK, TOPK]),
                                                top[:, 2 * h + 1:2 * h + 2, :].to_broadcast([P, TOPK, TOPK]), ALU.add))
                    yield
                    v.settle()
                    v.did(dve.tensor_copy(top_f[:], top_i[:]))
                    if n:
                        divide(n - 1)
                    flat = [cand[:, h].rearrange("p a b -> p (a b)") for h in range(2)]
                    for h in range(2):
                        v.did(dve.max(best[:, h, 0:8], flat[h]))
                    yield
                    v.settle()
                    for h in range(2):
                        v.did(dve.match_replace(cand_less[:, h, :], best[:, h, 0:8], flat[h], NEG))
                    v.did(dve.tensor_scalar(neg[:], best[:, :, 0], -1.0, None, ALU.mult))
                    yield
                    v.settle()
                    v.did(dve.max(best[:, 0, 8:16], cand_less[:, 0, :]))
                    dve.max(best[:, 1, 8:16], cand_less[:, 1, :]).then_inc(ranked, 1)
                    yield
                    v.settle()
                    dve.wait_ge(ranked, n + 1)
                    for h in range(2):
                        v.did(dve.max_index(pos[:, h * TOPK:h * TOPK + 8], best[:, h, 0:8], flat[h]))
                        v.did(dve.max_index(pos[:, h * TOPK + 8:(h + 1) * TOPK], best[:, h, 8:16], cand_less[:, h, :]))
                    yield
                    v.settle()
                    v.did(dve.tensor_scalar(side_i[:, 0, :], pos[:], 4, None, ALU.logical_shift_right))
                    v.did(dve.tensor_scalar(side_i[:, 1, :], pos[:], TOPK - 1, None, ALU.bitwise_and))
                    v.settle()
                    v.step(dve.tensor_copy(side[:], side_i[:]))
                    for c in range(2):
                        v.did(dve.tensor_tensor(hot[:, c], wide(side[:, c, :], [P, 2 * TOPK, TOPK]),
                                                iota[:].unsqueeze(1).to_broadcast([P, 2 * TOPK, TOPK]), ALU.is_equal))
                    yield
                    v.settle()
                    for c in range(2):
                        for h in range(2):
                            part = hot[:, c, h * TOPK:(h + 1) * TOPK, :]
                            v.did(dve.tensor_tensor(part, part,
                                                    top_f[:, 2 * h + c:2 * h + c + 1, :].to_broadcast([P, TOPK, TOPK]),
                                                    ALU.mult))
                    yield
                    v.settle()
                    v.step(dve.tensor_reduce(pick[:], hot[:], AX_X, ALU.add))
                    yield
                    v.step(dve.scalar_tensor_tensor(out=idx_f[:], in0=pick[:, 0, :], scalar=float(KEYS), in1=pick[:, 1, :],
                                                    op0=ALU.mult, op1=ALU.add))
                    c0 = 2 * n * TOPK
                    v.did(dve.tensor_copy(idx_next[:, c0:c0 + 2 * TOPK], idx_f[:]))
                    yield
                yield from pause(5)
                divide(3)

        class Gather:

            def __init__(self, slots):
                self.slots, self.steps = slots, range(slots + LAG)
                self.order = [it for i in self.steps
                              for it in [("u", i)] * (i < slots) + [("v", i - LAG)] * (i >= LAG)]
                self.at = {it: n for n, it in enumerate(self.order)}

            def start(self, dve, v, sample):
                if sample:
                    for r in range(REP):
                        rows, cols = slice(r * DEC, (r + 1) * DEC), slice(2 * r * TOPK, 2 * (r + 1) * TOPK)
                        v.did(dve.tensor_copy(idx_cur[rows, 0:2 * TOPK], idx_next[rows, cols]))
                        v.did(dve.tensor_copy(gate_cur[rows, 0:2 * TOPK], gate_next[rows, cols]))
                else:
                    v.did(dve.tensor_copy(idx_cur[:], idx_next[:]))
                    v.did(dve.tensor_copy(gate_cur[:], gate_next[:]))
                v.settle()
                dve.tensor_copy(m_cur[:], m[:]).then_inc(copied, 1)

            def landed(self, eng, it):
                n = self.at[it]
                eng.wait_ge(came[n % RING], 16 * (n // RING + 1))

            def pool(self, pool):
                pool.wait_ge(copied, 1)
                for n, (kind, slot) in enumerate(self.order):
                    if n >= RING:
                        k0, s0 = self.order[n - RING]
                        pool.wait_ge(u_used if k0 == "u" else v_used, s0 + 1)
                    table = t["expert_u"] if kind == "u" else t["expert_v"]
                    pool.indirect_dma_start(ring[:, n % RING, :], None, table,
                                            bass.IndirectOffsetOnAxis(idx_cur[:, slot:slot + 1], 0)).then_inc(
                        came[n % RING], 16)

            def vector(self, dve, front=iter(())):
                dve.wait_ge(copied, 1)
                for i in self.steps:
                    if i < self.slots:
                        self.landed(dve, ("u", i))
                        u = ring[:, self.at[("u", i)] % RING, :]
                        dve.tensor_tensor_reduce(out=u, in0=u, in1=m_cur[:], scale=1.0, scalar=0.0, op0=ALU.mult,
                                                 op1=ALU.add, accum_out=dots[:, i:i + 1]).then_inc(u_used, 1)
                    q = (i - COEF_LAG) // GRP
                    if (i - COEF_LAG) % GRP == 0 and 0 <= q < self.slots // GRP:
                        cols = slice(q * GRP, (q + 1) * GRP)
                        dve.wait_ge(gelu_done, q + 1)
                        dve.tensor_tensor(coef[:, cols], act_out[:, cols], gate_cur[:, cols], ALU.mult).then_inc(
                            coef_ready, 1)
                    if i >= LAG:
                        next(front, None)
                for _ in front:
                    pass

            def scalar(self, act, front=iter(())):
                for i in self.steps:
                    if i >= LAG:
                        slot = i - LAG
                        if slot % GRP == 0:
                            act.wait_ge(coef_ready, slot // GRP + 1)
                        if slot >= DIAGS:
                            act.wait_ge(v_used, slot - DIAGS + 1)
                        act.activation(diag[:, slot % DIAGS, :], ident[:], ACT.Copy,
                                       scale=coef[:, slot:slot + 1]).then_inc(diag_ready, 1)
                        next(front, None)
                    if i < self.slots and i % GRP == GRP - 1:
                        cols = slice(i + 1 - GRP, i + 1)
                        act.wait_ge(u_used, i + 1)
                        act.activation(act_out[:, cols], dots[:, cols], ACT.Gelu).then_inc(gelu_done, 1)
                for _ in front:
                    pass

            def tensor(self, pe, front=iter(())):
                for slot in range(self.slots):
                    pe.wait_ge(diag_ready, slot + 1)
                    self.landed(pe, ("v", slot))
                    row = self.at[("v", slot)] % RING
                    for n in range(2):
                        mm = pe.matmul(acc[n][:], diag[:, slot % DIAGS, :], ring[:, row, n * 512:(n + 1) * 512],
                                       start=(slot == 0), stop=(slot == self.slots - 1))
                    mm.then_inc(v_used, 1)
                    next(front, None)
                for _ in front:
                    pass

        front = Front(slice(0, P))
        with nc.Block() as block:
            @block.sync
            def _(sp):
                front.sync(sp)
                sp.wait_ge(stored, 16)
                sp.wait_ge(consts, 16 * (5 + 2 * KT))

            @block.gpsimd
            def _(pool):
                pool.iota(iota_i[:], pattern=[[1, TOPK]], base=0, channel_multiplier=0).then_inc(copied, 1)

            @block.scalar
            def _(act):
                act.dma_start(ident[:], t["ident"]).then_inc(consts, 16)
                act.dma_start(g[:], spread(t["g_ffn"])).then_inc(consts, 16)
                act.dma_start(fold[:], t["fold"]).then_inc(consts, 16)
                act.dma_start(keysT[:, 0, :], t["keysT"][:, 0, :]).then_inc(consts, 16)
                act.dma_start(keysT[:, 1, :], t["keysT"][:, 1, :]).then_inc(consts, 16)
                for k in range(KT):
                    act.dma_start(wo[:, k, :], t["w_out"][k * P:(k + 1) * P, :]).then_inc(consts, 16)
                for k in range(KT):
                    act.dma_start(wq[:, k, :], t["w_query"][k * P:(k + 1) * P, :]).then_inc(consts, 16)
                for _ in front.scalar(act):
                    pass

            @block.vector
            def _(dve):
                v = Tally(dve, v_done)
                v.did(dve.memset(eps[:], EPS))
                dve.wait_ge(copied, 1)
                v.step(dve.tensor_copy(iota[:], iota_i[:]))
                for _ in front.vector(dve, v):
                    pass

            @block.tensor
            def _(pe):
                pe.wait_ge(consts, 16 * (5 + 2 * KT))
                for _ in front.tensor(pe):
                    pass
        st.end_pass()

        gather = Gather(SLOTS)
        with nc.Fori(0, NT - 1) as k:
            front = Front(ds((k + 1) * P, P))
            with nc.Block() as block:
                @block.sync
                def _(sp):
                    sp.dma_start(h1_cur[:], t["h1"][ds(k * P, P), :]).then_inc(h1_in, 16)
                    sp.wait_ge(copied, 1)
                    front.sync(sp)
                    sp.wait_ge(h2_ready, 2)
                    sp.dma_start(t["h2"][ds(k * P, P), :], h1_cur[:]).then_inc(stored, 16)
                    sp.wait_ge(stored, 32)

                @block.gpsimd
                def _(pool):
                    gather.pool(pool)

                @block.scalar
                def _(act):
                    gather.scalar(act, front.scalar(act))

                @block.vector
                def _(dve):
                    v = Tally(dve, v_done)
                    gather.start(dve, v, False)
                    gather.vector(dve, front.vector(dve, v))
                    dve.wait_ge(h1_in, 16)
                    dve.wait_ge(v_used, SLOTS)
                    for n in range(2):
                        part = slice(n * 512, (n + 1) * 512)
                        dve.tensor_tensor(h1_cur[:, part], h1_cur[:, part], acc[n][:], ALU.add).then_inc(h2_ready, 1)

                @block.tensor
                def _(pe):
                    gather.tensor(pe, front.tensor(pe))
            st.end_pass()

        last = Gather(2 * TOPK)
        with nc.Block() as block:
            @block.sync
            def _(sp):
                sp.dma_start(h1_cur[0:DEC, :], t["h1"][SEQ:SEQ + DEC, :]).then_inc(h1_in, 16)
                sp.wait_ge(h2_ready, 2)
                for r in range(2 * REP):
                    sp.dma_start(t["h2"][SEQ + r * DEC:SEQ + (r + 1) * DEC, :], h1_cur[0:DEC, :]).then_inc(stored, 16)
                sp.wait_ge(stored, 16 * 2 * REP)

            @block.gpsimd
            def _(pool):
                last.pool(pool)

            @block.scalar
            def _(act):
                last.scalar(act)

            @block.vector
            def _(dve):
                v = Tally(dve, v_done)
                last.start(dve, v, True)
                last.vector(dve)
                dve.wait_ge(v_used, 2 * TOPK)
                for n in range(2):
                    part = slice(n * 512, (n + 1) * 512)
                    dve.tensor_copy(h1[:, part], acc[n][:]).then_inc(h1_ready, 1)
                dve.wait_ge(h1_in, 16)
                for n in range(2):
                    part = slice(n * 512, (n + 1) * 512)
                    dve.wait_ge(folded, n + 1)
                    dve.tensor_tensor(h1_cur[0:DEC, part], h1_cur[0:DEC, part], pt[n][0:DEC, :], ALU.add).then_inc(
                        h2_ready, 1)

            @block.tensor
            def _(pe):
                last.tensor(pe)
                for n in range(2):
                    pe.wait_ge(h1_ready, n + 1)
                    pe.matmul(pt[n][0:DEC, :], fold[:], h1[:, n * 512:(n + 1) * 512], start=True, stop=True).then_inc(
                        folded, 1)
        st.end_pass()


def finish(nc, t):
    with ExitStack() as ctx:
        st = Stage(nc, ctx, "fi")
        wg = st.sb("wg", [P, KT, D])
        wp = st.sb("wp", [P, PLE // P, D])
        g1 = st.sb("g1", [P, D])
        g2 = st.sb("g2", [P, D])
        ident = st.sb("ident", [P, P])
        eps = st.sb("eps", [P, 1])
        x = st.sb("x", [P, D])
        h = st.sb("h", [P, D])
        a = st.sb("a", [P, D])
        aT = st.sb("aT", [P, KT, P])
        pT = st.sb("pT", [P, PLE // P, P])
        ssq, rs, ssq2, rs2 = (st.sb(n, [P, 1]) for n in ("ssq", "rs", "ssq2", "rs2"))
        sig = st.sb("sig", [P, D])
        sq = st.sb("sq", [P, D])
        y = st.sb("y", [P, D])
        pg = [st.ps(f"pg{k}", [P, 512]) for k in range(2)]
        pp = [st.ps(f"pp{k}", [P, 512]) for k in range(2)]
        tr = [st.ps(f"tr{k}", [P, 512]) for k in range(2)]
        (consts, x_in, p_in, squared, rooted, inverted, normed, turned, taken, h_taken, gated, added, sig_ready, e_ready,
         h3_ready, squared2, rooted2, y_ready, v_done, stored) = (
            st.sem(n) for n in (
                "consts", "x_in", "p_in", "squared", "rooted", "inverted", "normed", "turned", "taken", "h_taken", "gated",
                "added", "sig_ready", "e_ready", "h3_ready", "squared2", "rooted2", "y_ready", "v_done", "stored"))

        def norm_act(act):
            act.wait_ge(x_in, 16)
            act.activation(sq[:], x[:], ACT.Square, accum_out=ssq[:]).then_inc(squared, 1)
            act.wait_ge(squared, 1)
            root(act, rs[:], ssq[:], D, eps[:]).then_inc(rooted, 1)

        def norm_dve(dve):
            dve.wait_ge(rooted, 1)
            dve.reciprocal(rs[:], rs[:]).then_inc(inverted, 1)
            dve.wait_ge(inverted, 1)
            dve.scalar_tensor_tensor(out=a[:], in0=x[:], scalar=rs[:], in1=g1[:], op0=ALU.mult,
                                     op1=ALU.mult).then_inc(normed, 1)

        def turn(pe):
            pe.wait_ge(normed, 1)
            for k in range(KT):
                last = pe.transpose(tr[k // 4][:, (k % 4) * P:(k % 4 + 1) * P], a[:, k * P:(k + 1) * P], ident[:])
            last.then_inc(turned, 1)

        def take_act(act):
            act.wait_ge(turned, 1)
            act.activation(aT[:, 0:4, :].rearrange("p k q -> p (k q)"), tr[0][:], ACT.Copy).then_inc(taken, 1)

        def take_dve(dve):
            dve.wait_ge(turned, 1)
            dve.tensor_copy(aT[:, 4:8, :].rearrange("p k q -> p (k q)"), tr[1][:]).then_inc(taken, 1)
            dve.tensor_copy(h[:], x[:]).then_inc(h_taken, 1)

        with nc.Block() as block:
            @block.sync
            def _(sp):
                sp.dma_start(x[:], t["h2"][0:P, :]).then_inc(x_in, 16)
                sp.dma_start(g1[:], spread(t["g_ple"])).then_inc(consts, 16)
                sp.dma_start(g2[:], spread(t["g_final"])).then_inc(consts, 16)
                sp.dma_start(ident[:], t["ident"]).then_inc(consts, 16)
                for k in range(KT):
                    sp.dma_start(wg[:, k, :], t["w_ple_gate"][k * P:(k + 1) * P, :]).then_inc(stored, 16)
                for k in range(PLE // P):
                    sp.dma_start(wp[:, k, :], t["w_ple"][k * P:(k + 1) * P, :]).then_inc(stored, 16)
                sp.wait_ge(stored, 16 * (KT + PLE // P))

            @block.scalar
            def _(act):
                act.wait_ge(v_done, 1)
                norm_act(act)
                take_act(act)

            @block.vector
            def _(dve):
                dve.memset(eps[:], EPS).then_inc(v_done, 1)
                dve.wait_ge(consts, 48)
                norm_dve(dve)
                take_dve(dve)

            @block.tensor
            def _(pe):
                pe.wait_ge(consts, 48)
                turn(pe)
        st.end_pass()

        with nc.Fori(0, NT) as i:
            with nc.Block() as block:
                @block.sync
                def _(sp):
                    sp.dma_start(pT[:].rearrange("p k q -> p (k q)"), t["pT"][ds(i * P, P), :]).then_inc(p_in, 16)
                    sp.dma_start(x[:], t["h2"][ds((i + 1) * P, P), :]).then_inc(x_in, 16)
                    sp.wait_ge(y_ready, 1)
                    sp.dma_start(t["y"][ds(i * P, P), :], y[:]).then_inc(stored, 16)
                    sp.wait_ge(stored, 16)

                @block.tensor
                def _(pe):
                    for n in range(2):
                        for k in range(KT):
                            mm = pe.matmul(pg[n][:], aT[:, k, :], wg[:, k, n * 512:(n + 1) * 512],
                                           start=(k == 0), stop=(k == KT - 1))
                        mm.then_inc(gated, 1)
                    pe.wait_ge(p_in, 16)
                    for n in range(2):
                        for k in range(PLE // P):
                            mm = pe.matmul(pp[n][:], pT[:, k, :], wp[:, k, n * 512:(n + 1) * 512],
                                           start=(k == 0), stop=(k == PLE // P - 1))
                        mm.then_inc(added, 1)
                    turn(pe)

                @block.scalar
                def _(act):
                    norm_act(act)
                    for n in range(2):
                        act.wait_ge(gated, n + 1)
                        act.activation(sig[:, n * 512:(n + 1) * 512], pg[n][:], ACT.Sigmoid).then_inc(sig_ready, 1)
                    act.wait_ge(h3_ready, 2)
                    act.activation(sq[:], y[:], ACT.Square, accum_out=ssq2[:]).then_inc(squared2, 1)
                    act.wait_ge(squared2, 1)
                    root(act, rs2[:], ssq2[:], D, eps[:]).then_inc(rooted2, 1)
                    take_act(act)

                @block.vector
                def _(dve):
                    v = Tally(dve, v_done)
                    norm_dve(dve)
                    for n in range(2):
                        part = slice(n * 512, (n + 1) * 512)
                        dve.wait_ge(sig_ready, n + 1)
                        dve.wait_ge(added, n + 1)
                        v.step(dve.tensor_tensor(sig[:, part], sig[:, part], pp[n][:], ALU.mult))
                        dve.tensor_tensor(y[:, part], h[:, part], sig[:, part], ALU.add).then_inc(h3_ready, 1)
                    dve.wait_ge(rooted2, 1)
                    v.step(dve.reciprocal(rs2[:], rs2[:]))
                    dve.scalar_tensor_tensor(out=y[:], in0=y[:], scalar=rs2[:], in1=g2[:], op0=ALU.mult,
                                             op1=ALU.mult).then_inc(y_ready, 1)
                    take_dve(dve)
            st.end_pass()


_SCRATCH = {
    "line": (HD, LINE), "fan": (HD, P, FAN), "qT": (NT * P, DV), "kT": (NT * P, DV), "z": (NT * P, D_SSM),
    "xbc": (CONV_W - 1 + NT * P, CONV_DIM), "xbc_s": (DEC_B, CONV_W - 1 + DEC_S, CONV_DIM), "dt": (NT * P, HS),
    "mix": (NT * P, D), "h1": (NT * P, D), "h2": ((NT + 1) * P, D),
}
_OUTPUTS = {
    "y": (NT * P, D), "k_all": (NT * P, DV), "v_all": (NT * P, DV), "ssm_p": (NS, D_SSM),
    "ssm_s": (DEC_B, NS, D_SSM), "conv_p": (CONV_W - 1, CONV_DIM), "conv_s": (DEC_B, CONV_W - 1, CONV_DIM),
}


def program(nc, t):
    tables(nc, t)
    project(nc, t)
    split_conv(nc, t)
    ssd(nc, t, sample=False)
    ssd(nc, t, sample=True)
    attend_prompt(nc, t)
    attend_sample(nc, t)
    experts(nc, t)
    finish(nc, t)


def _constants(np):
    f = np.float32
    low = [b if b <= 16 else math.ceil(16 * 8 ** ((b - 16) / 16)) for b in range(32)]
    seq = np.kron(np.eye(DEC_B, dtype=f), np.ones((DEC_S, DEC_S), f))
    own = np.kron(np.eye(DEC_B, dtype=f), np.ones((DEC_S, 1), f))
    pair = np.eye(HD * DEC_S, dtype=f)
    return {
        "edges": np.array(list(zip(low, low[1:] + [10 ** 9])), f),
        "ident": np.eye(P, dtype=f),
        "cum_p": np.triu(np.ones((P, P), f)), "cum_s": np.triu(seq), "same_s": seq,
        "own_s": own, "own_cols": np.ascontiguousarray(own.T),
        "sel_w": np.concatenate([pair, pair]),
        "sign_w": np.repeat(np.array([[1, 0], [0, -1]], f), HD * DEC_S, axis=0),
        "fold": np.tile(np.eye(DEC, dtype=f), (REP, 1)),
    }


def _layout(np, i):
    def tiled(prompt, sample, width):
        s = sample.reshape(DEC, width)
        return np.concatenate([prompt.reshape(SEQ, width)] + [s] * REP)

    x = tiled(i["x_prompt"], i["x_sample"], D)
    p = tiled(i["p_prompt"], i["p_sample"], PLE)
    n_pool = i["cache_k"].shape[1]
    pages = i["page_table"]
    out = {
        "x_all": np.concatenate([x, x[SEQ:]]),
        "pT": p.reshape(NT, P, PLE // P, P).transpose(0, 3, 2, 1).reshape(NT * P, PLE),
        "cache_kT": i["cache_k"].reshape(n_pool, PAGE, HD, 2 * DH).transpose(0, 3, 2, 1).reshape(n_pool, P, HD * PAGE),
        "cache_v": i["cache_v"].reshape(n_pool, PAGE, DV),
        "ssm_in": i["state_ssm"].reshape(DEC_B, D_SSM, NS).transpose(0, 2, 1),
        "state_conv": i["state_conv"][0],
        "pages": pages.reshape(1, -1),
        "keysT": i["sub_keys"][0].transpose(2, 0, 1),
        "lam": np.stack([i[n][0] for n in ("lam_q1", "lam_k1", "lam_q2", "lam_k2")]),
        "rel_bias": i["rel_bias"], "g_final": i["g_final"],
    }
    for n in ("g_mix", "w_in", "conv_w", "conv_b", "dt_bias", "a_log", "d_skip", "g_ssm_norm", "g_diff_norm", "w_out",
              "g_ffn", "w_query", "expert_u", "expert_v", "w_ple", "w_ple_gate", "g_ple"):
        out[n] = i[n][0]
    return out


def kernel(**inputs):
    import numpy as np
    import concourse.bacc as bacc
    from concourse.bass_utils import run_bass_kernel_spmd

    nc = bacc.Bacc("TRN2", target_bir_lowering=False, num_devices=1)
    data = {**_layout(np, {k: np.asarray(v) for k, v in inputs.items()}), **_constants(np)}
    arrays, t = {}, {}
    for name, a in data.items():
        a = np.ascontiguousarray(a)
        arrays[f"in_{name}"] = a
        t[name] = nc.dram_tensor(f"in_{name}", a.shape, mybir.dt.from_np(a.dtype), kind="ExternalInput").ap()
    for name, shape in _SCRATCH.items():
        t[name] = nc.dram_tensor(f"mid_{name}", shape, F32, kind="Internal").ap()
    for name, shape in _OUTPUTS.items():
        t[name] = nc.dram_tensor(f"out_{name}", shape, F32, kind="ExternalOutput").ap()
    program(nc, t)
    r = run_bass_kernel_spmd(nc, [arrays], core_ids=[0]).results[0]
    y, k, v = r["out_y"], r["out_k_all"], r["out_v_all"]
    s = slice(SEQ, SEQ + DEC)
    ssm_p = r["out_ssm_p"].T.reshape(1, 1, HS, PS, NS)
    ssm_s = r["out_ssm_s"].transpose(0, 2, 1).reshape(1, DEC_B, HS, PS, NS)
    return (y[:SEQ].reshape(1, SEQ, D), y[s].reshape(DEC_B, DEC_S, D),
            k[:SEQ].reshape(1, 1, SEQ, HD, 2, DH), v[:SEQ].reshape(1, 1, SEQ, HD, 2 * DH),
            np.ascontiguousarray(ssm_p), r["out_conv_p"].reshape(1, 1, CONV_W - 1, CONV_DIM),
            k[s].reshape(1, DEC_B, DEC_S, HD, 2, DH), v[s].reshape(1, DEC_B, DEC_S, HD, 2 * DH),
            np.ascontiguousarray(ssm_s), r["out_conv_s"].reshape(1, DEC_B, CONV_W - 1, CONV_DIM))
```

```python
import math
from contextlib import ExitStack

import concourse.bass as bass
from concourse import mybir

F32 = mybir.dt.float32
I32 = mybir.dt.int32
U32 = mybir.dt.uint32
ALU = mybir.AluOpType
ACT = mybir.ActivationFunctionType
AX_X = mybir.AxisListType.X
ds = bass.ds

P = 128
D = 1024
KT = D // P
SEQ = 1024
PT = SEQ // P
NT = PT + 1
DEC_B, DEC_S = 8, 4
DEC = DEC_B * DEC_S
REP = P // DEC
D_SSM = 512
HS, PS, NS = 8, 64, 128
G = 2
CONV_W = 4
CONV_DIM = 1024
HD, DH = 4, 64
DV = 512
IN_COLS = 3080
C_Z, C_X, C_DT, C_Q, C_K, C_V = 0, 512, 1536, 1544, 2056, 2568
PAGES, PAGE = 16, 128
PAST = PAGES * PAGE
NEG = -1e30
EPS = 1e-6
LAM_INIT = 0.8 - 0.6 * math.exp(0.0)
X_OFF = PAST + DEC_S - 1
LINE = 3200
FAN = 2 * SEQ - 1
FAN_AT = X_OFF - (SEQ - 1)
KEYS = 128
PH, TOPK = 8, 16
SLOTS = PH * TOPK
PLE = 256


class Stage:

    def __init__(self, nc, ctx, tag):
        self.nc, self.ctx, self.tag, self.sems, self.pool_sems = nc, ctx, tag, {}, []

    def sb(self, name, shape, dt=F32):
        return self.ctx.enter_context(self.nc.sbuf_tensor(f"{self.tag}_{name}", shape, dt))

    def ps(self, name, shape, dt=F32):
        return self.ctx.enter_context(self.nc.psum_tensor(f"{self.tag}_{name}", shape, dt))

    def sem(self, name):
        s = self.ctx.enter_context(self.nc.semaphore(f"{self.tag}_{name}"))
        self.sems[name] = s
        return s

    def pool_sem(self, name):
        s = self.sem(name)
        self.pool_sems.append(s)
        return s

    def end_pass(self):
        nums = [s.num for s in self.sems.values()]
        if self.pool_sems:
            own = [s.num for s in self.pool_sems]
            self.nc.gpsimd.dma_reset(range(min(own), max(own) + 1))
        self.nc.multi_engine_barrier(list(self.nc.engines), sems_to_clear=range(min(nums), max(nums) + 1))


class Tally:

    def __init__(self, eng, sem):
        self.eng, self.sem, self.n = eng, sem, 0

    def did(self, ins):
        self.n += 1
        ins.then_inc(self.sem, 1)
        return self.n

    def settle(self):
        self.eng.wait_ge(self.sem, self.n)

    def step(self, ins):
        self.did(ins)
        self.settle()
        return self.n


def spread(vec, n=P):
    flat = vec.flatten()
    return bass.AP(flat.tensor, flat.offset, [[0, n], [1, flat.shape[-1]]])


def wide(ap, shape):
    return ap.unsqueeze(len(ap.shape)).to_broadcast(shape)


class Tables:

    def __init__(self, nc, ctx, t, banks):
        self.t, self.ps = t, banks
        self.stage = st = Stage(nc, ctx, "tb")
        self.edges = st.sb("edges", [32, 2])
        self.rel = st.sb("rel", [32, HD])
        self.dist_i = st.sb("dist_i", [32, LINE], I32)
        self.dist = st.sb("dist", [32, LINE])
        self.hot = st.sb("hot", [32, LINE])
        self.below = st.sb("below", [HD, LINE])
        self.loaded, self.counted, self.v_done, self.line_mm = (
            st.sem(n) for n in ("loaded", "counted", "v_done", "line_mm"))
        self.chunks = [(a, min(512, LINE - a)) for a in range(0, LINE, 512)]

    def sync(self, sp, line_out):
        sp.dma_start(self.edges[:], self.t["edges"]).then_inc(self.loaded, 16)
        sp.dma_start(self.rel[:], self.t["rel_bias"]).then_inc(self.loaded, 16)
        sp.wait_ge(self.v_done, 4 + len(self.chunks))
        sp.dma_start(self.t["line"], self.below[:]).then_inc(line_out, 16)

    def gpsimd(self, pool):
        pool.iota(self.dist_i[:], pattern=[[-1, LINE]], base=X_OFF, channel_multiplier=0).then_inc(self.counted, 1)

    def vector(self, dve):
        v = Tally(dve, self.v_done)
        dve.wait_ge(self.counted, 1)
        v.step(dve.tensor_copy(self.dist[:], self.dist_i[:]))
        dve.wait_ge(self.loaded, 32)
        v.did(dve.tensor_scalar(self.hot[:], self.dist[:], self.edges[:, 0:1], None, ALU.is_ge))
        v.step(dve.tensor_scalar(self.below[:], self.dist[0:HD, :], 0.0, NEG, ALU.is_lt, ALU.mult))
        v.step(dve.scalar_tensor_tensor(out=self.hot[:], in0=self.dist[:], scalar=self.edges[:, 1:2], in1=self.hot[:],
                                        op0=ALU.is_lt, op1=ALU.mult))
        for n, (a, w) in enumerate(self.chunks):
            dve.wait_ge(self.line_mm, n + 1)
            v.did(dve.tensor_tensor(self.below[:, a:a + w], self.ps[n % 2][0:HD, 0:w], self.below[:, a:a + w], ALU.add))

    def tensor(self, pe):
        pe.wait_ge(self.v_done, 4)
        for n, (a, w) in enumerate(self.chunks):
            if n >= 2:
                pe.wait_ge(self.v_done, 4 + n - 1)
            pe.matmul(self.ps[n % 2][0:HD, 0:w], self.rel[:], self.hot[:, a:a + w], start=True, stop=True).then_inc(
                self.line_mm, 1)


def root(act, out, ssq, n, eps):
    return act.activation(out, ssq, ACT.Sqrt, scale=1.0 / n, bias=eps)


def project(nc, t, early):
    with ExitStack() as ctx:
        lasting = Stage(nc, ctx, "pjl")
        cols_in = [lasting.sem(f"cols_in{n}") for n in range(7)]
        line_out = lasting.sem("line_out")
        st = Stage(nc, ctx, "pj")
        w = st.sb("w", [P, KT, IN_COLS])
        g = st.sb("g", [P, D])
        ident = st.sb("ident", [P, P])
        x = st.sb("x", [P, D])
        sq = st.sb("sq", [P, D])
        a = st.sb("a", [P, D])
        aT = st.sb("aT", [P, KT, P])
        ssq = st.sb("ssq", [P, 1])
        rs = st.sb("rs", [P, 1])
        eps = st.sb("eps", [P, 1])
        zero = st.sb("zero", [CONV_W - 1, CONV_DIM])
        zeroed = st.sem("zeroed")
        o_k, o_v, o_q, o_z = (st.sb(f"o_{n}", [P, 512]) for n in "kvqz")
        o_x = st.sb("o_x", [P, CONV_DIM])
        o_dt = st.sb("o_dt", [P, HS])
        o_kT = st.sb("o_kT", [P, 512])
        bank = [st.ps(f"bank{k}", [P, 512]) for k in range(4)]
        tr = [st.ps(f"tr{k}", [P, 4, P]) for k in range(2)]
        ktp = st.ps("ktp", [P, HD, P])
        loaded, x_in, squared, inverted, rooted, normed, turned, taken = (
            st.sem(n) for n in ("loaded", "x_in", "squared", "inverted", "rooted", "normed", "turned", "taken"))
        made, out_a, out_v, k_turned, k_taken, stored = (
            st.sem(n) for n in ("made", "out_a", "out_v", "k_turned", "k_taken", "stored"))
        w_in = t["w_in"].rearrange("(k p) n -> p k n", p=P)

        plan = [("k", C_K, 512, o_k[:]), ("v", C_V, 512, o_v[:]), ("q", C_Q, 512, o_q[:]),
                ("z", C_Z, 512, o_z[:]), ("x0", C_X, 512, o_x[:, 0:512]), ("x1", C_X + 512, 512, o_x[:, 512:]),
                ("dt", C_DT, HS, o_dt[:])]

        def norm_act(act):
            act.wait_ge(x_in, 16)
            act.activation(sq[:], x[:], ACT.Square, accum_out=ssq[:]).then_inc(squared, 1)
            act.wait_ge(squared, 1)
            root(act, rs[:], ssq[:], D, eps[:]).then_inc(rooted, 1)

        def norm_dve(dve):
            dve.wait_ge(rooted, 1)
            dve.reciprocal(rs[:], rs[:]).then_inc(inverted, 1)
            dve.wait_ge(inverted, 1)
            dve.scalar_tensor_tensor(out=a[:], in0=x[:], scalar=rs[:], in1=g[:], op0=ALU.mult,
                                     op1=ALU.mult).then_inc(normed, 1)

        def turn(pe):
            pe.wait_ge(normed, 1)
            for k in range(KT):
                last = pe.transpose(tr[k // 4][:, k % 4, :], a[:, k * P:(k + 1) * P], ident[:])
            last.then_inc(turned, 1)

        def take(act, dve=None):
            eng, half = (act, 0) if dve is None else (dve, 1)
            eng.wait_ge(turned, 1)
            if half:
                dve.tensor_copy(aT[:, 4:8, :], tr[1][:]).then_inc(taken, 1)
            else:
                act.activation(aT[:, 0:4, :], tr[0][:], ACT.Copy).then_inc(taken, 1)

        with ExitStack() as brief:
            tables = Tables(nc, brief, t, bank[0:2])
            with nc.Block() as block:
                @block.sync
                def _(sp):
                    tables.sync(sp, line_out)

                @block.gpsimd
                def _(pool):
                    tables.gpsimd(pool)

                @block.scalar
                def _(act):
                    act.dma_start(x[:], t["x_all"][0:P, :]).then_inc(x_in, 16)
                    act.dma_start(ident[:], t["ident"]).then_inc(loaded, 16)
                    act.dma_start(g[:], spread(t["g_mix"])).then_inc(loaded, 16)
                    for n, (_, c0, cols, _) in enumerate(plan):
                        act.dma_start(w[:, :, c0:c0 + cols], w_in[:, :, c0:c0 + cols]).then_inc(cols_in[n], 16)
                    act.wait_ge(taken, 1)
                    norm_act(act)
                    take(act)
                    act.wait_ge(zeroed, 1)
                    act.dma_start(t["xbc"][0:CONV_W - 1, :], zero[:]).then_inc(stored, 16)
                    act.wait_ge(stored, 16)

                @block.vector
                def _(dve):
                    dve.memset(eps[:], EPS).then_inc(taken, 1)
                    dve.memset(zero[:], 0.0).then_inc(zeroed, 1)
                    dve.wait_ge(loaded, 32)
                    norm_dve(dve)
                    take(None, dve)
                    tables.vector(dve)

                @block.tensor
                def _(pe):
                    pe.wait_ge(loaded, 32)
                    turn(pe)
                    tables.tensor(pe)
            tables.stage.end_pass()
            st.end_pass()

        with nc.Fori(0, NT) as i:
            with nc.Block() as block:
                @block.sync
                def _(sp):
                    sp.dma_start(x[:], t["x_all"][ds((i + 1) * P, P), :]).then_inc(x_in, 16)
                    row = ds(i * P, P)
                    sp.wait_ge(out_a, 1)
                    sp.dma_start(t["k_all"][row, :], o_k[:]).then_inc(stored, 16)
                    sp.wait_ge(out_v, 1)
                    sp.dma_start(t["v_all"][row, :], o_v[:]).then_inc(stored, 16)
                    sp.wait_ge(out_a, 2)
                    sp.dma_start(t["qT"][row, :], o_q[:]).then_inc(stored, 16)
                    sp.wait_ge(k_taken, 1)
                    sp.dma_start(t["kT"][row, :], o_kT[:]).then_inc(stored, 16)
                    sp.wait_ge(out_v, 2)
                    sp.dma_start(t["z"][row, :], o_z[:]).then_inc(stored, 16)
                    sp.wait_ge(out_a, 3)
                    sp.wait_ge(out_v, 3)
                    sp.dma_start(t["xbc"][ds(i * P + CONV_W - 1, P), :], o_x[:]).then_inc(stored, 16)
                    sp.wait_ge(out_a, 4)
                    sp.dma_start(t["dt"][row, :], o_dt[:]).then_inc(stored, 16)
                    sp.wait_ge(stored, 16 * 7)

                @block.scalar
                def _(act):
                    norm_act(act)
                    for n in range(0, len(plan), 2):
                        act.wait_ge(made, n + 1)
                        name, _, cols, dest = plan[n]
                        act.activation(dest, bank[n % 4][:, 0:cols], ACT.Copy,
                                       scale=DH ** -0.5 if name == "q" else 1.0).then_inc(out_a, 1)
                    act.wait_ge(made, len(plan))
                    take(act)

                @block.vector
                def _(dve):
                    norm_dve(dve)
                    for n in range(1, len(plan), 2):
                        dve.wait_ge(made, n + 1)
                        _, _, cols, dest = plan[n]
                        dve.tensor_copy(dest, bank[n % 4][:, 0:cols]).then_inc(out_v, 1)
                        if n == 3:
                            dve.wait_ge(k_turned, 1)
                            dve.tensor_copy(o_kT[:], ktp[:].rearrange("p h q -> p (h q)")).then_inc(k_taken, 1)
                    dve.wait_ge(made, len(plan))
                    take(None, dve)

                @block.tensor
                def _(pe):
                    for n, (name, c0, cols, _) in enumerate(plan):
                        pe.wait_ge(cols_in[n], 16)
                        if n >= 4:
                            pe.wait_ge(out_a if n % 2 == 0 else out_v, (n - 4) // 2 + 1)
                        if name == "q":
                            for h in range(HD):
                                for k in range(KT):
                                    mm = pe.matmul(bank[n % 4][:, h * P:(h + 1) * P],
                                                   w[:, k, c0 + h * P:c0 + (h + 1) * P], aT[:, k, :],
                                                   start=(k == 0), stop=(k == KT - 1))
                        else:
                            for k in range(KT):
                                mm = pe.matmul(bank[n % 4][:, 0:cols], aT[:, k, :], w[:, k, c0:c0 + cols],
                                               start=(k == 0), stop=(k == KT - 1))
                        mm.then_inc(made, 1)
                        if n == 2:
                            pe.wait_ge(out_a, 1)
                            for h in range(HD):
                                mm = pe.transpose(ktp[:, h, :], o_k[:, h * P:(h + 1) * P], ident[:])
                            mm.then_inc(k_turned, 1)
                    turn(pe)
            st.end_pass()
        with nc.Block() as block:
            @block.sync
            def _(sp):
                sp.wait_ge(line_out, 16)
                for h in range(HD):
                    src = bass.AP(t["line"].tensor, h * LINE + FAN_AT, [[0, P], [1, FAN]])
                    sp.dma_start(t["fan"][h], src).then_inc(early.fan_out, 16)
        lasting.end_pass()


def ssd(nc, t, sample):
    R, NB = (DEC, DEC_B) if sample else (P, 1)
    HALF = NS * 2
    with ExitStack() as ctx:
        st = Stage(nc, ctx, "ss" if sample else "sp")
        taps = st.sb("taps", [R, CONV_W, CONV_DIM])
        cbias = st.sb("cbias", [R, CONV_DIM])
        gn = st.sb("gn", [R, D_SSM])
        dskip = st.sb("dskip", [R, HS])
        dtb = st.sb("dtb", [R, HS])
        nega = st.sb("nega", [R, HS])
        cum = st.sb("cum", [R, R])
        same = st.sb("same", [R, R])
        if sample:
            own = st.sb("own", [R, NB])
            own_col = st.sb("own_col", [P, NB, R])
        ident = st.sb("ident", [P, P])
        ones = st.sb("ones", [R, P])
        eps = st.sb("eps", [P, 1])
        one = st.sb("one", [P, 1])
        xw = st.sb("xw", [R, CONV_W, CONV_DIM])
        tapped = st.sb("tapped", [R, CONV_W, CONV_DIM])
        xc = st.sb("xc", [R, CONV_DIM])
        z, gate = (st.sb(n, [R, D_SSM]) for n in ("z", "gate"))
        dt_raw, dt = (st.sb(n, [R, HS]) for n in ("dt_raw", "dt"))
        u, ea, ln, adt, acs, eac, dec = (st.sb(n, [R, HS]) for n in ("u", "ea", "ln", "adt", "acs", "eac", "dec"))
        adtm = st.sb("adtm", [R, NB, HS]) if sample else None
        adtr = st.sb("adtr", [R, HS, R])
        et = st.sb("et", [P, NB, HS])
        xdt = st.sb("xdt", [R, HS, PS])
        xdd = st.sb("xdd", [R, HS, PS])
        xdm = st.sb("xdm", [R, NB, D_SSM]) if sample else None
        bcT = st.sb("bcT", [P, 4, R])
        cTm = st.sb("cTm", [P, NB, G, R]) if sample else None
        gt = st.sb("gt", [R, G, R])
        el = st.sb("el", [R, HS, R])
        state = st.sb("state", [P, NB, D_SSM])
        y = st.sb("y", [R, D_SSM])
        skip, sq = (st.sb(n, [R, D_SSM]) for n in ("skip", "sq"))
        ssq, rs = (st.sb(n, [R, G]) for n in ("ssq", "rs"))
        p_bc = st.ps("p_bc", [P, 4, P])
        p_sm = st.ps("p_sm", [P, 512])
        p_row = [st.ps(f"p_row{k}", [R, 4, P]) for k in range(2)]
        p_gt = st.ps("p_gt", [R, G, P])
        p_y = st.ps("p_y", [R, D_SSM])
        p_o = st.ps("p_o", [R, D_SSM])
        p_s = st.ps("p_s", [P, D_SSM])
        consts, loaded, z_in, v_done, a_done, stored = (
            st.sem(n) for n in ("consts", "loaded", "z_in", "v_done", "a_done", "stored"))
        (pool_done, rows_used, minus_abs, log_ready, adt_ready, summed, rows_up, convolved, acs_ready, less, decays, grown, activated,
         gate_ready, turned, bc_taken, scored, y_off, new_state, state_added, y_diag,
         y_ready, squared, rooted) = (
            st.sem(n) for n in (
                "pool_done", "rows_used", "minus_abs", "log_ready", "adt_ready", "summed", "rows_up", "convolved", "acs_ready", "less", "decays",
                "grown", "activated", "gate_ready", "turned", "bc_taken", "scored",
                "y_off", "new_state", "state_added", "y_diag", "y_ready", "squared", "rooted"))
        n_const = 12 if sample else 8

        def heads(ap):
            return ap.rearrange("p (h c) -> p h c", h=HS)

        per_head = [R, HS, PS]

        def load(sp, row, i, beside=False):
            if beside:
                sp.wait_ge(rows_used, 2)
                sp.wait_ge(pool_done, 2)
            if sample:
                for s_ in range(DEC_S):
                    sp.dma_start(xw[s_:R:DEC_S, :, :], t["xbc_s"][:, s_:s_ + CONV_W, :]).then_inc(loaded, 16)
            else:
                for k in range(CONV_W):
                    sp.dma_start(xw[:, k, :], t["xbc"][ds(i * P + k, P), :]).then_inc(loaded, 16)
            if beside:
                sp.wait_ge(minus_abs, 1)
            sp.dma_start(dt_raw[:], t["dt"][row, :]).then_inc(z_in, 16)
            if beside:
                sp.wait_ge(gate_ready, 1)
            sp.dma_start(z[:], t["z"][row, :]).then_inc(z_in, 16)

        def all_loaded(sp):
            sp.wait_ge(loaded, 16 * CONV_W)
            sp.wait_ge(z_in, 32)

        with nc.Block() as block:
            @block.sync
            def _(sp):
                sp.dma_start(taps[:].rearrange("p w c -> p (w c)"), spread(t["conv_w"], R)).then_inc(consts, 16)
                sp.dma_start(cbias[:], spread(t["conv_b"], R)).then_inc(consts, 16)
                sp.dma_start(gn[:], spread(t["g_ssm_norm"], R)).then_inc(consts, 16)
                sp.dma_start(dskip[:], spread(t["d_skip"], R)).then_inc(consts, 16)
                sp.dma_start(dtb[:], spread(t["dt_bias"], R)).then_inc(consts, 16)
                sp.dma_start(nega[:], spread(t["a_log"], R)).then_inc(consts, 16)
                sp.dma_start(ident[:], t["ident"]).then_inc(consts, 16)
                sp.dma_start(cum[:], t["cum_s" if sample else "cum_p"]).then_inc(consts, 16)
                if sample:
                    sp.dma_start(same[:], t["same_s"]).then_inc(consts, 16)
                    sp.dma_start(own[:], t["own_s"]).then_inc(consts, 16)
                    sp.dma_start(own_col[:].rearrange("p b r -> p (b r)"), spread(t["own_cols"])).then_inc(consts, 16)
                    sp.dma_start(state[:], t["ssm_in"].rearrange("b n c -> n b c")).then_inc(consts, 16)
                load(sp, slice(SEQ, SEQ + R) if sample else ds(0, P), 0)
                sp.wait_ge(consts, 16 * n_const)
                all_loaded(sp)

            @block.scalar
            def _(act):
                copies = [] if sample else conv_copies(t)
                for dst, src in copies:
                    act.dma_start(dst, src).then_inc(stored, 16)
                act.wait_ge(consts, 16 * n_const)
                act.activation(nega[:], nega[:], ACT.Exp).then_inc(a_done, 1)
                if copies:
                    act.wait_ge(stored, 16 * len(copies))

            @block.vector
            def _(dve):
                v = Tally(dve, v_done)
                v.did(dve.memset(eps[:], EPS))
                v.did(dve.memset(ones[:], 1.0))
                v.did(dve.memset(one[:], 1.0))
                if not sample:
                    v.did(dve.memset(same[:], 1.0))
                    v.did(dve.memset(state[:], 0.0))
                dve.wait_ge(a_done, 1)
                v.step(dve.tensor_scalar(nega[:], nega[:], -1.0, None, ALU.mult))
        st.end_pass()

        class Inner:

            def __init__(self, beside):
                self.beside = beside

            def after(self, eng, sem, n):
                if self.beside:
                    eng.wait_ge(sem, n)

            def gpsimd(self, pool):
                for k in range(2, CONV_W):
                    pool.tensor_tensor(tapped[:, k, :], xw[:, k, :], taps[:, k, :], ALU.mult).then_inc(pool_done, 1)
                pool.wait_ge(pool_done, 2)
                pool.tensor_tensor(tapped[:, 2, :], tapped[:, 2, :], tapped[:, 3, :], ALU.add).then_inc(pool_done, 1)
                pool.wait_ge(pool_done, 3)
                pool.tensor_tensor(tapped[:, 2, :], tapped[:, 2, :], cbias[:], ALU.add).then_inc(pool_done, 1)

            def vector_first(self, dve, v):
                v.step(dve.tensor_tensor(u[:], dt_raw[:], dtb[:], ALU.add))
                dve.scalar_tensor_tensor(out=ea[:], in0=u[:], scalar=-1.0, in1=u[:], op0=ALU.mult,
                                         op1=ALU.min).then_inc(minus_abs, 1)
                for k in range(2):
                    dve.tensor_tensor(tapped[:, k, :], xw[:, k, :], taps[:, k, :], ALU.mult).then_inc(rows_used, 1)
                dve.wait_ge(rows_used, 2)
                v.step(dve.tensor_tensor(tapped[:, 0, :], tapped[:, 0, :], tapped[:, 1, :], ALU.add))
                dve.wait_ge(log_ready, 2)
                v.step(dve.scalar_tensor_tensor(out=dt[:], in0=u[:], scalar=0.0, in1=ln[:], op0=ALU.max, op1=ALU.add))
                v.step(dve.tensor_tensor(adt[:], dt[:], nega[:], ALU.mult))
                if sample:
                    for b in range(NB):
                        v.did(dve.tensor_scalar(adtm[:, b, :], adt[:], own[:, b:b + 1], None, ALU.mult))
                    v.settle()
                dve.tensor_copy(adtr[:], wide(adt[:], [R, HS, R])).then_inc(adt_ready, 1)

            def vector_then(self, dve, v):
                dve.wait_ge(summed, 1)
                v.step(dve.tensor_copy(acs[:], p_sm[:R, 0:HS]))
                dve.tensor_tensor(dec[:], p_sm[:R, HS:2 * HS], acs[:], ALU.subtract).then_inc(acs_ready, 1)
                dve.wait_ge(pool_done, 4)
                dve.tensor_tensor(tapped[:, 0, :], tapped[:, 0, :], tapped[:, 2, :], ALU.add).then_inc(convolved, 1)
                dve.wait_ge(rows_up, 1)
                self.after(dve, y_diag, 1)
                for k in range(2):
                    v.did(dve.tensor_tensor(el[:, 4 * k:4 * k + 4, :], p_row[k][:, :, 0:R],
                                            wide(acs[:, 4 * k:4 * k + 4], [R, 4, R]), ALU.subtract))
                v.settle()
                dve.tensor_scalar(el[:], el[:], 0.0, None, ALU.min).then_inc(less, 1)

            def vector_last(self, dve, v):
                dve.wait_ge(activated, 1)
                xs = heads(xc[:, 0:D_SSM])
                v.did(dve.tensor_tensor(xdt[:], xs, wide(dt[:], per_head), ALU.mult))
                v.did(dve.tensor_tensor(heads(skip[:]), xs, wide(dskip[:], per_head), ALU.mult))
                v.settle()
                dve.wait_ge(decays, 1)
                self.after(dve, new_state, NB)
                v.step(dve.tensor_tensor(xdd[:], xdt[:], wide(dec[:], per_head), ALU.mult))
                if sample:
                    dve.wait_ge(bc_taken, 1)
                    for b in range(NB):
                        v.did(dve.tensor_scalar(xdm[:, b, :], xdd[:].rearrange("p h c -> p (h c)"),
                                                own[:, b:b + 1], None, ALU.mult))
                        v.did(dve.tensor_tensor(cTm[:, b], bcT[:, 2:4, :],
                                                own_col[:, b:b + 1, :].to_broadcast([P, G, R]), ALU.mult))
                dve.wait_ge(scored, 1)
                v.step(dve.tensor_tensor(gt[:], p_gt[:, :, 0:R], cum[:].unsqueeze(1).to_broadcast([R, G, R]), ALU.mult))
                dve.wait_ge(grown, 1)
                for g in range(G):
                    v.did(dve.tensor_tensor(el[:, 4 * g:4 * g + 4, :], el[:, 4 * g:4 * g + 4, :],
                                            gt[:, g:g + 1, :].to_broadcast([R, 4, R]), ALU.mult))

            def scalar_first(self, act):
                act.wait_ge(minus_abs, 1)
                act.activation(ea[:], ea[:], ACT.Exp).then_inc(log_ready, 1)
                act.wait_ge(log_ready, 1)
                act.activation(ln[:], ea[:], ACT.Ln, bias=one[:R]).then_inc(log_ready, 1)

            def scalar_then(self, act):
                act.wait_ge(convolved, 1)
                self.after(act, new_state, NB)
                act.activation(xc[:], tapped[:, 0, :], ACT.Silu).then_inc(activated, 1)
                self.after(act, y_ready, 1)
                act.activation(gate[:], z[:], ACT.Silu).then_inc(gate_ready, 1)
                act.wait_ge(turned, 1)
                self.after(act, y_off, 1)
                act.activation(bcT[:], p_bc[:, :, 0:R], ACT.Copy).then_inc(bc_taken, 1)
                act.wait_ge(acs_ready, 1)
                act.activation(dec[:], dec[:], ACT.Exp).then_inc(decays, 1)
                act.activation(eac[:], acs[:], ACT.Exp).then_inc(decays, 1)
                self.after(act, state_added, NB)
                act.activation(et[:].rearrange("p b h -> p (b h)"), p_sm[:, 2 * HS:2 * HS + NB * HS],
                               ACT.Exp).then_inc(decays, 1)
                act.wait_ge(less, 1)
                act.activation(el[:], el[:], ACT.Exp).then_inc(grown, 1)

            def tensor(self, pe):
                pe.wait_ge(adt_ready, 1)
                pe.matmul(p_sm[:R, 0:HS], cum[:], adt[:], start=True, stop=True)
                pe.matmul(p_sm[:R, HS:2 * HS], same[:], adt[:], start=True, stop=True)
                own_adt = adtm[:].rearrange("p b h -> p (b h)") if sample else adt[:]
                pe.matmul(p_sm[:, 2 * HS:2 * HS + NB * HS], ones[:], own_adt, start=True, stop=True).then_inc(summed, 1)
                for h in range(HS):
                    mm = pe.matmul(p_row[h // 4][:, h % 4, 0:R], adtr[:, h, :], cum[:], start=True, stop=True)
                mm.then_inc(rows_up, 1)
                pe.wait_ge(activated, 1)
                for k in range(4):
                    mm = pe.transpose(p_bc[:, k, 0:R], xc[:, D_SSM + k * NS:D_SSM + (k + 1) * NS], ident[:R, :R])
                mm.then_inc(turned, 1)
                pe.wait_ge(bc_taken, 1)
                for g in range(G):
                    mm = pe.matmul(p_gt[:, g, 0:R], bcT[:, g, :], bcT[:, 2 + g, :], start=True, stop=True)
                mm.then_inc(scored, 1)

        new_banks = [p_s[:], p_bc[:].rearrange("p k s -> p (k s)")]

        class Outer:
            @staticmethod
            def sync(sp, row):
                sp.wait_ge(y_ready, 1 + G)
                if sample:
                    for r in range(REP):
                        sp.dma_start(t["mix"][SEQ + r * R:SEQ + (r + 1) * R, 0:D_SSM], y[:]).then_inc(stored, 16)
                    for b in range(NB):
                        sp.wait_ge(state_added, b + 1)
                        sp.dma_start(t["ssm_s"][b], state[:, b, :]).then_inc(stored, 16)
                    sp.wait_ge(stored, 16 * (REP + NB))
                else:
                    sp.dma_start(t["mix"][row, 0:D_SSM], y[:]).then_inc(stored, 16)
                    sp.wait_ge(stored, 16)

            @staticmethod
            def tensor(pe):
                for g in range(G):
                    for b in range(NB):
                        c = cTm[:, b, g, :] if sample else bcT[:, 2 + g, :]
                        mm = pe.matmul(p_o[:, g * HALF:(g + 1) * HALF], c, state[:, b, g * HALF:(g + 1) * HALF],
                                       start=(b == 0), stop=(b == NB - 1))
                mm.then_inc(y_off, 1)
                for b in range(NB):
                    if b >= 2:
                        pe.wait_ge(state_added, b - 1)
                    for g in range(G):
                        part = slice(g * HALF, (g + 1) * HALF)
                        new = xdm[:, b, part] if sample else xdd[:, g * 4:(g + 1) * 4, :].rearrange("p h c -> p (h c)")
                        mm = pe.matmul(new_banks[b % 2][:, part], xc[:, D_SSM + g * NS:D_SSM + (g + 1) * NS], new,
                                       start=True, stop=True)
                    mm.then_inc(new_state, 1)
                    if b == 0:
                        for h in range(HS):
                            mm = pe.matmul(p_y[:, h * PS:(h + 1) * PS], el[:, h, :], xdt[:, h, :], start=True, stop=True)
                        mm.then_inc(y_diag, 1)

            @staticmethod
            def vector_first(dve, v):
                dve.wait_ge(y_off, 1)
                v.step(dve.tensor_tensor(heads(y[:]), heads(p_o[:]), wide(eac[:], per_head), ALU.mult))
                dve.wait_ge(y_diag, 1)
                v.step(dve.tensor_tensor(y[:], y[:], p_y[:], ALU.add))
                v.step(dve.tensor_tensor(y[:], y[:], skip[:], ALU.add))
                dve.tensor_tensor(y[:], y[:], gate[:], ALU.mult).then_inc(y_ready, 1)

            @staticmethod
            def vector_state(dve, v):
                for b in range(NB):
                    sb = state[:, b, :]
                    v.step(dve.tensor_tensor(heads(sb), heads(sb), wide(et[:, b, :], [P, HS, PS]), ALU.mult))
                    dve.wait_ge(new_state, b + 1)
                    dve.tensor_tensor(sb, sb, new_banks[b % 2], ALU.add).then_inc(state_added, 1)

            @staticmethod
            def vector_then(dve, v):
                dve.wait_ge(rooted, 1)
                v.step(dve.reciprocal(rs[:], rs[:]))
                for g in range(G):
                    part = slice(g * HALF, (g + 1) * HALF)
                    dve.scalar_tensor_tensor(out=y[:, part], in0=y[:, part], scalar=rs[:, g:g + 1], in1=gn[:, part],
                                             op0=ALU.mult, op1=ALU.mult).then_inc(y_ready, 1)

            @staticmethod
            def scalar(act):
                act.wait_ge(y_ready, 1)
                for g in range(G):
                    part = slice(g * HALF, (g + 1) * HALF)
                    act.activation(sq[:, part], y[:, part], ACT.Square, accum_out=ssq[:, g:g + 1]).then_inc(squared, 1)
                act.wait_ge(squared, G)
                root(act, rs[:], ssq[:], HALF, eps[:R]).then_inc(rooted, 1)

        def inner_block(row_ahead):
            inner = Inner(False)
            with nc.Block() as block:
                @block.sync
                def _(sp):
                    if row_ahead is not None:
                        load(sp, ds(row_ahead * P, P), row_ahead, True)
                        all_loaded(sp)

                @block.gpsimd
                def _(pool):
                    inner.gpsimd(pool)

                @block.vector
                def _(dve):
                    v = Tally(dve, v_done)
                    inner.vector_first(dve, v)
                    inner.vector_then(dve, v)
                    inner.vector_last(dve, v)

                @block.scalar
                def _(act):
                    inner.scalar_first(act)
                    inner.scalar_then(act)

                @block.tensor
                def _(pe):
                    inner.tensor(pe)
            st.end_pass()

        def outer_block(row):
            with nc.Block() as block:
                @block.sync
                def _(sp):
                    Outer.sync(sp, row)
                    if not sample:
                        sp.wait_ge(state_added, NB)
                        sp.dma_start(t["ssm_p"], state[:, 0, :]).then_inc(stored, 16)
                        sp.wait_ge(stored, 32)

                @block.vector
                def _(dve):
                    v = Tally(dve, v_done)
                    Outer.vector_first(dve, v)
                    Outer.vector_then(dve, v)
                    Outer.vector_state(dve, v)

                @block.scalar
                def _(act):
                    Outer.scalar(act)

                @block.tensor
                def _(pe):
                    Outer.tensor(pe)
            st.end_pass()

        if sample:
            inner_block(None)
            outer_block(None)
        else:
            inner_block(1)
            with nc.Fori(0, PT - 1) as i:
                inner = Inner(True)
                with nc.Block() as block:
                    @block.sync
                    def _(sp):
                        load(sp, ds((i + 2) * P, P), i + 2, True)
                        Outer.sync(sp, ds(i * P, P))
                        all_loaded(sp)

                    @block.gpsimd
                    def _(pool):
                        inner.gpsimd(pool)

                    @block.vector
                    def _(dve):
                        v = Tally(dve, v_done)
                        inner.vector_first(dve, v)
                        Outer.vector_first(dve, v)
                        Outer.vector_state(dve, v)
                        inner.vector_then(dve, v)
                        Outer.vector_then(dve, v)
                        inner.vector_last(dve, v)

                    @block.scalar
                    def _(act):
                        inner.scalar_first(act)
                        Outer.scalar(act)
                        inner.scalar_then(act)

                    @block.tensor
                    def _(pe):
                        Outer.tensor(pe)
                        inner.tensor(pe)
                st.end_pass()
            outer_block(slice(SEQ - P, SEQ))


def conv_copies(t):
    new = t["xbc"][CONV_W - 1 + SEQ:CONV_W - 1 + SEQ + DEC, :].rearrange("(b s) c -> b s c", s=DEC_S)
    return [(t["xbc_s"][:, 0:CONV_W - 1, :], t["state_conv"]), (t["xbc_s"][:, CONV_W - 1:, :], new),
            (t["conv_p"], t["xbc"][SEQ:SEQ + CONV_W - 1, :]), (t["conv_s"], new[:, 1:, :])]


def lambdas(act, dve, v, lq, prod, sums, lam, ready, back):
    if dve is not None:
        for m in range(2):
            v.did(dve.tensor_tensor(prod[:, m, :], lq[:, 2 * m, :], lq[:, 2 * m + 1, :], ALU.mult))
        v.settle()
        dve.tensor_reduce(sums[:], prod[:], AX_X, ALU.add).then_inc(ready, 1)
        dve.wait_ge(back, 1)
        dve.scalar_tensor_tensor(out=lam[:], in0=sums[:, 0:1], scalar=LAM_INIT, in1=sums[:, 1:2], op0=ALU.add,
                                 op1=ALU.subtract).then_inc(ready, 1)
    else:
        act.wait_ge(ready, 1)
        act.activation(sums[:], sums[:], ACT.Exp).then_inc(back, 1)


class Early:

    def __init__(self, nc, ctx):
        self.stage = st = Stage(nc, ctx, "ea")
        self.fan_out, self.pages_in, self.k_in, self.v_in = (st.sem(n) for n in ("fan_out", "pages_in", "k_in", "v_in"))

    def hold(self, ctx):
        st = Stage(self.stage.nc, ctx, "eb")
        self.pages = st.sb("pages", [1, PAGES * DEC_B], I32)
        self.kT = st.sb("kT", [P, PAGES, HD * PAGE])
        self.val = st.sb("val", [P, PAGES, DV])

    def fetch(self, eng, t, first, count):
        n_pool = t["cache_v"].shape[0]
        for j in range(count):
            page = eng.value_load(self.pages[0:1, ds(first + j, 1)], min_val=0, max_val=n_pool - 1)
            for dst, src, sem in ((self.kT, t["cache_kT"], self.k_in), (self.val, t["cache_v"], self.v_in)):
                eng.dma_start(dst[:, ds(first + j, 1), :].rearrange("p a n -> p (a n)"),
                              src[ds(page, 1), :, :].rearrange("a p n -> p (a n)")).then_inc(sem, 16)


def attend_prompt(nc, t, early):
    with ExitStack() as ctx:
        lasting = Stage(nc, ctx, "apl")
        rest_in = lasting.sem("rest_in")
        st = Stage(nc, ctx, "ap")
        kT = st.sb("kT", [P, HD, SEQ])
        qT = st.sb("qT", [P, HD, SEQ])
        val = st.sb("val", [P, PT, DV])
        bias = st.sb("bias", [P, HD, SEQ])
        k_cur, q_cur, b_cur = (st.sb(n, [P, SEQ]) for n in ("k_cur", "q_cur", "b_cur"))
        v_cur = st.sb("v_cur", [P, PT, P])
        ident = st.sb("ident", [P, P])
        gd = st.sb("gd", [P, 2 * DH])
        lq = st.sb("lq", [P, 4, DH])
        prod = st.sb("prod", [P, 2, DH])
        sums = st.sb("sums", [P, 2])
        lam = st.sb("lam", [P, 1])
        neg_lam = st.sb("neg_lam", [P, 1])
        eps = st.sb("eps", [P, 1])
        AHEAD = 3
        s = [[st.sb(f"s{k}{m}", [P, SEQ]) for m in range(2)] for k in range(AHEAD)]
        mx = st.sb("mx", [P, 2 * PT])
        total = st.sb("total", [P, 2 * PT])
        inv = st.sb("inv", [P, 2 * PT])
        ratio = st.sb("ratio", [P, PT])
        wT = [st.sb(f"wT{k}", [P, PT, P]) for k in range(2)]
        o = st.sb("o", [P, PT, HD, P])
        sq = st.sb("sq", [P, 2 * DH])
        ssq_cur = st.sb("ssq_cur", [P, PT])
        ssq, rs = (st.sb(n, [P, HD, PT]) for n in ("ssq", "rs"))
        p_s = [st.ps(f"p_s{k}", [P, SEQ]) for k in range(2)]
        p_t = [st.ps(f"p_t{k}", [P, 4, P]) for k in range(2)]
        p_o = [st.ps(f"p_o{k}", [P, P]) for k in range(2)]
        consts, head_in, v_done, stored = (st.sem(n) for n in ("consts", "head_in", "v_done", "stored"))
        (lam_ready, lam_back, cur_v, cur_a, scored, maxed, neg_ready, grown, weighed, turned_a, turned_v, taken_a,
         taken_v, mixed, o_taken, squared, rooted, o_done) = (
            st.sem(n) for n in (
                "lam_ready", "lam_back", "cur_v", "cur_a", "scored", "maxed", "neg_ready", "grown", "weighed",
                "turned_a", "turned_v", "taken_a", "taken_v", "mixed", "o_taken", "squared", "rooted", "o_done"))

        def load_head(eng, h, sem):
            cols = slice(h * P, (h + 1) * P)
            for dst, src in ((kT, t["kT"]), (qT, t["qT"])):
                eng.dma_start(dst[:, h, :].rearrange("p (j k) -> p j k", k=P),
                              src[0:SEQ, cols].rearrange("(j p) k -> p j k", p=P)).then_inc(sem, 16)
            eng.dma_start(bias[:, h, :], bass.AP(t["fan"].tensor, h * P * FAN + SEQ - 1 - (PT - 1) * P,
                                                 [[FAN - 1, P], [1, SEQ]])).then_inc(sem, 16)
            eng.dma_start(val[:, :, cols], t["v_all"][0:SEQ, cols].rearrange("(j p) e -> p j e", p=P)).then_inc(sem, 16)

        with nc.Block() as block:
            @block.sync
            def _(sp):
                sp.dma_start(early.pages[:], t["pages"]).then_inc(early.pages_in, 16)
                sp.wait_ge(early.fan_out, 16 * HD)
                load_head(sp, 0, head_in)
                for h in range(1, HD):
                    load_head(sp, h, rest_in)
                sp.wait_ge(head_in, 16 * 4)

            @block.scalar
            def _(act):
                for n in range(4):
                    act.dma_start(lq[:, n, :], spread(t["lam"][n])).then_inc(consts, 16)
                act.dma_start(ident[:], t["ident"]).then_inc(consts, 16)
                act.dma_start(gd[:], spread(t["g_diff_norm"])).then_inc(consts, 16)
                lambdas(act, None, None, lq, prod, sums, lam, lam_ready, lam_back)

            @block.vector
            def _(dve):
                v = Tally(dve, v_done)
                v.did(dve.memset(eps[:], EPS))
                dve.wait_ge(consts, 16 * 6)
                v.did(dve.tensor_scalar(gd[:], gd[:], 1.0 - LAM_INIT, None, ALU.mult))
                lambdas(None, dve, v, lq, prod, sums, lam, lam_ready, lam_back)
                dve.wait_ge(lam_ready, 2)
                v.step(dve.tensor_scalar(neg_lam[:], lam[:], -1.0, None, ALU.mult))
        st.end_pass()

        with nc.Fori(0, HD) as h:
            with nc.Block() as block:
                @block.sync
                def _(sp):
                    sp.wait_ge(early.pages_in, 16)
                    early.fetch(sp, t, h * (PAGES // HD), PAGES // HD)
                    sp.wait_ge(rest_in, 16 * 4 * (HD - 1))

                @block.tensor
                def _(pe):
                    def scores(u):
                        i = PT - 1 - u
                        width = (i + 1) * P
                        for m in range(2):
                            n = 2 * u + m
                            if n >= 2:
                                pe.wait_ge(maxed, n - 1)
                            part = slice(m * DH, (m + 1) * DH)
                            for c in range(0, width, 512):
                                end = min(c + 512, width)
                                mm = pe.matmul(p_s[m][:, c:end], q_cur[part, i * P:(i + 1) * P], k_cur[part, c:end],
                                               start=True, stop=True)
                            mm.then_inc(scored, 1)

                    def turn(u):
                        i = PT - 1 - u
                        pe.wait_ge(weighed, u + 1)
                        if i >= 4:
                            if u:
                                pe.wait_ge(taken_v, u)
                            for j in range(4, i + 1):
                                mm = pe.transpose(p_t[1][:, j - 4, :], s[u % AHEAD][0][:, j * P:(j + 1) * P], ident[:])
                            mm.then_inc(turned_v, 1)
                        if u:
                            pe.wait_ge(taken_a, u)
                        for j in range(min(4, i + 1)):
                            mm = pe.transpose(p_t[0][:, j, :], s[u % AHEAD][0][:, j * P:(j + 1) * P], ident[:])
                        mm.then_inc(turned_a, 1)

                    def mix(u):
                        i = PT - 1 - u
                        if u >= 2:
                            pe.wait_ge(o_taken, u - 1)
                        pe.wait_ge(taken_a, u + 1)
                        for j in range(i + 1):
                            if j == 4:
                                pe.wait_ge(taken_v, u + 1)
                            mm = pe.matmul(p_o[u % 2][:], wT[u % 2][:, j, :], v_cur[:, j, :], start=(j == 0),
                                           stop=(j == i))
                        mm.then_inc(mixed, 1)

                    pe.wait_ge(cur_v, 1)
                    pe.wait_ge(cur_a, 1)
                    for u in range(AHEAD):
                        scores(u)
                    for u in range(PT):
                        turn(u)
                        if u + AHEAD < PT:
                            scores(u + AHEAD)
                        if u == 0:
                            pe.wait_ge(cur_a, 2)
                        mix(u)

                @block.vector
                def _(dve):
                    v = Tally(dve, v_done)

                    def soften(u):
                        i = PT - 1 - u
                        width = (i + 1) * P
                        if u >= AHEAD:
                            dve.wait_ge(turned_a, u - AHEAD + 1)
                        for m in range(2):
                            n = 2 * u + m
                            dve.wait_ge(scored, n + 1)
                            dve.tensor_tensor_reduce(out=s[u % AHEAD][m][:, 0:width], in0=p_s[m][:, 0:width],
                                                     in1=b_cur[:, SEQ - width:], scale=1.0, scalar=NEG, op0=ALU.add,
                                                     op1=ALU.max, accum_out=mx[:, n:n + 1]).then_inc(maxed, 1)
                            dve.wait_ge(maxed, n + 1)
                            dve.tensor_scalar(mx[:, n:n + 1], mx[:, n:n + 1], -1.0, None, ALU.mult).then_inc(neg_ready, 1)

                    def weigh(u):
                        width = (PT - u) * P
                        a, b = (s[u % AHEAD][m][:, 0:width] for m in range(2))
                        dve.wait_ge(grown, 2 * u + 2)
                        v.step(dve.reciprocal(inv[:, 2 * u:2 * u + 2], total[:, 2 * u:2 * u + 2]))
                        v.step(dve.scalar_tensor_tensor(out=ratio[:, u:u + 1], in0=total[:, 2 * u:2 * u + 1],
                                                        scalar=inv[:, 2 * u + 1:2 * u + 2], in1=neg_lam[:], op0=ALU.mult,
                                                        op1=ALU.mult))
                        dve.scalar_tensor_tensor(out=a, in0=b, scalar=ratio[:, u:u + 1], in1=a, op0=ALU.mult,
                                                 op1=ALU.add).then_inc(weighed, 1)

                    def take(u):
                        i = PT - 1 - u
                        if i >= 4:
                            dve.wait_ge(turned_v, u + 1)
                            if u >= 2:
                                dve.wait_ge(mixed, u - 1)
                            dve.tensor_copy(wT[u % 2][:, 4:i + 1, :], p_t[1][:, 0:i - 3, :]).then_inc(taken_v, 1)

                    def out(u):
                        dve.wait_ge(mixed, u + 1)
                        dve.tensor_scalar(o[:, PT - 1 - u, ds(h, 1), :].rearrange("p a e -> p (a e)"), p_o[u % 2][:],
                                          inv[:, 2 * u:2 * u + 1], None, ALU.mult).then_inc(o_taken, 1)

                    dve.tensor_copy(q_cur[:], qT[:, ds(h, 1), :].rearrange("p a k -> p (a k)")).then_inc(cur_v, 1)
                    v.did(dve.tensor_copy(b_cur[:], bias[:, ds(h, 1), :].rearrange("p a k -> p (a k)")))
                    v.settle()
                    soften(0)
                    soften(1)
                    for u in range(PT):
                        weigh(u)
                        if u + 2 < PT:
                            soften(u + 2)
                        take(u)
                        if u:
                            out(u - 1)
                    out(PT - 1)

                @block.scalar
                def _(act):
                    def grow(u):
                        width = (PT - u) * P
                        for m in range(2):
                            n = 2 * u + m
                            act.wait_ge(neg_ready, n + 1)
                            part = s[u % AHEAD][m][:, 0:width]
                            act.activation(part, part, ACT.Exp, bias=mx[:, n:n + 1],
                                           accum_out=total[:, n:n + 1]).then_inc(grown, 1)

                    def take(u):
                        n = min(4, PT - u)
                        act.wait_ge(turned_a, u + 1)
                        if u >= 2:
                            act.wait_ge(mixed, u - 1)
                        act.activation(wT[u % 2][:, 0:n, :], p_t[0][:, 0:n, :], ACT.Copy).then_inc(taken_a, 1)

                    def square(u):
                        act.wait_ge(o_taken, u + 1)
                        if u:
                            act.wait_ge(squared, u)
                        i = PT - 1 - u
                        act.activation(sq[:], o[:, i, ds(h, 1), :].rearrange("p a e -> p (a e)"), ACT.Square,
                                       accum_out=ssq_cur[:, i:i + 1]).then_inc(squared, 1)

                    act.activation(k_cur[:], kT[:, ds(h, 1), :].rearrange("p a k -> p (a k)"), ACT.Copy).then_inc(cur_a, 1)
                    act.activation(v_cur[:], val[:, :, ds(h * P, P)], ACT.Copy).then_inc(cur_a, 1)
                    grow(0)
                    grow(1)
                    for u in range(PT):
                        if u + 2 < PT:
                            grow(u + 2)
                        take(u)
                        if u:
                            square(u - 1)
                    square(PT - 1)
                    act.wait_ge(squared, PT)
                    act.activation(ssq[:, ds(h, 1), :].rearrange("p a i -> p (a i)"), ssq_cur[:], ACT.Copy)
            st.end_pass()

        with nc.Block() as block:
            @block.scalar
            def _(act):
                root(act, rs[:], ssq[:], 2 * DH, eps[:]).then_inc(rooted, 1)

            @block.vector
            def _(dve):
                v = Tally(dve, v_done)
                dve.wait_ge(rooted, 1)
                v.step(dve.reciprocal(rs[:], rs[:]))
                for i in range(PT):
                    v.step(dve.tensor_tensor(o[:, i], o[:, i], wide(rs[:, :, i], [P, HD, P]), ALU.mult))
                    dve.tensor_tensor(o[:, i], o[:, i], gd[:].unsqueeze(1).to_broadcast([P, HD, P]), ALU.mult).then_inc(
                        o_done, 1)

            @block.sync
            def _(sp):
                for i in range(PT):
                    sp.wait_ge(o_done, i + 1)
                    sp.dma_start(t["mix"][i * P:(i + 1) * P, D_SSM:], o[:, i].rearrange("p h e -> p (h e)")).then_inc(
                        stored, 16)
                sp.wait_ge(stored, 16 * PT)
        st.end_pass()
        lasting.end_pass()


def attend_sample(nc, t, early):
    NR, NW = 2 * HD * DEC_S, HD * DEC_S
    NKEY = PAST + DEC_S
    with ExitStack() as ctx:
        st = Stage(nc, ctx, "as")
        kT = [early.kT, st.sb("kT1", [P, PAGES, HD * PAGE])]
        val = [early.val, st.sb("val1", [P, PAGES, DV])]
        kN = [st.sb(f"kN{k}", [P, HD, DEC_S]) for k in range(2)]
        vN = [st.sb(f"vN{k}", [DEC_S, DV]) for k in range(2)]
        pages = early.pages
        qT = st.sb("qT", [P, HD, DEC])
        qm = st.sb("qm", [P, HD, DEC_B, NR])
        bias = st.sb("bias", [NR, NKEY])
        sel = st.sb("sel", [NR, NW])
        lq = st.sb("lq", [P, 4, DH])
        prod = st.sb("prod", [P, 2, DH])
        sums = st.sb("sums", [P, 2])
        lam = st.sb("lam", [P, 1])
        sign = st.sb("sign", [NR, 2])
        coef = st.sb("coef", [NR, 1])
        eps = st.sb("eps", [P, 1])
        gd = st.sb("gd", [DEC, 2 * DH])
        s = [st.sb(f"s{k}", [NR, NKEY]) for k in range(2)]
        mx, top, total, inv = (st.sb(n, [NR, 1]) for n in ("mx", "top", "total", "inv"))
        mix = [st.sb(f"mix{k}", [NR, NW]) for k in range(2)]
        qc = [st.sb(f"qc{k}", [P, HD, NR]) for k in range(2)]
        wT = st.sb("wT", [P, PAGES + 1, NW])
        o_all = st.sb("o_all", [NW, DEC_B, DV])
        o = st.sb("o", [DEC, HD, 2 * DH])
        sq = st.sb("sq", [DEC, 2 * DH])
        ssq, rs = (st.sb(n, [DEC, HD]) for n in ("ssq", "rs"))
        p_s = st.ps("p_s", [NR, PAST])
        p_n = st.ps("p_n", [NR, DEC_S])
        p_w = st.ps("p_w", [P, PAGES + 1, NW])
        p_o = st.ps("p_o", [NW, DV])
        consts, v_done, stored, first = (st.sem(n) for n in ("consts", "v_done", "stored", "first"))
        k_in = [st.sem(f"k_in{k}") for k in range(2)]
        v_in = [st.pool_sem(f"v_in{k}") for k in range(2)]
        (lam_ready, lam_back, q_ready, scored, maxed, neg_ready, grown, mix_ready, weighed, w_taken, mixed, o_taken,
         squared, rooted, o_done) = (
            st.sem(n) for n in (
                "lam_ready", "lam_back", "q_ready", "scored", "maxed", "neg_ready", "grown", "mix_ready", "weighed",
                "w_taken", "mixed", "o_taken", "squared", "rooted", "o_done"))
        k_pool = t["cache_kT"]
        v_pool = t["cache_v"]
        N_POOL = k_pool.shape[0]
        FETCHED = 16 * (PAGES + 1)

        def new_keys(eng, b, slot):
            kt = t["kT"][SEQ:SEQ + P, :].rearrange("p (h q) -> p h q", h=HD)
            eng.dma_start(kN[slot][:], kt[:, :, ds(b * DEC_S, DEC_S)]).then_inc(k_in[slot], 16)

        def new_values(eng, b, slot, sem):
            eng.dma_start(vN[slot][:], t["v_all"][ds(SEQ + b * DEC_S, DEC_S), :]).then_inc(sem, 16)

        def fetch_keys(eng, b, slot):
            for p in range(PAGES):
                page = eng.value_load(pages[0:1, ds(b * PAGES + p, 1)], min_val=0, max_val=N_POOL - 1)
                eng.dma_start(kT[slot][:, p, :], k_pool[ds(page, 1), :, :].rearrange("a p n -> p (a n)")).then_inc(
                    k_in[slot], 16)
            new_keys(eng, b, slot)

        def fetch_values(eng, b, slot):
            for p in range(PAGES):
                page = eng.value_load(pages[0:1, ds(b * PAGES + p, 1)], min_val=0, max_val=N_POOL - 1)
                eng.dma_start(val[slot][:, p, :], v_pool[ds(page, 1), :, :].rearrange("a p n -> p (a n)")).then_inc(
                    v_in[slot], 16)
            new_values(eng, b, slot, v_in[slot])

        def make_scores(pe, k):
            for c in range(PAGES // 4):
                for h in range(HD):
                    pe.matmul(p_s[:, c * 512:(c + 1) * 512], qc[k][:, h, :],
                              kT[k][:, 4 * c:4 * c + 4, h * PAGE:(h + 1) * PAGE], start=(h == 0), stop=(h == HD - 1))
            for h in range(HD):
                mm = pe.matmul(p_n[:], qc[k][:, h, :], kN[k][:, h, :], start=(h == 0), stop=(h == HD - 1))
            mm.then_inc(scored, 1)

        def soften(dve, v, k, n):
            dve.wait_ge(scored, n + 1)
            dve.tensor_tensor_reduce(out=s[k][:, 0:PAST], in0=p_s[:], in1=bias[:, 0:PAST], scale=1.0, scalar=NEG,
                                     op0=ALU.add, op1=ALU.max, accum_out=mx[:]).then_inc(maxed, 1)
            dve.wait_ge(maxed, 2 * n + 1)
            dve.tensor_tensor_reduce(out=s[k][:, PAST:], in0=p_n[:], in1=bias[:, PAST:], scale=1.0, scalar=mx[:],
                                     op0=ALU.add, op1=ALU.max, accum_out=top[:]).then_inc(maxed, 1)
            dve.wait_ge(maxed, 2 * n + 2)
            dve.tensor_scalar(mx[:], top[:], -1.0, None, ALU.mult).then_inc(neg_ready, 1)
            dve.wait_ge(grown, n + 1)
            v.step(dve.reciprocal(inv[:], total[:]))
            v.step(dve.tensor_tensor(inv[:], inv[:], coef[:], ALU.mult))
            dve.tensor_scalar(mix[k][:], sel[:], inv[:], None, ALU.mult).then_inc(mix_ready, 1)

        def grow(act, k, n):
            act.wait_ge(neg_ready, n + 1)
            act.activation(s[k][:], s[k][:], ACT.Exp, bias=mx[:], accum_out=total[:]).then_inc(grown, 1)

        def queries(dve, b, k):
            dve.tensor_copy(qc[k][:], qm[:, :, ds(b, 1), :].rearrange("p h a r -> p h (a r)")).then_inc(q_ready, 1)

        with nc.Block() as block:
            @block.sync
            def _(sp):
                new_keys(sp, 0, 0)
                new_values(sp, 0, 0, first)
                for m in range(2):
                    for tok in range(DEC_S):
                        r = m * NW + tok
                        sp.dma_start(bias[r:r + NW - DEC_S + 1:DEC_S, :],
                                     bass.AP(t["line"].tensor, X_OFF - PAST - tok, [[LINE, HD], [1, NKEY]])).then_inc(
                            consts, 16)
                sp.wait_ge(consts, 16 * (8 + 2 * HD))
                fetch_keys(sp, 1, 1)
                sp.wait_ge(first, 16)
                sp.wait_ge(early.v_in, 16 * PAGES)
                sp.wait_ge(k_in[1], FETCHED)

            @block.scalar
            def _(act):
                act.dma_start(qT[:], t["qT"][SEQ:SEQ + P, :].rearrange("p (h q) -> p h q", h=HD)[:, :, 0:DEC]).then_inc(
                    consts, 16)
                for n in range(4):
                    act.dma_start(lq[:, n, :], spread(t["lam"][n])).then_inc(consts, 16)
                act.dma_start(sel[:], t["sel_w"]).then_inc(consts, 16)
                act.dma_start(sign[:], t["sign_w"]).then_inc(consts, 16)
                act.dma_start(gd[:], spread(t["g_diff_norm"], DEC)).then_inc(consts, 16)
                act.wait_ge(consts, 16 * (8 + 2 * HD))
                lambdas(act, None, None, lq, prod, sums, lam, lam_ready, lam_back)
                grow(act, 0, 0)

            @block.vector
            def _(dve):
                v = Tally(dve, v_done)
                v.did(dve.memset(eps[:], EPS))
                v.did(dve.memset(qm[:], 0.0))
                dve.wait_ge(consts, 16 * (8 + 2 * HD))
                v.did(dve.tensor_scalar(gd[:], gd[:], 1.0 - LAM_INIT, None, ALU.mult))
                v.settle()
                for m in range(2):
                    for h in range(HD):
                        r = (m * HD + h) * DEC_S
                        part = slice(m * DH, (m + 1) * DH)
                        v.did(dve.tensor_copy(qm[part, h, :, r:r + DEC_S],
                                              qT[part, h, :].rearrange("p (b s) -> p b s", s=DEC_S)))
                v.settle()
                queries(dve, 0, 0)
                lambdas(None, dve, v, lq, prod, sums, lam, lam_ready, lam_back)
                dve.wait_ge(lam_ready, 2)
                v.step(dve.scalar_tensor_tensor(out=coef[:], in0=sign[:, 1:2], scalar=lam[0:NR, :], in1=sign[:, 0:1],
                                                op0=ALU.mult, op1=ALU.add))
                soften(dve, v, 0, 0)

            @block.tensor
            def _(pe):
                pe.wait_ge(q_ready, 1)
                pe.wait_ge(early.k_in, 16 * PAGES)
                pe.wait_ge(k_in[0], 16)
                make_scores(pe, 0)
        st.end_pass()

        def two_sequences(i, last):
            ahead = 1 if last else 2
            with nc.Block() as block:
                @block.sync
                def _(sp):
                    if not last:
                        fetch_keys(sp, 2 * i + 2, 0)
                        sp.wait_ge(scored, 1)
                        fetch_keys(sp, 2 * i + 3, 1)
                        sp.wait_ge(k_in[1], FETCHED)

                @block.tensor
                def _(pe):
                    for j in range(2):
                        if j < ahead:
                            pe.wait_ge(q_ready, j + 1)
                            if j:
                                pe.wait_ge(k_in[0], FETCHED)
                                pe.wait_ge(maxed, 2)
                            make_scores(pe, 1 - j)
                        if j:
                            pe.wait_ge(mix_ready, 1)
                            pe.wait_ge(w_taken, 2)
                        for p in range(PAGES):
                            pe.matmul(p_w[:, p, :], s[j][:, p * PAGE:(p + 1) * PAGE], mix[j][:], start=True, stop=True)
                        pe.matmul(p_w[0:DEC_S, PAGES, :], s[j][:, PAST:], mix[j][:], start=True, stop=True).then_inc(
                            weighed, 1)
                        pe.wait_ge(w_taken, 2 * j + 2)
                        if j:
                            pe.wait_ge(v_in[1], FETCHED)
                            pe.wait_ge(o_taken, 1)
                        for p in range(PAGES):
                            pe.matmul(p_o[:], wT[:, p, :], val[j][:, p, :], start=(p == 0), stop=False)
                        pe.matmul(p_o[:], wT[0:DEC_S, PAGES, :], vN[j][:], start=False, stop=True).then_inc(mixed, 1)

                @block.vector
                def _(dve):
                    v = Tally(dve, v_done)
                    for j in range(ahead):
                        queries(dve, 2 * i + 1 + j, 1 - j)
                    for j in range(2):
                        if j < ahead:
                            if j:
                                dve.wait_ge(weighed, 1)
                            soften(dve, v, 1 - j, j)
                        dve.wait_ge(weighed, j + 1)
                        if j:
                            dve.wait_ge(mixed, 1)
                        dve.tensor_copy(wT[:, 0:PAGES, :], p_w[:, 0:PAGES, :]).then_inc(w_taken, 1)
                        dve.tensor_copy(wT[0:DEC_S, PAGES, :], p_w[0:DEC_S, PAGES, :]).then_inc(w_taken, 1)
                        dve.wait_ge(mixed, j + 1)
                        dve.tensor_copy(o_all[:, ds(2 * i + j, 1), :].rearrange("p a e -> p (a e)"), p_o[:]).then_inc(o_taken, 1)

                @block.scalar
                def _(act):
                    for j in range(ahead):
                        grow(act, 1 - j, j)

                @block.gpsimd
                def _(pool):
                    fetch_values(pool, 2 * i + 1, 1)
                    if not last:
                        pool.wait_ge(mixed, 1)
                        fetch_values(pool, 2 * i + 2, 0)
                        pool.wait_ge(v_in[0], FETCHED)
            st.end_pass()

        with nc.Fori(0, DEC_B // 2 - 1) as i:
            two_sequences(i, False)
        two_sequences(DEC_B // 2 - 1, True)

        with nc.Block() as block:
            @block.scalar
            def _(act):
                act.wait_ge(first, 16)
                for h in range(HD):
                    if h:
                        act.wait_ge(squared, h)
                    act.activation(sq[:], o[:, h, :], ACT.Square, accum_out=ssq[:, h:h + 1]).then_inc(squared, 1)
                act.wait_ge(squared, HD)
                root(act, rs[:], ssq[:], 2 * DH, eps[:DEC]).then_inc(rooted, 1)

            @block.vector
            def _(dve):
                v = Tally(dve, v_done)
                dve.wait_ge(first, 16)
                dve.wait_ge(rooted, 1)
                v.step(dve.reciprocal(rs[:], rs[:]))
                for h in range(HD):
                    dve.scalar_tensor_tensor(out=o[:, h, :], in0=o[:, h, :], scalar=rs[:, h:h + 1], in1=gd[:],
                                             op0=ALU.mult, op1=ALU.mult).then_inc(o_done, 1)

            @block.sync
            def _(sp):
                flat = o[:].rearrange("p h e -> p (h e)")
                for h in range(HD):
                    cols = slice(h * P, (h + 1) * P)
                    sp.dma_start(t["mix"][SEQ:SEQ + DEC, D_SSM + h * P:D_SSM + (h + 1) * P].rearrange(
                        "(b s) e -> s b e", s=DEC_S), o_all[h * DEC_S:(h + 1) * DEC_S, :, cols]).then_inc(consts, 16)
                sp.wait_ge(consts, 16 * HD)
                sp.dma_start(flat, t["mix"][SEQ:SEQ + DEC, D_SSM:]).then_inc(first, 16)
                sp.wait_ge(o_done, HD)
                for r in range(REP):
                    sp.dma_start(t["mix"][SEQ + r * DEC:SEQ + (r + 1) * DEC, D_SSM:], flat).then_inc(stored, 16)
                sp.wait_ge(stored, 16 * REP)
        st.end_pass()


def experts(nc, t):
    RING = 15
    DIAGS = 8
    GRP = 4
    COEF_LAG = GRP + 1
    LAG = GRP + 3
    with ExitStack() as ctx:
        st = Stage(nc, ctx, "ex")
        wo = st.sb("wo", [P, KT, D])
        wq = st.sb("wq", [P, KT, 2 * PH * KEYS])
        keysT = st.sb("keysT", [P, 2, KEYS])
        ident = st.sb("ident", [P, P])
        fold = st.sb("fold", [P, DEC])
        g = st.sb("g", [P, D])
        eps = st.sb("eps", [P, 1])
        iota_i = st.sb("iota_i", [P, TOPK], I32)
        iota = st.sb("iota", [P, TOPK])
        ring = st.sb("ring", [P, RING, D])
        m_cur = st.sb("m_cur", [P, D])
        idx_cur = st.sb("idx_cur", [P, SLOTS], I32)
        gate_cur = st.sb("gate_cur", [P, SLOTS])
        dots = st.sb("dots", [P, SLOTS])
        act_out = st.sb("act_out", [P, SLOTS])
        coef = st.sb("coef", [P, SLOTS])
        diag = st.sb("diag", [P, DIAGS, P])
        h1_cur = st.sb("h1_cur", [P, D])
        h1 = st.sb("h1", [P, D])
        m = st.sb("m", [P, D])
        aT = st.sb("aT", [P, KT, P])
        ssq, rs = (st.sb(n, [P, 1]) for n in ("ssq", "rs"))
        qT = [st.sb(f"qT{k}", [P, 4, P]) for k in range(2)]
        s = st.sb("s", [P, 4, KEYS])
        s_less = st.sb("s_less", [P, 4, KEYS])
        top = st.sb("top", [P, 4, TOPK])
        top_i = st.sb("top_i", [P, 4, TOPK], U32)
        top_f = st.sb("top_f", [P, 4, TOPK])
        cand = st.sb("cand", [P, 2, TOPK, TOPK])
        cand_less = st.sb("cand_less", [P, 2, TOPK * TOPK])
        best = st.sb("best", [P, 2, TOPK])
        pos = st.sb("pos", [P, 2 * TOPK], U32)
        side_i = st.sb("side_i", [P, 2, 2 * TOPK], U32)
        side = st.sb("side", [P, 2, 2 * TOPK])
        hot = st.sb("hot", [P, 2, 2 * TOPK, TOPK])
        pick = st.sb("pick", [P, 2, 2 * TOPK])
        idx_f = st.sb("idx_f", [P, 2 * TOPK])
        neg = st.sb("neg", [P, 2])
        total = st.sb("total", [P, 2])
        idx_next = st.sb("idx_next", [P, SLOTS], I32)
        gate_next = st.sb("gate_next", [P, SLOTS])
        acc = [st.ps(f"acc{k}", [P, 512]) for k in range(2)]
        pt = [st.ps(f"pt{k}", [P, 512]) for k in range(2)]
        pq = [st.ps(f"pq{k}", [P, 4, P]) for k in range(2)]
        pk = [st.ps(f"pk{k}", [P, 4, KEYS]) for k in range(2)]
        consts, wo_in, v_done, idx_ready, copied, stored = (
            st.sem(n) for n in ("consts", "wo_in", "v_done", "idx_ready", "copied", "stored"))
        wq_in = [st.sem(f"wq_in{n}") for n in range(4)]
        u_used, v_used, gelu_done, coef_ready, diag_ready, folded, h2_ready = (
            st.sem(n) for n in ("u_used", "v_used", "gelu_done", "coef_ready", "diag_ready", "folded", "h2_ready"))
        (x_in, f_turned, f_taken_a, f_taken_v, projected, h1_ready, squared, rooted, m_ready, q_made, q_taken, s_made,
         s_taken, ranked, grown) = (
            st.sem(n) for n in (
                "x_in", "f_turned", "f_taken_a", "f_taken_v", "projected", "h1_ready", "squared", "rooted", "m_ready",
                "q_made", "q_taken", "s_made", "s_taken", "ranked", "grown"))
        came = [st.pool_sem(f"came{k}") for k in range(RING)]

        def pause(steps):
            return (None for _ in range(steps))

        class Front:

            def __init__(self, row):
                self.row = row

            def sync(self, sp):
                sp.dma_start(m[:], t["mix"][self.row, :]).then_inc(x_in, 16)
                sp.dma_start(h1[:], t["x_all"][self.row, :]).then_inc(x_in, 16)

            @staticmethod
            def tensor(pe, first=False):
                def turn():
                    for k in range(KT):
                        mm = pe.transpose(pt[k // 4][:, (k % 4) * P:(k % 4 + 1) * P], m[:, k * P:(k + 1) * P], ident[:])
                    mm.then_inc(f_turned, 1)

                pe.wait_ge(x_in, 32)
                turn()
                yield from pause(4)
                pe.wait_ge(f_taken_a, 1)
                pe.wait_ge(f_taken_v, 1)
                if first:
                    pe.wait_ge(wo_in, 16 * KT)
                for n in range(2):
                    for k in range(KT):
                        mm = pe.matmul(pt[n][:], aT[:, k, :], wo[:, k, n * 512:(n + 1) * 512],
                                       start=(k == 0), stop=(k == KT - 1))
                        if k % 2:
                            if k == KT - 1:
                                mm.then_inc(projected, 1)
                            yield
                yield from pause(7)
                pe.wait_ge(m_ready, 1)
                turn()
                yield from pause(4)
                pe.wait_ge(f_taken_a, 2)
                pe.wait_ge(f_taken_v, 2)
                behind = 0 if first else 1
                for n in range(4 + behind):
                    if n < 4:
                        if n >= 2:
                            pe.wait_ge(q_taken, n - 1)
                        if first:
                            pe.wait_ge(wq_in[n], 16)
                        for j in range(4):
                            c = (4 * n + j) * KEYS
                            for k in range(KT):
                                mm = pe.matmul(pq[n % 2][:, j, :], wq[:, k, c:c + KEYS], aT[:, k, :],
                                               start=(k == 0), stop=(k == KT - 1))
                            if j == 3:
                                mm.then_inc(q_made, 1)
                            yield
                    if n >= behind:
                        c = n - behind
                        pe.wait_ge(q_taken, c + 1)
                        if c >= 2:
                            pe.wait_ge(s_taken, c - 1)
                        for j in range(4):
                            mm = pe.matmul(pk[c % 2][:, j, :], qT[c % 2][:, j, :], keysT[:, j % 2, :],
                                           start=True, stop=True)
                        mm.then_inc(s_made, 1)
                        yield from pause(11)

            @staticmethod
            def scalar(act):
                def take(n):
                    act.wait_ge(f_turned, n)
                    act.activation(aT[:, 0:4, :].rearrange("p k q -> p (k q)"), pt[0][:], ACT.Copy).then_inc(f_taken_a, 1)

                def take_queries(n):
                    act.wait_ge(q_made, n + 1)
                    if n >= 2:
                        act.wait_ge(s_made, n - 1)
                    act.activation(qT[n % 2][:], pq[n % 2][:], ACT.Copy).then_inc(q_taken, 1)

                yield from pause(2)
                take(1)
                yield from pause(13)
                act.wait_ge(h1_ready, 2)
                act.activation(m[:], h1[:], ACT.Square, accum_out=ssq[:]).then_inc(squared, 1)
                act.wait_ge(squared, 1)
                root(act, rs[:], ssq[:], D, eps[:]).then_inc(rooted, 1)
                yield from pause(6)
                take(2)
                yield from pause(7)
                for n in range(5):
                    if n < 4:
                        take_queries(n)
                    yield from pause(12 if n < 4 else 14)
                    if n:
                        act.wait_ge(ranked, n)
                        for h in range(2):
                            c = (2 * (n - 1) + h) * TOPK
                            act.activation(gate_next[:, c:c + TOPK], best[:, h, :], ACT.Exp, bias=neg[:, h:h + 1],
                                           accum_out=total[:, h:h + 1]).then_inc(grown, 1)

            @staticmethod
            def vector(dve, v):
                def take(n):
                    dve.wait_ge(f_turned, n)
                    dve.tensor_copy(aT[:, 4:8, :].rearrange("p k q -> p (k q)"), pt[1][:]).then_inc(f_taken_v, 1)

                def divide(n):
                    dve.wait_ge(grown, 2 * n + 2)
                    v.step(dve.reciprocal(total[:], total[:]))
                    for h in range(2):
                        c = (2 * n + h) * TOPK
                        v.did(dve.tensor_scalar(gate_next[:, c:c + TOPK], gate_next[:, c:c + TOPK], total[:, h:h + 1],
                                                None, ALU.mult))
                    v.settle()

                yield from pause(2)
                take(1)
                yield from pause(11)
                for n in range(2):
                    dve.wait_ge(projected, n + 1)
                    part = slice(n * 512, (n + 1) * 512)
                    dve.tensor_tensor(h1[:, part], h1[:, part], pt[n][:], ALU.add).then_inc(h1_ready, 1)
                yield from pause(4)
                dve.wait_ge(rooted, 1)
                v.step(dve.reciprocal(rs[:], rs[:]))
                dve.scalar_tensor_tensor(out=m[:], in0=h1[:], scalar=rs[:], in1=g[:], op0=ALU.mult,
                                         op1=ALU.mult).then_inc(m_ready, 1)
                yield from pause(4)
                take(2)
                yield from pause(12)
                for n in range(4):
                    dve.wait_ge(s_made, n + 1)
                    dve.tensor_copy(s[:], pk[n % 2][:]).then_inc(s_taken, 1)
                    dve.wait_ge(s_taken, n + 1)
                    for j in range(4):
                        v.did(dve.max(top[:, j, 0:8], s[:, j, :]))
                    yield
                    v.settle()
                    for j in range(4):
                        v.did(dve.match_replace(s_less[:, j, :], top[:, j, 0:8], s[:, j, :], NEG))
                    yield
                    v.settle()
                    for j in range(4):
                        v.did(dve.max(top[:, j, 8:16], s_less[:, j, :]))
                    yield
                    for j in range(4):
                        v.did(dve.max_index(top_i[:, j, 0:8], top[:, j, 0:8], s[:, j, :]))
                    yield
                    v.settle()
                    for j in range(4):
                        v.did(dve.max_index(top_i[:, j, 8:16], top[:, j, 8:16], s_less[:, j, :]))
                    yield
                    for h in range(2):
                        v.did(dve.tensor_tensor(cand[:, h], wide(top[:, 2 * h, :], [P, TOPK, TOPK]),
                                                top[:, 2 * h + 1:2 * h + 2, :].to_broadcast([P, TOPK, TOPK]), ALU.add))
                    yield
                    v.settle()
                    v.did(dve.tensor_copy(top_f[:], top_i[:]))
                    if n:
                        divide(n - 1)
                    flat = [cand[:, h].rearrange("p a b -> p (a b)") for h in range(2)]
                    for h in range(2):
                        v.did(dve.max(best[:, h, 0:8], flat[h]))
                    yield
                    v.settle()
                    for h in range(2):
                        v.did(dve.match_replace(cand_less[:, h, :], best[:, h, 0:8], flat[h], NEG))
                    v.did(dve.tensor_scalar(neg[:], best[:, :, 0], -1.0, None, ALU.mult))
                    yield
                    v.settle()
                    v.did(dve.max(best[:, 0, 8:16], cand_less[:, 0, :]))
                    dve.max(best[:, 1, 8:16], cand_less[:, 1, :]).then_inc(ranked, 1)
                    yield
                    v.settle()
                    dve.wait_ge(ranked, n + 1)
                    for h in range(2):
                        v.did(dve.max_index(pos[:, h * TOPK:h * TOPK + 8], best[:, h, 0:8], flat[h]))
                        v.did(dve.max_index(pos[:, h * TOPK + 8:(h + 1) * TOPK], best[:, h, 8:16], cand_less[:, h, :]))
                    yield
                    v.settle()
                    v.did(dve.tensor_scalar(side_i[:, 0, :], pos[:], 4, None, ALU.logical_shift_right))
                    v.did(dve.tensor_scalar(side_i[:, 1, :], pos[:], TOPK - 1, None, ALU.bitwise_and))
                    v.settle()
                    v.step(dve.tensor_copy(side[:], side_i[:]))
                    for c in range(2):
                        v.did(dve.tensor_tensor(hot[:, c], wide(side[:, c, :], [P, 2 * TOPK, TOPK]),
                                                iota[:].unsqueeze(1).to_broadcast([P, 2 * TOPK, TOPK]), ALU.is_equal))
                    yield
                    v.settle()
                    for c in range(2):
                        for h in range(2):
                            part = hot[:, c, h * TOPK:(h + 1) * TOPK, :]
                            v.did(dve.tensor_tensor(part, part,
                                                    top_f[:, 2 * h + c:2 * h + c + 1, :].to_broadcast([P, TOPK, TOPK]),
                                                    ALU.mult))
                    yield
                    v.settle()
                    v.step(dve.tensor_reduce(pick[:], hot[:], AX_X, ALU.add))
                    yield
                    v.step(dve.scalar_tensor_tensor(out=idx_f[:], in0=pick[:, 0, :], scalar=float(KEYS), in1=pick[:, 1, :],
                                                    op0=ALU.mult, op1=ALU.add))
                    c0 = 2 * n * TOPK
                    v.did(dve.tensor_copy(idx_next[:, c0:c0 + 2 * TOPK], idx_f[:]))
                    yield
                yield from pause(5)
                divide(3)

        class Gather:

            def __init__(self, slots):
                self.slots, self.steps = slots, range(slots + LAG)
                self.order = [it for i in self.steps
                              for it in [("u", i)] * (i < slots) + [("v", i - LAG)] * (i >= LAG)]
                self.at = {it: n for n, it in enumerate(self.order)}

            def start(self, dve, v, sample):
                if sample:
                    for r in range(REP):
                        rows, cols = slice(r * DEC, (r + 1) * DEC), slice(2 * r * TOPK, 2 * (r + 1) * TOPK)
                        dve.tensor_copy(idx_cur[rows, 0:2 * TOPK], idx_next[rows, cols]).then_inc(idx_ready, 1)
                        v.did(dve.tensor_copy(gate_cur[rows, 0:2 * TOPK], gate_next[rows, cols]))
                else:
                    dve.tensor_copy(idx_cur[:], idx_next[:]).then_inc(idx_ready, REP)
                    v.did(dve.tensor_copy(gate_cur[:], gate_next[:]))
                dve.tensor_copy(m_cur[:], m[:]).then_inc(copied, 1)
                v.settle()

            def close(self, dve):
                yield
                for n in range(2):
                    part = slice(n * 512, (n + 1) * 512)
                    dve.tensor_tensor(h1_cur[:, part], h1_cur[:, part], acc[n][:], ALU.add).then_inc(h2_ready, 1)
                    yield
                yield from pause(3)
                dve.wait_ge(stored, 16)
                dve.tensor_copy(h1_cur[:], h1[:]).then_inc(copied, 1)

            def sync(self, sp, row):
                sp.wait_ge(h2_ready, 2)
                sp.dma_start(t["h2"][row, :], h1_cur[:]).then_inc(stored, 16)

            def landed(self, eng, it):
                n = self.at[it]
                eng.wait_ge(came[n % RING], 16 * (n // RING + 1))

            def pool(self, pool):
                pool.wait_ge(idx_ready, REP)
                for n, (kind, slot) in enumerate(self.order):
                    if n >= RING:
                        k0, s0 = self.order[n - RING]
                        pool.wait_ge(u_used if k0 == "u" else v_used, s0 + 1)
                    table = t["expert_u"] if kind == "u" else t["expert_v"]
                    pool.indirect_dma_start(ring[:, n % RING, :], None, table,
                                            bass.IndirectOffsetOnAxis(idx_cur[:, slot:slot + 1], 0)).then_inc(
                        came[n % RING], 16)

            def vector(self, dve, front=iter(())):
                close = self.close(dve)
                dve.wait_ge(copied, 1)
                for i in self.steps:
                    if i < self.slots:
                        self.landed(dve, ("u", i))
                        u = ring[:, self.at[("u", i)] % RING, :]
                        dve.tensor_tensor_reduce(out=u, in0=u, in1=m_cur[:], scale=1.0, scalar=0.0, op0=ALU.mult,
                                                 op1=ALU.add, accum_out=dots[:, i:i + 1]).then_inc(u_used, 1)
                    q = (i - COEF_LAG) // GRP
                    if (i - COEF_LAG) % GRP == 0 and 0 <= q < self.slots // GRP:
                        cols = slice(q * GRP, (q + 1) * GRP)
                        dve.wait_ge(gelu_done, q + 1)
                        dve.tensor_tensor(coef[:, cols], act_out[:, cols], gate_cur[:, cols], ALU.mult).then_inc(
                            coef_ready, 1)
                    next(close if i < LAG else front, None)
                for _ in front:
                    pass

            def scalar(self, act, front=iter(())):
                for i in self.steps:
                    if i >= LAG:
                        slot = i - LAG
                        if slot % GRP == 0:
                            act.wait_ge(coef_ready, slot // GRP + 1)
                        if slot >= DIAGS:
                            act.wait_ge(v_used, slot - DIAGS + 1)
                        act.activation(diag[:, slot % DIAGS, :], ident[:], ACT.Copy,
                                       scale=coef[:, slot:slot + 1]).then_inc(diag_ready, 1)
                        next(front, None)
                    if i < self.slots and i % GRP == GRP - 1:
                        cols = slice(i + 1 - GRP, i + 1)
                        act.wait_ge(u_used, i + 1)
                        act.activation(act_out[:, cols], dots[:, cols], ACT.Gelu).then_inc(gelu_done, 1)
                for _ in front:
                    pass

            def tensor(self, pe, front=iter(())):
                for slot in range(self.slots):
                    pe.wait_ge(diag_ready, slot + 1)
                    self.landed(pe, ("v", slot))
                    if slot == 0:
                        pe.wait_ge(h2_ready, 2)
                    row = self.at[("v", slot)] % RING
                    for n in range(2):
                        mm = pe.matmul(acc[n][:], diag[:, slot % DIAGS, :], ring[:, row, n * 512:(n + 1) * 512],
                                       start=(slot == 0), stop=(slot == self.slots - 1))
                    mm.then_inc(v_used, 1)
                    next(front, None)
                for _ in front:
                    pass

        front = Front(slice(0, P))
        with nc.Block() as block:
            @block.sync
            def _(sp):
                front.sync(sp)
                sp.wait_ge(consts, 16 * 5)

            @block.gpsimd
            def _(pool):
                pool.iota(iota_i[:], pattern=[[1, TOPK]], base=0, channel_multiplier=0).then_inc(copied, 1)

            @block.scalar
            def _(act):
                act.dma_start(ident[:], t["ident"]).then_inc(consts, 16)
                act.dma_start(g[:], spread(t["g_ffn"])).then_inc(consts, 16)
                act.dma_start(fold[:], t["fold"]).then_inc(consts, 16)
                act.dma_start(keysT[:, 0, :], t["keysT"][:, 0, :]).then_inc(consts, 16)
                act.dma_start(keysT[:, 1, :], t["keysT"][:, 1, :]).then_inc(consts, 16)
                for k in range(KT):
                    act.dma_start(wo[:, k, :], t["w_out"][k * P:(k + 1) * P, :]).then_inc(wo_in, 16)
                for n in range(4):
                    cols = slice(n * 4 * KEYS, (n + 1) * 4 * KEYS)
                    act.dma_start(wq[:, :, cols], t["w_query"].rearrange("(k p) n -> p k n", p=P)[:, :, cols]).then_inc(
                        wq_in[n], 16)
                for _ in front.scalar(act):
                    pass

            @block.vector
            def _(dve):
                v = Tally(dve, v_done)
                v.did(dve.memset(eps[:], EPS))
                v.did(dve.memset(h1_cur[:], 0.0))
                dve.wait_ge(copied, 1)
                v.step(dve.tensor_copy(iota[:], iota_i[:]))
                dve.wait_ge(consts, 16 * 5)
                for _ in front.vector(dve, v):
                    pass

            @block.tensor
            def _(pe):
                pe.wait_ge(consts, 16 * 5)
                for _ in front.tensor(pe, first=True):
                    pass
                for n in range(2):
                    pe.matmul(acc[n][:], ident[:], m[:, n * 512:(n + 1) * 512], start=True, stop=True)
        st.end_pass()

        gather = Gather(SLOTS)
        with nc.Fori(0, NT - 1) as k:
            front = Front(ds((k + 1) * P, P))
            with nc.Block() as block:
                @block.sync
                def _(sp):
                    gather.sync(sp, ds(k * P, P))
                    sp.wait_ge(copied, 2)
                    front.sync(sp)
                    sp.wait_ge(stored, 16)

                @block.gpsimd
                def _(pool):
                    gather.pool(pool)

                @block.scalar
                def _(act):
                    gather.scalar(act, front.scalar(act))

                @block.vector
                def _(dve):
                    v = Tally(dve, v_done)
                    gather.start(dve, v, False)
                    gather.vector(dve, front.vector(dve, v))

                @block.tensor
                def _(pe):
                    gather.tensor(pe, front.tensor(pe))
            st.end_pass()

        last = Gather(2 * TOPK)
        with nc.Block() as block:
            @block.sync
            def _(sp):
                last.sync(sp, slice(SEQ, SEQ + P))
                sp.wait_ge(h2_ready, 4)
                for r in range(2 * REP):
                    at = SEQ + P + r * DEC
                    sp.dma_start(t["h2"][at:at + DEC, :], h1_cur[0:DEC, :]).then_inc(stored, 16)
                sp.wait_ge(stored, 16 * (1 + 2 * REP))

            @block.gpsimd
            def _(pool):
                last.pool(pool)

            @block.scalar
            def _(act):
                last.scalar(act)

            @block.vector
            def _(dve):
                v = Tally(dve, v_done)
                last.start(dve, v, True)
                last.vector(dve)
                dve.wait_ge(v_used, 2 * TOPK)
                for n in range(2):
                    part = slice(n * 512, (n + 1) * 512)
                    dve.tensor_copy(h1[:, part], acc[n][:]).then_inc(h1_ready, 1)
                for n in range(2):
                    part = slice(n * 512, (n + 1) * 512)
                    dve.wait_ge(folded, n + 1)
                    dve.tensor_tensor(h1_cur[0:DEC, part], h1_cur[0:DEC, part], pt[n][0:DEC, :], ALU.add).then_inc(
                        h2_ready, 1)

            @block.tensor
            def _(pe):
                last.tensor(pe)
                for n in range(2):
                    pe.wait_ge(h1_ready, n + 1)
                    pe.matmul(pt[n][0:DEC, :], fold[:], h1[:, n * 512:(n + 1) * 512], start=True, stop=True).then_inc(
                        folded, 1)
        st.end_pass()


def finish(nc, t):
    with ExitStack() as ctx:
        lasting = Stage(nc, ctx, "fil")
        gate_in = [lasting.sem(f"gate_in{n}") for n in range(2)]
        ple_in = lasting.sem("ple_in")
        st = Stage(nc, ctx, "fi")
        wg = st.sb("wg", [P, KT, D])
        wp = st.sb("wp", [P, PLE // P, D])
        g1 = st.sb("g1", [P, D])
        g2 = st.sb("g2", [P, D])
        ident = st.sb("ident", [P, P])
        eps = st.sb("eps", [P, 1])
        x = st.sb("x", [P, D])
        h = st.sb("h", [P, D])
        a = st.sb("a", [P, D])
        aT = st.sb("aT", [P, KT, P])
        pT = st.sb("pT", [P, PLE // P, P])
        ssq, rs, ssq2, rs2 = (st.sb(n, [P, 1]) for n in ("ssq", "rs", "ssq2", "rs2"))
        sig = st.sb("sig", [P, D])
        sq, sq2 = (st.sb(n, [P, D]) for n in ("sq", "sq2"))
        h3 = st.sb("h3", [P, D])
        y = st.sb("y", [P, D])
        pg = [st.ps(f"pg{k}", [P, 512]) for k in range(2)]
        pp = [st.ps(f"pp{k}", [P, 512]) for k in range(2)]
        tr = [st.ps(f"tr{k}", [P, 512]) for k in range(2)]
        (consts, x_in, p_in, squared, rooted, inverted, normed, turned, taken, h_taken, gated, added, sig_ready,
         h3_ready, squared2, rooted2, y_ready, v_done, stored) = (
            st.sem(n) for n in (
                "consts", "x_in", "p_in", "squared", "rooted", "inverted", "normed", "turned", "taken", "h_taken", "gated",
                "added", "sig_ready", "h3_ready", "squared2", "rooted2", "y_ready", "v_done", "stored"))

        def norm_act(act):
            act.wait_ge(x_in, 16)
            act.activation(sq[:], x[:], ACT.Square, accum_out=ssq[:]).then_inc(squared, 1)
            act.wait_ge(squared, 1)
            root(act, rs[:], ssq[:], D, eps[:]).then_inc(rooted, 1)

        def norm_dve(dve):
            dve.wait_ge(rooted, 1)
            dve.reciprocal(rs[:], rs[:]).then_inc(inverted, 1)
            dve.wait_ge(inverted, 1)
            dve.scalar_tensor_tensor(out=a[:], in0=x[:], scalar=rs[:], in1=g1[:], op0=ALU.mult,
                                     op1=ALU.mult).then_inc(normed, 1)

        def turn(pe):
            pe.wait_ge(normed, 1)
            for k in range(KT):
                last = pe.transpose(tr[k // 4][:, (k % 4) * P:(k % 4 + 1) * P], a[:, k * P:(k + 1) * P], ident[:])
            last.then_inc(turned, 1)

        def take_act(act):
            act.wait_ge(turned, 1)
            act.activation(aT[:, 0:4, :].rearrange("p k q -> p (k q)"), tr[0][:], ACT.Copy).then_inc(taken, 1)

        def take_dve(dve):
            dve.wait_ge(turned, 1)
            dve.tensor_copy(aT[:, 4:8, :].rearrange("p k q -> p (k q)"), tr[1][:]).then_inc(taken, 1)
            dve.tensor_copy(h[:], x[:]).then_inc(h_taken, 1)

        with nc.Block() as block:
            @block.sync
            def _(sp):
                sp.dma_start(x[:], t["h2"][P:2 * P, :]).then_inc(x_in, 16)
                sp.dma_start(g1[:], spread(t["g_ple"])).then_inc(consts, 16)
                sp.dma_start(g2[:], spread(t["g_final"])).then_inc(consts, 16)
                sp.dma_start(ident[:], t["ident"]).then_inc(consts, 16)
                w_gate = t["w_ple_gate"].rearrange("(k p) n -> p k n", p=P)
                for n in range(2):
                    part = slice(n * 512, (n + 1) * 512)
                    sp.dma_start(wg[:, :, part], w_gate[:, :, part]).then_inc(gate_in[n], 16)
                    if n == 0:
                        sp.dma_start(wp[:], t["w_ple"].rearrange("(k p) n -> p k n", p=P)).then_inc(ple_in, 16)

            @block.scalar
            def _(act):
                act.wait_ge(v_done, 1)
                norm_act(act)
                take_act(act)

            @block.vector
            def _(dve):
                dve.memset(eps[:], EPS).then_inc(v_done, 1)
                dve.memset(h3[:], 0.0)
                dve.wait_ge(consts, 48)
                norm_dve(dve)
                take_dve(dve)

            @block.tensor
            def _(pe):
                pe.wait_ge(consts, 48)
                turn(pe)
        st.end_pass()

        def out_act(act):
            act.activation(sq2[:], h3[:], ACT.Square, accum_out=ssq2[:]).then_inc(squared2, 1)
            act.wait_ge(squared2, 1)
            root(act, rs2[:], ssq2[:], D, eps[:]).then_inc(rooted2, 1)

        def out_dve(dve, v):
            dve.wait_ge(rooted2, 1)
            v.step(dve.reciprocal(rs2[:], rs2[:]))
            dve.scalar_tensor_tensor(out=y[:], in0=h3[:], scalar=rs2[:], in1=g2[:], op0=ALU.mult,
                                     op1=ALU.mult).then_inc(y_ready, 1)

        with nc.Fori(0, NT) as i:
            with nc.Block() as block:
                @block.sync
                def _(sp):
                    sp.dma_start(x[:], t["h2"][ds((i + 2) * P, P), :]).then_inc(x_in, 16)
                    sp.dma_start(pT[:].rearrange("p k q -> p (k q)"), t["pT"][ds(i * P, P), :]).then_inc(p_in, 16)
                    sp.wait_ge(y_ready, 1)
                    sp.dma_start(t["y"][ds(i * P, P), :], y[:]).then_inc(stored, 16)
                    sp.wait_ge(stored, 16)

                @block.tensor
                def _(pe):
                    def gate(n):
                        pe.wait_ge(gate_in[n], 16)
                        for k in range(KT):
                            mm = pe.matmul(pg[n][:], aT[:, k, :], wg[:, k, n * 512:(n + 1) * 512],
                                           start=(k == 0), stop=(k == KT - 1))
                        mm.then_inc(gated, 1)

                    gate(0)
                    pe.wait_ge(p_in, 16)
                    pe.wait_ge(ple_in, 16)
                    for n in range(2):
                        for k in range(PLE // P):
                            mm = pe.matmul(pp[n][:], pT[:, k, :], wp[:, k, n * 512:(n + 1) * 512],
                                           start=(k == 0), stop=(k == PLE // P - 1))
                        mm.then_inc(added, 1)
                    gate(1)
                    turn(pe)

                @block.scalar
                def _(act):
                    out_act(act)
                    norm_act(act)
                    for n in range(2):
                        act.wait_ge(gated, n + 1)
                        act.activation(sig[:, n * 512:(n + 1) * 512], pg[n][:], ACT.Sigmoid).then_inc(sig_ready, 1)
                    take_act(act)

                @block.vector
                def _(dve):
                    v = Tally(dve, v_done)
                    out_dve(dve, v)
                    norm_dve(dve)
                    dve.wait_ge(y_ready, 1)
                    for n in range(2):
                        part = slice(n * 512, (n + 1) * 512)
                        dve.wait_ge(sig_ready, n + 1)
                        dve.wait_ge(added, n + 1)
                        v.step(dve.tensor_tensor(sig[:, part], sig[:, part], pp[n][:], ALU.mult))
                        dve.tensor_tensor(h3[:, part], h[:, part], sig[:, part], ALU.add).then_inc(h3_ready, 1)
                    dve.wait_ge(h3_ready, 2)
                    take_dve(dve)
            st.end_pass()

        with nc.Block() as block:
            @block.scalar
            def _(act):
                out_act(act)

            @block.vector
            def _(dve):
                out_dve(dve, Tally(dve, v_done))

            @block.sync
            def _(sp):
                sp.wait_ge(y_ready, 1)
                sp.dma_start(t["y"][NT * P:(NT + 1) * P, :], y[:]).then_inc(stored, 16)
                sp.wait_ge(stored, 16)
        st.end_pass()
        lasting.end_pass()


_SCRATCH = {
    "line": (HD, LINE), "fan": (HD, P, FAN), "qT": (NT * P, DV), "kT": (NT * P, DV), "z": (NT * P, D_SSM),
    "xbc": (CONV_W - 1 + NT * P, CONV_DIM), "xbc_s": (DEC_B, CONV_W - 1 + DEC_S, CONV_DIM), "dt": (NT * P, HS),
    "mix": (NT * P, D), "h2": ((NT + 2) * P, D),
}
_OUTPUTS = {
    "y": ((NT + 1) * P, D), "k_all": (NT * P, DV), "v_all": (NT * P, DV), "ssm_p": (NS, D_SSM),
    "ssm_s": (DEC_B, NS, D_SSM), "conv_p": (CONV_W - 1, CONV_DIM), "conv_s": (DEC_B, CONV_W - 1, CONV_DIM),
}


def program(nc, t):
    with ExitStack() as ctx:
        early = Early(nc, ctx)
        project(nc, t, early)
        ssd(nc, t, sample=False)
        ssd(nc, t, sample=True)
        with ExitStack() as both:
            early.hold(both)
            attend_prompt(nc, t, early)
            attend_sample(nc, t, early)
        early.stage.end_pass()
    experts(nc, t)
    finish(nc, t)


def _constants(np):
    f = np.float32
    low = [b if b <= 16 else math.ceil(16 * 8 ** ((b - 16) / 16)) for b in range(32)]
    seq = np.kron(np.eye(DEC_B, dtype=f), np.ones((DEC_S, DEC_S), f))
    own = np.kron(np.eye(DEC_B, dtype=f), np.ones((DEC_S, 1), f))
    pair = np.eye(HD * DEC_S, dtype=f)
    return {
        "edges": np.array(list(zip(low, low[1:] + [10 ** 9])), f),
        "ident": np.eye(P, dtype=f),
        "cum_p": np.triu(np.ones((P, P), f)), "cum_s": np.triu(seq), "same_s": seq,
        "own_s": own, "own_cols": np.ascontiguousarray(own.T),
        "sel_w": np.concatenate([pair, pair]),
        "sign_w": np.repeat(np.array([[1, 0], [0, -1]], f), HD * DEC_S, axis=0),
        "fold": np.tile(np.eye(DEC, dtype=f), (REP, 1)),
    }


def _layout(np, i):
    def tiled(prompt, sample, width):
        s = sample.reshape(DEC, width)
        return np.concatenate([prompt.reshape(SEQ, width)] + [s] * REP)

    x = tiled(i["x_prompt"], i["x_sample"], D)
    p = tiled(i["p_prompt"], i["p_sample"], PLE)
    n_pool = i["cache_k"].shape[1]
    pages = i["page_table"]
    out = {
        "x_all": np.concatenate([x, x[SEQ:]]),
        "pT": p.reshape(NT, P, PLE // P, P).transpose(0, 3, 2, 1).reshape(NT * P, PLE),
        "cache_kT": i["cache_k"].reshape(n_pool, PAGE, HD, 2 * DH).transpose(0, 3, 2, 1).reshape(n_pool, P, HD * PAGE),
        "cache_v": i["cache_v"].reshape(n_pool, PAGE, DV),
        "ssm_in": i["state_ssm"].reshape(DEC_B, D_SSM, NS).transpose(0, 2, 1),
        "state_conv": i["state_conv"][0],
        "pages": pages.reshape(1, -1),
        "keysT": i["sub_keys"][0].transpose(2, 0, 1),
        "lam": np.stack([i[n][0] for n in ("lam_q1", "lam_k1", "lam_q2", "lam_k2")]),
        "rel_bias": i["rel_bias"], "g_final": i["g_final"],
    }
    for n in ("g_mix", "w_in", "conv_w", "conv_b", "dt_bias", "a_log", "d_skip", "g_ssm_norm", "g_diff_norm", "w_out",
              "g_ffn", "w_query", "expert_u", "expert_v", "w_ple", "w_ple_gate", "g_ple"):
        out[n] = i[n][0]
    return out


def kernel(**inputs):
    import numpy as np
    import concourse.bacc as bacc
    from concourse.bass_utils import run_bass_kernel_spmd

    nc = bacc.Bacc("TRN2", target_bir_lowering=False, num_devices=1)
    data = {**_layout(np, {k: np.asarray(v) for k, v in inputs.items()}), **_constants(np)}
    arrays, t = {}, {}
    for name, a in data.items():
        a = np.ascontiguousarray(a)
        arrays[f"in_{name}"] = a
        t[name] = nc.dram_tensor(f"in_{name}", a.shape, mybir.dt.from_np(a.dtype), kind="ExternalInput").ap()
    for name, shape in _SCRATCH.items():
        t[name] = nc.dram_tensor(f"mid_{name}", shape, F32, kind="Internal").ap()
    for name, shape in _OUTPUTS.items():
        t[name] = nc.dram_tensor(f"out_{name}", shape, F32, kind="ExternalOutput").ap()
    program(nc, t)
    r = run_bass_kernel_spmd(nc, [arrays], core_ids=[0]).results[0]
    y, k, v = r["out_y"][P:], r["out_k_all"], r["out_v_all"]
    s = slice(SEQ, SEQ + DEC)
    ssm_p = r["out_ssm_p"].T.reshape(1, 1, HS, PS, NS)
    ssm_s = r["out_ssm_s"].transpose(0, 2, 1).reshape(1, DEC_B, HS, PS, NS)
    return (y[:SEQ].reshape(1, SEQ, D), y[s].reshape(DEC_B, DEC_S, D),
            k[:SEQ].reshape(1, 1, SEQ, HD, 2, DH), v[:SEQ].reshape(1, 1, SEQ, HD, 2 * DH),
            np.ascontiguousarray(ssm_p), r["out_conv_p"].reshape(1, 1, CONV_W - 1, CONV_DIM),
            k[s].reshape(1, DEC_B, DEC_S, HD, 2, DH), v[s].reshape(1, DEC_B, DEC_S, HD, 2 * DH),
            np.ascontiguousarray(ssm_s), r["out_conv_s"].reshape(1, DEC_B, CONV_W - 1, CONV_DIM))
```
